# Optimizing a Trainium2 kernel written in Bass

```python
import jax, jax.numpy as jnp
from jax import lax
import numpy as np

D_MODEL = 1024
BATCH = 1
SEQ = 1024
DEPTH = 2
DEC_BATCH = 8
DEC_SEQ = 8
PAST_LEN = 8192
PAGE_SIZE = 128

N_MIXERS = 2
N_ATT_LAYERS = (DEPTH + 1) // 2
N_DN_LAYERS = DEPTH // 2
EPS = 1e-6

N_HEADS = 8
HEAD_DIM = D_MODEL // N_HEADS
N_KV_HEADS = 2
GROUP = N_HEADS // N_KV_HEADS
ATT_WIDTH = N_HEADS * HEAD_DIM
IDX_HEADS = 8
IDX_DIM = 64
TOPK_MAX = 256
Q_BLOCK = 128
ATT_SIZES = (ATT_WIDTH, N_KV_HEADS * HEAD_DIM, N_KV_HEADS * HEAD_DIM, IDX_HEADS * IDX_DIM, IDX_DIM, IDX_HEADS, ATT_WIDTH)
ATT_IN = 2 * ATT_WIDTH + 2 * N_KV_HEADS * HEAD_DIM + IDX_HEADS * IDX_DIM + IDX_DIM + IDX_HEADS

DN_HEADS = 8
DN_DK = 128
DN_DV = 128
DN_WIDTH = DN_HEADS * DN_DV
CONV_W = 4
CONV_DIM = 2 * DN_HEADS * DN_DK + DN_WIDTH
CHUNK = 64
DN_IN = CONV_DIM + DN_WIDTH + 2 * DN_HEADS

kernel_name = 'dsa_gated_deltanet_hybrid_step'

def _rms_norm(x, gain):
    xf = x.astype(jnp.float32)
    y = xf * lax.rsqrt(jnp.mean(xf * xf, axis=-1, keepdims=True) + EPS)
    return (y * gain.astype(jnp.float32)).astype(x.dtype)

def _l2norm(x):
    xf = x.astype(jnp.float32)
    return xf * lax.rsqrt(jnp.sum(xf * xf, axis=-1, keepdims=True) + EPS)

def _split(p, sizes):
    offs, acc = [], 0
    for s in sizes[:-1]:
        acc += s
        offs.append(acc)
    return jnp.split(p, offs, axis=-1)

def _gather_rows(rows, idx):
    return jax.vmap(lambda r, i: r[i])(rows, idx)

def _gated_out(o, gate, w_out):
    return (o * jax.nn.silu(gate)) @ w_out

def _att_project(xn, w_in, q_gain, k_gain, ik_gain):
    B, T, _ = xn.shape
    q, k, v, iq, ik, iw, gate = _split(xn @ w_in, ATT_SIZES)
    q = _rms_norm(q.reshape(B, T, N_HEADS, HEAD_DIM), q_gain) * (HEAD_DIM ** -0.5)
    k = _rms_norm(k.reshape(B, T, N_KV_HEADS, HEAD_DIM), k_gain)
    v = v.reshape(B, T, N_KV_HEADS, HEAD_DIM)
    iq = iq.reshape(B, T, IDX_HEADS, IDX_DIM)
    ik = _rms_norm(ik, ik_gain)
    iw = iw * (IDX_HEADS ** -0.5 * IDX_DIM ** -0.5)
    return q, k, v, iq, ik, iw, gate

def _indexer_topk(iq, iw, ik, q_pos, topk):
    L = ik.shape[1]
    s = jnp.einsum('bthd,bld->bthl', iq.astype(jnp.float32), ik.astype(jnp.float32))
    score = jnp.einsum('bth,bthl->btl', iw.astype(jnp.float32), jax.nn.relu(s))
    admissible = jnp.arange(L)[None, None, :] <= q_pos[None, :, None]
    score = jnp.where(admissible, score, -jnp.inf)
    _, idx = lax.top_k(score, topk)
    return idx, idx <= q_pos[None, :, None]

def _sparse_attend(q, k_sel, v_sel, valid):
    B, T = q.shape[:2]
    qg = q.reshape(B, T, N_KV_HEADS, GROUP, HEAD_DIM).astype(jnp.float32)
    logits = jnp.einsum('btgrd,btkgd->btgrk', qg, k_sel.astype(jnp.float32))
    logits = jnp.where(valid[:, :, None, None, :], logits, -jnp.inf)
    p = jax.nn.softmax(logits, axis=-1)
    o = jnp.einsum('btgrk,btkgd->btgrd', p, v_sel.astype(jnp.float32))
    return o.reshape(B, T, ATT_WIDTH).astype(q.dtype)

def _att_prompt(q, k, v, iq, iw, ik):
    B, S = q.shape[:2]
    nb = S // Q_BLOCK
    topk = min(TOPK_MAX, S // 4)

    def to_blocks(a):
        return jnp.swapaxes(a.reshape(B, nb, Q_BLOCK, *a.shape[2:]), 0, 1)

    def block(args):
        qb, iqb, iwb, pos = args
        idx, valid = _indexer_topk(iqb, iwb, ik, pos, topk)
        return _sparse_attend(qb, _gather_rows(k, idx), _gather_rows(v, idx), valid)

    pos = jnp.arange(S).reshape(nb, Q_BLOCK)
    out = lax.map(block, (to_blocks(q), to_blocks(iq), to_blocks(iw), pos))
    return jnp.swapaxes(out, 0, 1).reshape(B, S, ATT_WIDTH)

def _att_sample(q, k, v, iq, iw, ik, cache_k, cache_v, cache_idx_k, page_table, layer):
    B, T = q.shape[:2]
    past = page_table.shape[1] * PAGE_SIZE
    ik_past = cache_idx_k[page_table][..., layer, :].reshape(B, past, IDX_DIM)
    ik_all = jnp.concatenate([ik_past.astype(ik.dtype), ik], axis=1)
    q_pos = past + jnp.arange(T)
    idx, valid = _indexer_topk(iq, iw, ik_all, q_pos, min(TOPK_MAX, (past + T) // 4))
    in_past = idx < past
    pidx = jnp.minimum(idx, past - 1)
    phys = jax.vmap(lambda pt, pg: pt[pg])(page_table, pidx // PAGE_SIZE)
    off = pidx % PAGE_SIZE
    nidx = jnp.clip(idx - past, 0, T - 1)

    def select(cache, new):
        old = cache[phys, off][:, :, :, layer]
        return jnp.where(in_past[..., None, None], old.astype(new.dtype), _gather_rows(new, nidx))

    return _sparse_attend(q, select(cache_k, k), select(cache_v, v), valid)

def _short_conv(x, buf, w):
    T = x.shape[1]
    xp = jnp.concatenate([buf.astype(x.dtype), x], axis=1)
    y = sum(xp[:, i:i + T] * w[i] for i in range(CONV_W))
    return jax.nn.silu(y), xp[:, T:]

def _gated_delta_chunked(q, k, v, g, beta, S0):
    B, T, H, _ = q.shape
    n = -(-T // CHUNK)
    pad = n * CHUNK - T

    def blocks(a):
        a = jnp.pad(a, [(0, 0), (0, pad)] + [(0, 0)] * (a.ndim - 2))
        return a.reshape(B, n, CHUNK, H, -1).transpose(1, 0, 3, 2, 4)

    qc, kc, vc = blocks(q), blocks(k), blocks(v)
    gc, bc = blocks(g[..., None])[..., 0], blocks(beta[..., None])[..., 0]
    incl = jnp.tril(jnp.ones((CHUNK, CHUNK), bool))
    strict = jnp.tril(jnp.ones((CHUNK, CHUNK), bool), k=-1)
    eye = jnp.eye(CHUNK, dtype=jnp.float32)

    def step(S, inp):
        qb, kb, vb, gb, bb = inp
        gcum = jnp.cumsum(gb, axis=-1)
        diff = gcum[..., :, None] - gcum[..., None, :]
        decay = jnp.exp(jnp.where(incl, diff, -jnp.inf))
        kk = jnp.einsum('bhid,bhjd->bhij', kb, kb)
        a_mat = bb[..., :, None] * kk * jnp.where(strict, decay, 0.0)
        rhs = bb[..., None] * (vb - jnp.exp(gcum)[..., None] * jnp.einsum('bhcd,bhdv->bhcv', kb, S))
        u = lax.linalg.triangular_solve(eye + a_mat, rhs, left_side=True, lower=True, unit_diagonal=True)
        qk = jnp.einsum('bhid,bhjd->bhij', qb, kb) * decay
        o = jnp.exp(gcum)[..., None] * jnp.einsum('bhcd,bhdv->bhcv', qb, S) + jnp.einsum('bhij,bhjv->bhiv', qk, u)
        glast = gcum[..., -1]
        S_new = jnp.exp(glast)[..., None, None] * S + jnp.einsum(
            'bhcd,bhcv->bhdv', kb * jnp.exp(glast[..., None] - gcum)[..., None], u)
        return S_new, o

    S_fin, o = lax.scan(step, S0, (qc, kc, vc, gc, bc))
    o = o.transpose(1, 0, 3, 2, 4).reshape(B, n * CHUNK, H, -1)[:, :T]
    return o, S_fin

def _dn_branch(xn, S0, conv_buf, w_in, conv_w, A_log, dt_bias, o_gain, w_out):
    B, T, _ = xn.shape
    qkv, z, b, a = _split(xn @ w_in, (CONV_DIM, DN_WIDTH, DN_HEADS, DN_HEADS))
    qkv, new_buf = _short_conv(qkv, conv_buf, conv_w)
    q, k, v = _split(qkv, (DN_HEADS * DN_DK, DN_HEADS * DN_DK, DN_WIDTH))
    q = _l2norm(q.reshape(B, T, DN_HEADS, DN_DK)) * (DN_DK ** -0.5)
    k = _l2norm(k.reshape(B, T, DN_HEADS, DN_DK))
    v = v.reshape(B, T, DN_HEADS, DN_DV).astype(jnp.float32)
    beta = jax.nn.sigmoid(b.astype(jnp.float32))
    g = -jnp.exp(A_log.astype(jnp.float32)) * jax.nn.softplus(a.astype(jnp.float32) + dt_bias.astype(jnp.float32))
    o, S_new = _gated_delta_chunked(q, k, v, g, beta, S0.astype(jnp.float32))
    o = _rms_norm(o, o_gain).astype(xn.dtype).reshape(B, T, DN_WIDTH)
    return _gated_out(o, z, w_out), S_new.astype(S0.dtype), new_buf

def setup_inputs(seed: int = 0) -> dict:
    key = jax.random.key(seed)
    ks = jax.random.split(key, 24)
    n_pages = PAST_LEN // PAGE_SIZE
    n_pool = (5 * DEC_BATCH * n_pages) // 4

    def nrm(k, shape, scale=1.0):
        return scale * jax.random.normal(k, shape, jnp.float32)

    page_table = jax.random.permutation(ks[7], n_pool)[: DEC_BATCH * n_pages].reshape(DEC_BATCH, n_pages).astype(jnp.int32)
    dt = jnp.exp(jax.random.uniform(ks[20], (N_DN_LAYERS, DN_HEADS), jnp.float32, np.log(1e-3), np.log(1e-1)))
    return {
        'x_prompt': nrm(ks[0], (BATCH, SEQ, D_MODEL)),
        'x_sample': nrm(ks[1], (DEC_BATCH, DEC_SEQ, D_MODEL)),
        'cache_k': nrm(ks[2], (n_pool, PAGE_SIZE, N_ATT_LAYERS, N_KV_HEADS, HEAD_DIM)),
        'cache_v': nrm(ks[3], (n_pool, PAGE_SIZE, N_ATT_LAYERS, N_KV_HEADS, HEAD_DIM)),
        'cache_idx_k': nrm(ks[4], (n_pool, PAGE_SIZE, N_ATT_LAYERS, IDX_DIM)),
        'state_dn_S': nrm(ks[5], (DEC_BATCH, N_DN_LAYERS, DN_HEADS, DN_DK, DN_DV), 0.1),
        'state_dn_conv': nrm(ks[6], (DEC_BATCH, N_DN_LAYERS, CONV_W - 1, CONV_DIM)),
        'page_table': page_table,
        'att_norm': 1.0 + nrm(ks[8], (N_ATT_LAYERS, D_MODEL), 0.05),
        'att_w_in': nrm(ks[9], (N_ATT_LAYERS, D_MODEL, ATT_IN), D_MODEL ** -0.5),
        'att_q_gain': 1.0 + nrm(ks[10], (N_ATT_LAYERS, HEAD_DIM), 0.05),
        'att_k_gain': 1.0 + nrm(ks[11], (N_ATT_LAYERS, HEAD_DIM), 0.05),
        'att_ik_gain': 1.0 + nrm(ks[12], (N_ATT_LAYERS, IDX_DIM), 0.05),
        'att_w_out': nrm(ks[13], (N_ATT_LAYERS, ATT_WIDTH, D_MODEL), ATT_WIDTH ** -0.5),
        'dn_norm': 1.0 + nrm(ks[14], (N_DN_LAYERS, D_MODEL), 0.05),
        'dn_w_in': nrm(ks[15], (N_DN_LAYERS, D_MODEL, DN_IN), D_MODEL ** -0.5),
        'dn_conv_w': nrm(ks[16], (N_DN_LAYERS, CONV_W, CONV_DIM), CONV_W ** -0.5),
        'dn_A_log': jnp.log(jax.random.uniform(ks[17], (N_DN_LAYERS, DN_HEADS), jnp.float32, 1.0, 16.0)),
        'dn_dt_bias': dt + jnp.log(-jnp.expm1(-dt)),
        'dn_o_gain': 1.0 + nrm(ks[18], (N_DN_LAYERS, DN_DV), 0.05),
        'dn_w_out': nrm(ks[19], (N_DN_LAYERS, DN_WIDTH, D_MODEL), DN_WIDTH ** -0.5),
    }

def reference(x_prompt, x_sample, cache_k, cache_v, cache_idx_k, state_dn_S, state_dn_conv, page_table,
              att_norm, att_w_in, att_q_gain, att_k_gain, att_ik_gain, att_w_out,
              dn_norm, dn_w_in, dn_conv_w, dn_A_log, dn_dt_bias, dn_o_gain, dn_w_out):
    y_p, y_s = x_prompt, x_sample
    kp, vp, ikp, ks_, vs_, iks = [], [], [], [], [], []
    Sp, cp, Ss, cs = [], [], [], []
    for i in range(DEPTH):
        l = i // N_MIXERS
        if i % N_MIXERS == 0:
            xn = _rms_norm(y_p, att_norm[l])
            q, k, v, iq, ik, iw, gate = _att_project(xn, att_w_in[l], att_q_gain[l], att_k_gain[l], att_ik_gain[l])
            y_p = y_p + _gated_out(_att_prompt(q, k, v, iq, iw, ik), gate, att_w_out[l])
            kp.append(k); vp.append(v); ikp.append(ik)
            xn = _rms_norm(y_s, att_norm[l])
            q, k, v, iq, ik, iw, gate = _att_project(xn, att_w_in[l], att_q_gain[l], att_k_gain[l], att_ik_gain[l])
            o = _att_sample(q, k, v, iq, iw, ik, cache_k, cache_v, cache_idx_k, page_table, l)
            y_s = y_s + _gated_out(o, gate, att_w_out[l])
            ks_.append(k); vs_.append(v); iks.append(ik)
        else:
            xn = _rms_norm(y_p, dn_norm[l])
            B = xn.shape[0]
            S0 = jnp.zeros((B, DN_HEADS, DN_DK, DN_DV), xn.dtype)
            buf0 = jnp.zeros((B, CONV_W - 1, CONV_DIM), xn.dtype)
            out, S_new, buf_new = _dn_branch(xn, S0, buf0, dn_w_in[l], dn_conv_w[l], dn_A_log[l], dn_dt_bias[l], dn_o_gain[l], dn_w_out[l])
            y_p = y_p + out
            Sp.append(S_new); cp.append(buf_new)
            xn = _rms_norm(y_s, dn_norm[l])
            out, S_new, buf_new = _dn_branch(xn, state_dn_S[:, l], state_dn_conv[:, l], dn_w_in[l], dn_conv_w[l], dn_A_log[l], dn_dt_bias[l], dn_o_gain[l], dn_w_out[l])
            y_s = y_s + out
            Ss.append(S_new); cs.append(buf_new)
    k_prompt = jnp.stack(kp, axis=2)
    v_prompt = jnp.stack(vp, axis=2)
    idx_k_prompt = jnp.stack(ikp, axis=2)
    k_sample = jnp.stack(ks_, axis=2)
    v_sample = jnp.stack(vs_, axis=2)
    idx_k_sample = jnp.stack(iks, axis=2)
    dn_S_prompt = jnp.stack(Sp, axis=1)
    dn_conv_prompt = jnp.stack(cp, axis=1)
    dn_S_sample = jnp.stack(Ss, axis=1)
    dn_conv_sample = jnp.stack(cs, axis=1)
    return (y_p, y_s, k_prompt, v_prompt, idx_k_prompt, k_sample, v_sample, idx_k_sample,
            dn_S_prompt, dn_conv_prompt, dn_S_sample, dn_conv_sample)


_drawn_inputs = setup_inputs


def setup_inputs(seed=0):
    import zlib

    import numpy as np

    out = dict(_drawn_inputs(seed))
    spreads = {}
    factors = {'att_q_gain': 8.0}
    for name, (base, spread) in spreads.items():
        noise = np.random.default_rng([zlib.crc32(name.encode()), seed]).standard_normal(out[name].shape)
        drawn = base * np.exp(spread * noise) if base else spread * noise
        out[name] = __import__('jax').numpy.asarray(drawn.astype(out[name].dtype))
    for name, factor in factors.items():
        out[name] = (out[name] * factor).astype(out[name].dtype)
    return out
```

```python
from contextlib import ExitStack

import numpy as np
import concourse.bass as bass
from concourse import mybir

F32 = mybir.dt.float32
I32 = mybir.dt.int32
U32 = mybir.dt.uint32
ALU = mybir.AluOpType
ACT = mybir.ActivationFunctionType
AX = mybir.AxisListType

P = 128
DM = 1024
KT = DM // P
SEQ = 1024
NT = SEQ // P + 1
ROWS = NT * P
DB, DS = 8, 8
NS = DB * DS
PAST = 8192
PAGE = 128
NPG = PAST // PAGE
POOLN = 640
H, G, HD = 8, 2, 128
GRP = H // G
IH, ID = 8, 64
TOPK = 256
EPS = 1e-6
CONV = 3072
CW_TAPS = 4
BIG = 1e30

Q0, K0, V0 = 0, 1024, 1280
IQ0, IK0, IW0, G0 = 1536, 2048, 2112, 2120
ATT_IN = 3144
CHUNKS = [(0, 512), (512, 512), (1024, 512), (1536, 512), (2048, 72), (2120, 512), (2632, 512)]


def new_sem(nc, env, name):
    s = nc.alloc_semaphore(name=name)
    env["sems"].append(s)
    return s


def clear_sems(nc, env):
    nc.clear_and_free_semaphores(env["sems"])
    env["sems"] = []
    nc.all_engine_barrier()


def chain(eng, sem):
    n = [0]

    def link(ins):
        n[0] += 1
        ins.then_inc(sem, 1)
        eng.wait_ge(sem, n[0])
    return link


def att_project(nc, env, t0, m, first, between):
    d, keep = env["dram"], env["keep"]
    with ExitStack() as ctx:
        def sb(name, shape, dt=F32):
            return ctx.enter_context(nc.sbuf_tensor(f"{name}_{t0}", shape, dt))

        def sem(name):
            return new_sem(nc, env, f"{name}_{t0}")

        x = sb("x", [P, 2, DM])
        xnT = sb("xnT", [P, 2, KT, P])
        raw = sb("raw", [P, 2, ATT_IN])
        sq = sb("sq", [P, 1280 + 64])
        ikk = sb("ikk", [P, 2, 2, ID])
        sgate = sb("sgate", [P, 2, DM])
        qTb = sb("qTb", [P, H * HD])
        iqTb = sb("iqTb", [P, IH * ID])
        ssx = sb("ssx", [P, 2, 1])
        rsx = sb("rsx", [P, 2, 1])
        msx = sb("msx", [P, 2, 1])
        ssh = sb("ssh", [P, 2, 11])
        msh = sb("msh", [P, 2, 11])
        rsh = sb("rsh", [P, 2, 11])
        mhalf = sb("mhalf", [P, 16])
        tpb = ctx.enter_context(nc.psum_tensor(f"tpb_{t0}", [P, 2, 4, P], F32))
        acc = ctx.enter_context(nc.psum_tensor(f"acc_{t0}", [P, 6, 512], F32))
        w, gx, gq, gqs, gk, gik = (keep[k] for k in ("w", "gx", "gq", "gqs", "gk", "gik"))
        ident, kT, v_nat, ikT, iw_nat = keep["ident"], keep["kT"], keep["v_nat"], keep["ikT"], keep["iw_nat"]

        x_in = [sem("x_in0"), sem("x_in1")]
        w_in = [sem(f"w_in{c}") for c in range(7)]
        const_in = sem("const_in")
        gains_ok = sem("gains_ok")
        ssx_ok = sem("ssx_ok")
        rsx_ok = sem("rsx_ok")
        pool_chain = sem("pool_chain")
        xn_ok = sem("xn_ok")
        tp_done = sem("tp_done")
        tp_evac = sem("tp_evac")
        mm_done = sem("mm_done")
        raw_ok = sem("raw_ok")
        sq_ok = sem("sq_ok")
        ssh_ok = sem("ssh_ok")
        rsh_ok = sem("rsh_ok")
        exp_ok = sem("exp_ok")
        den_ok = sem("den_ok")
        rec_ok = sem("rec_ok")
        gate_ok = sem("gate_ok")
        nat_ok = sem("nat_ok")
        st = [env["stores"][f"st{u}_{t0}"] for u in range(2)]
        NST = 6

        def run(step):
            for n in range(m):
                step(n, n % 2, n // 2)

        t_base, q_base, uses = {}, {}, 0
        for what, n in [("T", 0)] + [e for i in range(m) for e in (("T", i + 1), ("Q", i - 1))] + [("Q", m - 1)]:
            if 0 <= n < m:
                (t_base if what == "T" else q_base)[n] = uses
                uses += 2 if what == "T" else 4

        block = ctx.enter_context(nc.Block())

        @block.gpsimd
        def _(pool):
            if first:
                pool.dma_start(ident[:], d["c_ident"]).then_inc(const_in, 16)
                pool.dma_start(gx[:], d["att_norm"][0:1, :].partition_broadcast(P)).then_inc(const_in, 16)
                pool.dma_start(gq[:], d["att_q_gain"][0:1, :].partition_broadcast(P)).then_inc(const_in, 16)
                pool.dma_start(gk[:], d["att_k_gain"][0:1, :].partition_broadcast(P)).then_inc(const_in, 16)
                pool.dma_start(gik[:], d["att_ik_gain"][0:1, :].partition_broadcast(P)).then_inc(const_in, 16)
            link = chain(pool, pool_chain)
            link(pool.memset(mhalf[:], -0.5))

            def rms_x(n, par):
                pool.wait_ge(ssx_ok, n + 1)
                link(pool.tensor_scalar(msx[:, par, :], ssx[:, par, :], 1.0 / DM, EPS, ALU.mult, ALU.add))
                pool.tensor_tensor(rsx[:, par, :], msx[:, par, :], mhalf[:, 0:1], ALU.pow).then_inc(rsx_ok, 1)
            rms_x(0, 0)
            if m > 1:
                rms_x(1, 1)

            def step(n, par, k):
                if n + 2 < m:
                    rms_x(n + 2, par)
                pool.wait_ge(ssh_ok, n + 1)
                pool.tensor_scalar(msh[:, par, 0:10], ssh[:, par, 0:10], 1.0 / HD, EPS, ALU.mult, ALU.add)
                link(pool.tensor_scalar(msh[:, par, 10:11], ssh[:, par, 10:11], 1.0 / ID, EPS, ALU.mult, ALU.add))
                pool.tensor_tensor(rsh[:, par, :], msh[:, par, :], mhalf[:, 0:11], ALU.pow).then_inc(rsh_ok, 1)
                pool.wait_ge(exp_ok, n + 1)
                pool.tensor_scalar(sgate[:, par, :], sgate[:, par, :], 1.0, None, ALU.add).then_inc(den_ok, 1)
                pool.wait_ge(rec_ok, n + 1)
                pool.tensor_tensor(sgate[:, par, :], sgate[:, par, :], raw[:, par, G0:ATT_IN], ALU.mult).then_inc(gate_ok, 1)
            run(step)

        @block.sync
        def _(sp):
            def rows(t, n):
                return t[(t0 + n) * P:(t0 + n + 1) * P, :]

            def load(n, par):
                sp.dma_start(x[:, par, :], rows(d["x_all"], n)).then_inc(x_in[par], 16)
            load(0, 0)
            if m > 1:
                load(1, 1)
            wv = d["att_w_in"].rearrange("l (k p) n -> p (l k) n", p=P)
            for c, (a, cw) in enumerate(CHUNKS if first else ()):
                sp.dma_start(w[:, :, a:a + cw], wv[:, :, a:a + cw]).then_inc(w_in[c], 16)

            def store(n, par):
                sp.wait_ge(tp_evac, q_base[n] + 4)
                sp.wait_ge(gate_ok, n + 1)
                sp.dma_start(rows(d["qT_d"], n), qTb[:]).then_inc(st[par], 16)
                sp.dma_start(rows(d["iqT_d"], n), iqTb[:]).then_inc(st[par], 16)
                sp.dma_start(rows(d["gate_d"], n), sgate[:, par, :]).then_inc(st[par], 16)
                sp.dma_start(rows(d["k_all"], n), raw[:, par, K0:K0 + 256]).then_inc(st[par], 16)
                sp.dma_start(rows(d["v_all"], n), v_nat[:, t0 + n, :]).then_inc(st[par], 16)
                sp.dma_start(rows(d["ik_all"], n), ikk[:, par, 0, :]).then_inc(st[par], 16)

            def step(n, par, k):
                if n + 2 < m:
                    sp.wait_ge(tp_done, t_base[n] + 2)
                    load(n + 2, par)
                if n > 0:
                    store(n - 1, 1 - par)
            run(step)
            store(m - 1, (m - 1) % 2)
            sp.wait_ge(st[0], 16 * NST * ((m + 1) // 2))
            sp.wait_ge(st[1], 16 * NST * (m // 2))

        @block.tensor
        def _(pe):
            def transposes_x(n, par):
                b = t_base[n]
                pe.wait_ge(xn_ok, n + 1)
                for u in range(2):
                    if n > 0:
                        pe.wait_ge(tp_evac, b + u - 1)
                    for j in range(4):
                        k = 4 * u + j
                        ins = pe.transpose(tpb[:, u, j, :], x[:, par, k * P:(k + 1) * P], ident[:])
                    ins.then_inc(tp_done, 1)

            def project(n, par, k):
                pe.wait_ge(tp_evac, t_base[n] + 2)
                for c, (a, cw) in enumerate(CHUNKS):
                    if n == 0 and first:
                        pe.wait_ge(w_in[c], 16)
                    if n > 0 or c == 6:
                        pe.wait_ge(raw_ok, 7 * n if c == 0 else 7 * n + 1 if c == 6 else 7 * n + c - 6)
                    for kk in range(KT):
                        ins = pe.matmul(acc[:, c % 6, 0:cw], xnT[:, par, kk, :], w[:, kk, a:a + cw],
                                        start=(kk == 0), stop=(kk == KT - 1))
                    ins.then_inc(mm_done, 1)

            def transposes_q(n, par):
                b = q_base[n]
                pe.wait_ge(nat_ok, n + 1)
                for u in range(4):
                    pe.wait_ge(tp_evac, b + u - 1)
                    if u < 2:
                        src = [raw[:, par, (4 * u + j) * P:(4 * u + j + 1) * P] for j in range(4)]
                    elif u == 2:
                        src = [raw[:, par, IQ0 + j * P:IQ0 + (j + 1) * P] for j in range(4)]
                    else:
                        src = [raw[:, par, K0 + j * P:K0 + (j + 1) * P] for j in range(2)]
                        src.append(ikk[:, par, :, :].rearrange("p a d -> p (a d)"))
                    for j, s in enumerate(src):
                        ins = pe.transpose(tpb[:, u % 2, j, :], s, ident[:])
                    ins.then_inc(tp_done, 1)

            if first:
                pe.wait_ge(const_in, 80)
            transposes_x(0, 0)

            def step(n, par, k):
                if n + 1 < m:
                    transposes_x(n + 1, 1 - par)
                project(n, par, k)
                if n > 0:
                    transposes_q(n - 1, 1 - par)
            run(step)
            transposes_q(m - 1, (m - 1) % 2)

        @block.scalar
        def _(act):
            def square_x(n, par, k):
                act.wait_ge(x_in[par], 16 * (k + 1))
                if n > 0:
                    act.wait_ge(ssx_ok, n)
                if n > 1:
                    act.wait_ge(rsx_ok, n - 1)
                if n > 2:
                    act.wait_ge(ssh_ok, n - 2)
                act.activation(sq[:, 0:DM], x[:, par, :], ACT.Square, accum_out=ssx[:, par, :]).then_inc(ssx_ok, 1)

            def evac_x(n, par):
                b = t_base[n]
                if n > 1:
                    act.wait_ge(mm_done, 7 * (n - 1))
                for u in range(2):
                    act.wait_ge(tp_done, b + u + 1)
                    act.copy(xnT[:, par, 4 * u:4 * u + 4, :], tpb[:, u, :, :]).then_inc(tp_evac, 1)

            def evac_q(n, par, k):
                b = q_base[n]
                if n > 0:
                    act.wait_ge(st[1 - par], 16 * NST * ((n - 1) // 2 + 1))
                for u in range(4):
                    act.wait_ge(tp_done, b + u + 1)
                    if u < 2:
                        ins = act.copy(qTb[:, u * 512:(u + 1) * 512], tpb[:, u, :, :].rearrange("p a b -> p (a b)"))
                    elif u == 2:
                        ins = act.copy(iqTb[:], tpb[:, 0, :, :].rearrange("p a b -> p (a b)"))
                    else:
                        act.copy(kT[:, :, (t0 + n) * P:(t0 + n + 1) * P], tpb[:, 1, 0:2, :])
                        ins = act.copy(ikT[:, (t0 + n) * P:(t0 + n + 1) * P], tpb[:, 1, 2, :])
                    ins.then_inc(tp_evac, 1)

            def copy_raw(n, par, k):
                if n > 1:
                    act.wait_ge(tp_done, q_base[n - 2] + 4)
                    act.wait_ge(gate_ok, n - 1)
                act.wait_ge(st[par], 16 * NST * k)
                for c, (a, cw) in enumerate(CHUNKS):
                    act.wait_ge(mm_done, 7 * n + c + 1)
                    src = acc[:, c % 6, 0:cw]
                    if c == 2:
                        act.copy(v_nat[:, t0 + n, :], src[:, 256:512])
                        ins = act.copy(raw[:, par, K0:K0 + 256], src[:, 0:256])
                    elif c == 4:
                        act.mul(iw_nat[:, t0 + n, :], src[:, 64:72], IH ** -0.5 * ID ** -0.5)
                        ins = act.copy(raw[:, par, IK0:IK0 + 64], src[:, 0:64])
                    else:
                        ins = act.copy(raw[:, par, a:a + cw], src)
                    ins.then_inc(raw_ok, 1)

            def squares(n, par):
                if n > 0:
                    act.wait_ge(ssh_ok, n)
                act.wait_ge(raw_ok, 7 * n + 5)
                act.activation(sq[:, 0:1280], raw[:, par, 0:1280], ACT.Square)
                act.activation(sq[:, 1280:1344], raw[:, par, IK0:IK0 + 64], ACT.Square).then_inc(sq_ok, 1)
                act.wait_ge(raw_ok, 7 * n + 7)
                act.activation(sgate[:, par, :], raw[:, par, G0:ATT_IN], ACT.Exp, scale=-1.0).then_inc(exp_ok, 1)

            square_x(0, 0, 0)
            if m > 1:
                square_x(1, 1, 0)
            evac_x(0, 0)

            def step(n, par, k):
                if n + 1 < m:
                    evac_x(n + 1, 1 - par)
                if n + 2 < m:
                    square_x(n + 2, par, k + 1)
                copy_raw(n, par, k)
                if n > 0:
                    evac_q(n - 1, 1 - par, k if par else k - 1)
                squares(n, par)
            run(step)
            evac_q(m - 1, (m - 1) % 2, (m - 1) // 2)

        @block.vector
        def _(dve):
            if first:
                dve.wait_ge(const_in, 80)
                dve.tensor_scalar(gqs[:], gq[:], HD ** -0.5, None, ALU.mult).then_inc(gains_ok, 1)
                dve.wait_ge(gains_ok, 1)

            def norm_x(n, par):
                dve.wait_ge(rsx_ok, n + 1)
                dve.scalar_tensor_tensor(x[:, par, :], x[:, par, :], rsx[:, par, :], gx[:], ALU.mult, ALU.mult).then_inc(xn_ok, 1)
            norm_x(0, 0)
            if m > 1:
                norm_x(1, 1)

            def step(n, par, k):
                if n + 2 < m:
                    norm_x(n + 2, par)
                dve.wait_ge(sq_ok, n + 1)
                if n > 1:
                    dve.wait_ge(rsh_ok, n - 1)
                dve.tensor_reduce(ssh[:, par, 0:10], sq[:, 0:1280].rearrange("p (h d) -> p h d", h=10), AX.X, ALU.add)
                dve.tensor_reduce(ssh[:, par, 10:11], sq[:, 1280:1344], AX.X, ALU.add).then_inc(ssh_ok, 1)
                dve.wait_ge(rsh_ok, n + 1)
                for h in range(10):
                    r = raw[:, par, h * HD:(h + 1) * HD]
                    dve.scalar_tensor_tensor(r, r, rsh[:, par, h:h + 1], (gqs if h < H else gk)[:], ALU.mult, ALU.mult)
                r = raw[:, par, IK0:IK0 + 64]
                dve.wait_ge(st[par], 16 * NST * k)
                for a in range(2):
                    ins = dve.scalar_tensor_tensor(ikk[:, par, a, :], r, rsh[:, par, 10:11], gik[:], ALU.mult, ALU.mult)
                ins.then_inc(nat_ok, 1)
                dve.wait_ge(den_ok, n + 1)
                dve.reciprocal(sgate[:, par, :], sgate[:, par, :]).then_inc(rec_ok, 1)
                between(dve, n)
            run(step)


def sample_scores(nc, env):
    d, keep = env["dram"], env["keep"]
    HALF, CW = PAST // 2, 512
    NSTEP = 64
    RING = 4
    with ExitStack() as ctx:
        def sb(name, shape, dt=F32):
            return ctx.enter_context(nc.sbuf_tensor(name, shape, dt))

        def sem(name):
            return new_sem(nc, env, name)

        iqs = sb("iqs", [P, 4, P])
        bd = sb("iq_blockdiag", [P, 4, P])
        wred = sb("iw_reduce", [P, 4, 2, P])
        iwcol = sb("iwcol", [P, 4])
        delta16 = sb("delta16", [P, 16])
        ikn = sb("ik_new", [P, 4, DS])
        cmn = sb("new_causal", [P, DS])
        pti = sb("pt_int", [4, 8 * 16], I32)
        ptf = sb("pt_f", [4, 8 * 16])
        e4 = sb("e4", [4, P])
        j32 = sb("j32", [P, 1])
        idxf = sb("idx_f", [P, 8 * 16])
        idx = sb("idx_page", [P, 8, 16], U32)
        kraw = sb("kraw", [P, RING, 2, 4, ID])
        kTs = sb("kTs", [P, 2, CW])
        rl = sb("relu_s", [P, 2, CW])
        tps = ctx.enter_context(nc.psum_tensor("tps", [P, 2, 4, P], F32))
        sps = ctx.enter_context(nc.psum_tensor("sps", [P, 2, CW], F32))
        rps = ctx.enter_context(nc.psum_tensor("rps", [P, 2, CW], F32))
        mps = ctx.enter_context(nc.psum_tensor("mps", [P, CW], F32))
        ident, ikT, iw_nat, scores = keep["ident"], keep["ikT"], keep["iw_nat"], keep["scores"]

        loads = sem("loads")
        iwl_out = env["stores"]["iwl_out"]
        iwl_in = sem("iwl_in")
        zeroed = sem("zeroed")
        ptf_ok = sem("ptf_ok")
        ptb_ok = sem("ptb_ok")
        idx_ok = sem("idx_ok")
        prep_ok = sem("prep_ok")
        k_in = [sem(f"k_in{i}") for i in range(RING)]
        kT_done = sem("kT_done")
        kT_ok = sem("kT_ok")
        s_done = sem("s_done")
        relu_ok = sem("relu_ok")
        red_done = sem("red_done")
        sc_ok = sem("sc_ok")
        dv = sem("dve_chain_scores")
        steps = [(c, s, p) for c in range(HALF // CW) for s in range(2) for p in range(4)]

        block = ctx.enter_context(nc.Block())

        @block.sync
        def _(sp):
            sp.dma_start(iqs[:].rearrange("p a b -> p (a b)"), d["iqT_d"][0:P, :]).then_inc(loads, 16)
            sp.dma_start(delta16[:], d["c_delta16"]).then_inc(loads, 16)
            sp.dma_start(cmn[:], d["c_new_causal"]).then_inc(loads, 16)
            sp.dma_start(e4[:], d["c_e4"]).then_inc(loads, 16)
            sp.dma_start(j32[:], d["c_j32"]).then_inc(loads, 16)
            with nc.allow_non_contiguous_dma(reason="512 page ids"):
                sp.dma_start(pti[:], d["page_table"].rearrange("b (g k) -> k (b g)", k=4)).then_inc(loads, 16)
                for b in range(DB):
                    sp.dma_start(d["iwl_d"][b].rearrange("h t -> t h"), iw_nat[b * DS:(b + 1) * DS, 0, :]).then_inc(iwl_out, 16)
                sp.wait_ge(iwl_out, 16 * DB)
                sp.dma_start(iwcol[:], d["iwl_d"].rearrange("(p b) h t -> (b h t) p", p=4)).then_inc(iwl_in, 16)

        @block.gpsimd
        def _(pool):
            pool.memset(bd[:], 0.0)
            pool.memset(wred[:], 0.0).then_inc(zeroed, 1)
            pool.wait_ge(idx_ok, 1)
            rows = d["cache_idx_k"].rearrange("n (j r) l e -> (n j) (r l e)", r=4)
            for j, (c, s, p) in enumerate(steps):
                if j >= RING:
                    pool.wait_ge(kT_done, j - RING + 1)
                for b2 in range(2):
                    pool.indirect_dma_start(
                        kraw[:, j % RING, b2, :, :].rearrange("p r e -> p (r e)"), None, rows,
                        bass.IndirectOffsetOnAxis(ap=idx[:, 2 * p + b2, s * 8 + c:s * 8 + c + 1], axis=0),
                    ).then_inc(k_in[j % RING], 16)

        @block.tensor
        def _(pe):
            pe.wait_ge(ptf_ok, 1)
            pe.matmul(mps[:, 0:128], e4[:], ptf[:], start=True, stop=True).then_inc(ptb_ok, 1)

            def turn(j):
                pe.wait_ge(k_in[j % RING], 32 * (j // RING + 1))
                if j >= 2:
                    pe.wait_ge(kT_ok, j - 1)
                for b2 in range(2):
                    for rp in range(2):
                        ins = pe.transpose(tps[:, j % 2, 2 * b2 + rp, :],
                                           kraw[:, j % RING, b2, 2 * rp:2 * rp + 2, :].rearrange("p r e -> p (r e)"), ident[:])
                ins.then_inc(kT_done, 1)

            def dots(j):
                c, s, p = steps[j]
                pe.wait_ge(kT_ok, j + 1)
                if j >= 2:
                    pe.wait_ge(relu_ok, j - 1)
                pe.matmul(sps[:, j % 2, :], bd[:, p, :], kTs[:, j % 2, :], start=True, stop=True).then_inc(s_done, 1)

            def head_sum(j):
                c, s, p = steps[j]
                pe.wait_ge(relu_ok, j + 1)
                if c >= 2 and s == 0 and p == 0:
                    pe.wait_ge(sc_ok, c - 1)
                pe.matmul(rps[:, c % 2, :], wred[:, p, s, :], rl[:, j % 2, :],
                          start=(s == 0 and p == 0), stop=(s == 1 and p == 3)).then_inc(red_done, 1)

            pe.wait_ge(prep_ok, 1)
            turn(0)
            for j in range(NSTEP):
                if j + 1 < NSTEP:
                    turn(j + 1)
                dots(j)
                if j >= 1:
                    head_sum(j - 1)
            head_sum(NSTEP - 1)
            for p in range(4):
                j = NSTEP + p
                pe.wait_ge(relu_ok, j - 1)
                pe.matmul(sps[:, j % 2, 0:DS], bd[:, p, :], ikn[:, p, :], start=True, stop=True).then_inc(s_done, 1)
                if p == 0:
                    pe.wait_ge(ptb_ok, 1)
                    pe.wait_ge(idx_ok, 1)
                pe.wait_ge(relu_ok, j + 1)
                pe.matmul(mps[:, 0:DS], wred[:, p, 1, :], rl[:, j % 2, 0:DS], start=(p == 0), stop=(p == 3)).then_inc(red_done, 1)

        @block.scalar
        def _(act):
            def scores_out(c):
                act.wait_ge(red_done, 8 * (c + 1))
                act.copy(scores[:, c * CW:(c + 1) * CW], rps[:, c % 2, :]).then_inc(sc_ok, 1)
            for j in range(NSTEP + 4):
                act.wait_ge(s_done, j + 1)
                if j >= 2:
                    act.wait_ge(red_done, j - 1)
                n = CW if j < NSTEP else DS
                act.activation(rl[:, j % 2, 0:n], sps[:, j % 2, 0:n], ACT.Relu).then_inc(relu_ok, 1)
                if j % 8 == 1 and 8 < j:
                    scores_out(j // 8 - 1)

        @block.vector
        def _(dve):
            link = chain(dve, dv)
            dve.wait_ge(loads, 96)
            dve.tensor_copy(ptf[:], pti[:]).then_inc(ptf_ok, 1)
            dve.wait_ge(ptb_ok, 1)
            link(dve.tensor_scalar(idxf[:], mps[:, 0:128], 32.0, j32[:], ALU.mult, ALU.add))
            dve.tensor_copy(idx[:].rearrange("p a b -> p (a b)"), idxf[:]).then_inc(idx_ok, 1)
            dve.wait_ge(zeroed, 1)
            for b2 in range(2):
                for hp in range(2):
                    dst = bd[b2 * 64:(b2 + 1) * 64, :, b2 * 64:(b2 + 1) * 64].rearrange("k p (hh two t) -> k p hh two t", two=2, t=DS)[:, :, :, hp, :]
                    src = iqs[hp * 64:(hp + 1) * 64, :, 0:NS].rearrange("k hh (p two t) -> k p hh two t", two=2, t=DS)[:, :, :, b2, :]
                    dve.tensor_copy(dst, src)
                dve.tensor_copy(ikn[b2 * 64:(b2 + 1) * 64, :, :],
                                ikT[b2 * 64:(b2 + 1) * 64, 0:NS].rearrange("k (p two t) -> k p two t", two=2, t=DS)[:, :, b2, :])
            dve.wait_ge(iwl_in, 16)
            for p in range(4):
                for s in range(2):
                    a = 64 * s + 16 * p
                    ins = dve.tensor_scalar(wred[:, p, s, a:a + 16], delta16[:], iwcol[:, p:p + 1], None, ALU.mult)
            ins.then_inc(prep_ok, 1)
            for j in range(NSTEP):
                dve.wait_ge(kT_done, j + 1)
                if j >= 2:
                    dve.wait_ge(s_done, j - 1)
                for b2 in range(2):
                    for r2 in range(2):
                        dst = kTs[b2 * 64:(b2 + 1) * 64, j % 2, :].rearrange("k (q rp r2) -> k rp q r2", r2=2, rp=2)[:, :, :, r2]
                        ins = dve.tensor_copy(dst, tps[r2 * 64:(r2 + 1) * 64, j % 2, 2 * b2:2 * b2 + 2, :])
                ins.then_inc(kT_ok, 1)
            dve.wait_ge(red_done, NSTEP + 4)
            dve.tensor_copy(scores[:, HALF - CW:HALF], rps[:, (HALF // CW - 1) % 2, :])
            link(dve.tensor_tensor(scores[:, HALF:HALF + DS], mps[:, 0:DS], cmn[:], ALU.add))


def extraction(env, sem):
    keep = env["keep"]
    scores, top_v, top_i = keep["scores"], keep["top_v"], keep["top_i"]
    state = {}

    def rounds(dve, n):
        link = state.setdefault("link", chain(dve, sem))
        for r in range(4 * n, 4 * n + 4):
            v = top_v[:, 8 * r:8 * r + 8]
            link(dve.max(v, scores[:]))
            dve.max_index(top_i[:, 8 * r:8 * r + 8], v, scores[:])
            link(dve.match_replace(scores[:], v, scores[:], -3e38))
    return rounds


def sample_select(nc, env):
    d, keep = env["dram"], env["keep"]
    top_v, top_i, ident = keep["top_v"], keep["top_i"], keep["ident"]
    rowidx, mask_s, mask_n = keep["rowidx"], keep["mask_s"], keep["mask_n"]
    with ExitStack() as ctx:
        def sb(name, shape, dt=F32):
            return ctx.enter_context(nc.sbuf_tensor(name, shape, dt))

        def sem(name):
            return new_sem(nc, env, name)

        off = sb("half_off", [P, 1])
        idxf = sb("key_f", [P, TOPK])
        rv = sb("rev_v", [NS, TOPK])
        ri = sb("rev_i", [NS, TOPK])
        take = sb("take_a", [NS, TOPK])
        key = sb("key", [NS, TOPK])
        keyi = sb("key_i", [NS, TOPK], I32)
        pgi = sb("page_i", [NS, TOPK], I32)
        ofi = sb("off_i", [NS, TOPK], I32)
        pg = sb("page_f", [NS, TOPK])
        of = sb("off_f", [NS, TOPK])
        phys = sb("phys", [NS, TOPK])
        tmp = sb("tmp_page", [NS, 2, TOPK])
        pti = sb("pt_rows_i", [NS, NPG], I32)
        ptf = sb("pt_rows", [NS, NPG])
        bias = sb("slot_bias", [NS, TOPK])
        sel = sb("sel_new", [NS, DS])
        selb = sb("sel_bias", [NS, 4, DS])
        hit = sb("hit", [NS, TOPK])
        eq = sb("expand_q", [NS, 4, P])
        cmn = sb("new_allowed", [P, 32])
        tp = ctx.enter_context(nc.psum_tensor("tp_rows", [P, 2, NS], F32))
        mp = ctx.enter_context(nc.psum_tensor("mp", [P, 4, 512], F32))
        loads = sem("sel_loads")
        key_ok = sem("key_ok")
        rows_ok = sem("rows_ok")
        mm = sem("sel_mm")
        dv = sem("dve_chain_select")
        block = ctx.enter_context(nc.Block())

        @block.sync
        def _(sp):
            sp.dma_start(off[:], d["c_half_off"]).then_inc(loads, 16)
            sp.dma_start(eq[:].rearrange("p a b -> p (a b)"), d["c_expand_q"]).then_inc(loads, 16)
            sp.dma_start(cmn[:], d["c_new_allowed"]).then_inc(loads, 16)
            for b in range(DB):
                sp.dma_start(pti[b * DS:(b + 1) * DS, :], d["page_table"][b:b + 1, :].partition_broadcast(DS)).then_inc(loads, 16)

        @block.vector
        def _(dve):
            link = chain(dve, dv)
            dve.wait_ge(loads, 16 * 11)
            link(dve.tensor_copy(idxf[:], top_i[:]))
            link(dve.tensor_scalar(idxf[:], idxf[:], off[:], None, ALU.add))
            link(dve.tensor_copy(rv[:], top_v[NS:P, ::-1]))
            link(dve.tensor_copy(ri[:], idxf[NS:P, ::-1]))
            link(dve.tensor_tensor(take[:], top_v[0:NS, :], rv[:], ALU.is_ge))
            link(dve.tensor_tensor(key[:], idxf[0:NS, :], ri[:], ALU.subtract))
            link(dve.tensor_tensor(key[:], key[:], take[:], ALU.mult))
            link(dve.tensor_tensor(key[:], key[:], ri[:], ALU.add))
            link(dve.tensor_scalar(bias[:], key[:], float(PAST), -BIG, ALU.is_ge, ALU.mult))
            for s in range(DS):
                link(dve.tensor_scalar(hit[:], key[:], float(PAST + s), 0.0, ALU.is_equal, ALU.add, accum_out=sel[:, s:s + 1]))
            for a in range(4):
                link(dve.tensor_scalar(selb[:, a, :], sel[:], -1.0, BIG, ALU.add, ALU.mult))
            dve.nop().then_inc(key_ok, 1) if False else None
            link(dve.tensor_copy(keyi[:], key[:]))
            link(dve.tensor_scalar(pgi[:], keyi[:], 7, None, ALU.arith_shift_right))
            link(dve.tensor_scalar(ofi[:], keyi[:], 127, None, ALU.bitwise_and))
            link(dve.tensor_copy(pg[:], pgi[:]))
            link(dve.tensor_copy(of[:], ofi[:]))
            link(dve.tensor_copy(ptf[:], pti[:]))
            link(dve.memset(phys[:], 0.0))
            for g in range(NPG):
                link(dve.tensor_scalar(tmp[:, g % 2, :], pg[:], float(g), ptf[:, g:g + 1], ALU.is_equal, ALU.mult))
                link(dve.tensor_tensor(phys[:], phys[:], tmp[:, g % 2, :], ALU.add))
            dve.scalar_tensor_tensor(phys[:], phys[:], float(PAGE), of[:], ALU.mult, ALU.add).then_inc(key_ok, 1)
            dve.wait_ge(mm, 1)
            link(dve.tensor_copy(rowidx[:], tp[:]))
            dve.wait_ge(mm, 2)
            link(dve.tensor_copy(mask_s[:], mp[:, :, 0:TOPK]))
            for t in range(4):
                link(dve.tensor_tensor(mask_n[:, t, :], mp[:, t, TOPK:TOPK + 32], cmn[:], ALU.add))

        @block.tensor
        def _(pe):
            pe.wait_ge(key_ok, 1)
            for c in range(2):
                ins = pe.transpose(tp[:, c, :], phys[:, c * P:(c + 1) * P], ident[0:NS, 0:NS])
            ins.then_inc(mm, 1)
            for t in range(4):
                pe.matmul(mp[:, t, 0:TOPK], eq[:, t, :], bias[:], start=True, stop=True)
                ins = pe.matmul(mp[:, t, TOPK:TOPK + 32], eq[:, t, :], selb[:].rearrange("p a b -> p (a b)"), start=True, stop=True)
            ins.then_inc(mm, 1)


def sample_attend(nc, env):
    d, keep = env["dram"], env["keep"]
    ident, kT, og = keep["ident"], keep["kT"], keep["og_s"]
    rowidx, mask_s, mask_n = keep["rowidx"], keep["mask_s"], keep["mask_n"]
    KR = 8
    QT = 16
    NQT = NS // QT
    with ExitStack() as ctx:
        def sb(name, shape, dt=F32):
            return ctx.enter_context(nc.sbuf_tensor(name, shape, dt))

        def sem(name):
            return new_sem(nc, env, name)

        qs = sb("qs", [P, H, P])
        qTq = sb("qTq", [P, NS, H])
        kg = sb("kg", [P, KR, 256])
        vg = sb("vg", [P, 2, 2 * QT, 256])
        ktg = sb("ktg", [P, 2, 2, P])
        vnew = sb("vnew", [32, NQT, HD])
        gnat = sb("gnat", [NS, DM])
        gT = sb("gT", [P, H, NS])
        lt = sb("lt", [P, 2, P])
        lg = sb("lg", [P, TOPK + 32])
        pr = sb("pr", [P, TOPK + 32])
        mx = sb("mx", [P, 1])
        rs = sb("rs", [P, 1])
        pT = sb("pT", [P, 3, P])
        tpk = ctx.enter_context(nc.psum_tensor("tpk", [P, 2, 512], F32))
        ltp = ctx.enter_context(nc.psum_tensor("ltp", [P, 512], F32))
        lgp = ctx.enter_context(nc.psum_tensor("lgp", [P, 512], F32))
        ptp = ctx.enter_context(nc.psum_tensor("ptp", [P, 512], F32))
        op = ctx.enter_context(nc.psum_tensor("op", [P, 512], F32))
        loads = sem("sa_loads")
        k_in = [sem(f"kg_in{i}") for i in range(KR)]
        v_in = [sem("vg_in0"), sem("vg_in1")]
        qTq_ok = sem("qTq_ok")
        gT_done = sem("gT_done")
        gT_ok = sem("gT_ok")
        kT_done = sem("kgT_done")
        kT_ok = sem("kgT_ok")
        dot_done = sem("dot_done")
        lt_done = sem("lt_done")
        lt_ok = sem("lt_ok")
        lg_done = sem("lg_done")
        mx_ok = sem("mx_ok")
        ex_ok = sem("ex_ok")
        pr_ok = sem("pr_ok")
        pt_done = sem("pt_done")
        pt_ok = sem("pt_ok")
        o_done = sem("o_done")
        o_ok = sem("o_ok")
        dv = sem("dve_chain_sa")
        block = ctx.enter_context(nc.Block())
        ck = d["cache_k"].rearrange("n j l g e -> (n j) (l g e)")
        cv = d["cache_v"].rearrange("n j l g e -> (n j) (l g e)")

        @block.sync
        def _(sp):
            sp.dma_start(qs[:].rearrange("p a b -> p (a b)"), d["qT_d"][0:P, :]).then_inc(loads, 16)
            sp.dma_start(gnat[:], d["gate_d"][0:NS, :]).then_inc(loads, 16)
            for g in range(G):
                sp.dma_start(vnew[g * QT:(g + 1) * QT, :, :],
                             d["v_all"][0:NS, g * HD:(g + 1) * HD].rearrange("(t q) e -> q t e", t=NQT)).then_inc(loads, 16)

        @block.gpsimd
        def _(pool):
            for t in range(NQT):
                for u in range(2 * QT):
                    q, c = t * QT + u // 2, u % 2
                    j = t * 2 * QT + u
                    if j >= KR:
                        pool.wait_ge(kT_done, j - KR + 1)
                    pool.indirect_dma_start(kg[:, j % KR, :], None, ck,
                                            bass.IndirectOffsetOnAxis(ap=rowidx[:, c, q:q + 1], axis=0)).then_inc(k_in[j % KR], 16)
                    if t >= 2 and u == 0:
                        pool.wait_ge(o_done, t - 1)
                    pool.indirect_dma_start(vg[:, t % 2, u, :], None, cv,
                                            bass.IndirectOffsetOnAxis(ap=rowidx[:, c, q:q + 1], axis=0)).then_inc(v_in[t % 2], 16)

        @block.tensor
        def _(pe):
            pe.wait_ge(loads, 64)
            for h in range(H):
                ins = pe.transpose(tpk[:, h // 4, (h % 4) * NS:(h % 4 + 1) * NS], gnat[:, h * HD:(h + 1) * HD], ident[0:NS, 0:NS])
            ins.then_inc(gT_done, 1)
            pe.wait_ge(gT_ok, 1)
            pe.wait_ge(qTq_ok, 1)

            def turn(j):
                pe.wait_ge(k_in[j % KR], 16 * (j // KR + 1))
                if j >= 2:
                    pe.wait_ge(kT_ok, j - 1)
                for g in range(G):
                    ins = pe.transpose(tpk[:, j % 2, g * P:(g + 1) * P], kg[:, j % KR, g * HD:(g + 1) * HD], ident[:])
                ins.then_inc(kT_done, 1)

            def dots(j):
                t, u = divmod(j, 2 * QT)
                q, c = t * QT + u // 2, u % 2
                pe.wait_ge(kT_ok, j + 1)
                if u == 0 and t >= 1:
                    pe.wait_ge(lt_ok, t)
                for g in range(G):
                    a = c * P + (u // 2) * H + g * GRP
                    ins = pe.matmul(ltp[:, a:a + GRP], ktg[:, j % 2, g, :], qTq[:, q, g * GRP:(g + 1) * GRP], start=True, stop=True)
                ins.then_inc(dot_done, 1)

            NJ = NQT * 2 * QT
            turn(0)
            for t in range(NQT):
                for u in range(2 * QT):
                    j = t * 2 * QT + u
                    if j + 1 < NJ:
                        turn(j + 1)
                    dots(j)
                pe.wait_ge(lt_ok, t + 1)
                if t >= 1:
                    pe.wait_ge(mx_ok, t)
                for c in range(2):
                    pe.transpose(lgp[:, c * P:(c + 1) * P], lt[:, c, :], ident[:])
                pe.matmul(lgp[:, TOPK:TOPK + 32], qTq[:, t * QT:(t + 1) * QT, :].rearrange("p a b -> p (a b)"),
                          kT[:, :, t * QT:(t + 1) * QT], start=True, stop=True).then_inc(lg_done, 1)
                pe.wait_ge(pr_ok, t + 1)
                for c in range(2):
                    pe.transpose(ptp[:, c * P:(c + 1) * P], pr[:, c * P:(c + 1) * P], ident[:])
                pe.transpose(ptp[0:32, 256:256 + P], pr[:, TOPK:TOPK + 32], ident[:]).then_inc(pt_done, 1)
                pe.wait_ge(pt_ok, t + 1)
                pe.wait_ge(v_in[t % 2], 16 * 2 * QT * (t // 2 + 1))
                if t >= 1:
                    pe.wait_ge(o_ok, t)
                pe.matmul(op[:, 0:P], vnew[:, t, :], pT[0:32, 2, :], start=True, stop=False, skip_group_check=True)
                for u in range(2 * QT):
                    for g in range(G):
                        a = (u // 2) * H + g * GRP
                        ins = pe.matmul(op[:, a:a + GRP], vg[:, t % 2, u, g * HD:(g + 1) * HD], pT[:, u % 2, a:a + GRP],
                                        start=False, stop=(u == 2 * QT - 1 and g == G - 1), skip_group_check=True)
                ins.then_inc(o_done, 1)

        @block.scalar
        def _(act):
            for t in range(NQT):
                for u in range(2 * QT):
                    j = t * 2 * QT + u
                    act.wait_ge(kT_done, j + 1)
                    if j >= 2:
                        act.wait_ge(dot_done, j - 1)
                    act.copy(ktg[:, j % 2, :, :].rearrange("p a b -> p (a b)"), tpk[:, j % 2, 0:256]).then_inc(kT_ok, 1)
                act.wait_ge(mx_ok, t + 1)
                act.activation(pr[:], lg[:], ACT.Exp, bias=mx[:], accum_out=rs[:]).then_inc(ex_ok, 1)

        @block.vector
        def _(dve):
            link = chain(dve, dv)
            dve.wait_ge(loads, 64)
            dve.tensor_copy(qTq[:], qs[:, :, 0:NS].rearrange("p h q -> p q h")).then_inc(qTq_ok, 1)
            dve.memset(og[:], 0.0)
            dve.wait_ge(gT_done, 1)
            for a in range(2):
                ins = dve.tensor_copy(gT[:, 4 * a:4 * a + 4, :].rearrange("p a b -> p (a b)"), tpk[:, a, 0:256])
            ins.then_inc(gT_ok, 1)
            dve.wait_ge(gT_ok, 1)
            for t in range(NQT):
                dve.wait_ge(dot_done, (t + 1) * 2 * QT)
                if t >= 1:
                    dve.wait_ge(lg_done, t)
                dve.tensor_copy(lt[:].rearrange("p a b -> p (a b)"), ltp[:, 0:256]).then_inc(lt_ok, 1)
                dve.wait_ge(lg_done, t + 1)
                if t >= 1:
                    dve.wait_ge(pt_done, t)
                link(dve.tensor_tensor(lg[:, 0:TOPK], lgp[:, 0:TOPK], mask_s[:, t, :], ALU.add))
                link(dve.tensor_tensor(lg[:, TOPK:], lgp[:, TOPK:TOPK + 32], mask_n[:, t, :], ALU.add))
                dve.tensor_reduce(mx[:], lg[:], AX.X, ALU.max, negate=True).then_inc(mx_ok, 1)
                dve.wait_ge(ex_ok, t + 1)
                link(dve.reciprocal(rs[:], rs[:]))
                dve.tensor_scalar(pr[:], pr[:], rs[:], None, ALU.mult).then_inc(pr_ok, 1)
                dve.wait_ge(pt_done, t + 1)
                if t >= 1:
                    dve.wait_ge(o_done, t)
                dve.tensor_copy(pT[:, 0:2, :].rearrange("p a b -> p (a b)"), ptp[:, 0:256])
                dve.tensor_copy(pT[0:32, 2, :], ptp[0:32, 256:256 + P]).then_inc(pt_ok, 1)
                dve.wait_ge(o_done, t + 1)
                dve.tensor_tensor(og[:, :, t * QT:(t + 1) * QT], op[:, 0:P].rearrange("p (q h) -> p h q", h=H),
                                  gT[:, :, t * QT:(t + 1) * QT], ALU.mult).then_inc(o_ok, 1)


def prompt_attend(nc, env):
    d, keep = env["dram"], env["keep"]
    ident, kT, ikT, v_nat, iw_nat, og_s = (keep[k] for k in ("ident", "kT", "ikT", "v_nat", "iw_nat", "og_s"))
    NB = SEQ // P
    FREE = TOPK // P
    with ExitStack() as ctx:
        def sb(name, shape, dt=F32):
            return ctx.enter_context(nc.sbuf_tensor(name, shape, dt))

        def sem(name):
            return new_sem(nc, env, name)

        wo = sb("w_out_att", [P, H, DM])
        causal = sb("causal_p", [P, P])
        q = sb("q_blk", [P, 2, H, P])
        iq = sb("iq_blk", [P, 2, IH // 2, P])
        gate = sb("gate_blk", [P, 2, DM])
        x = sb("x_blk", [P, 2, DM])
        rl = sb("relu_blk", [P, 2, SEQ])
        sc = sb("score_blk", [P, 2, SEQ])
        v8 = sb("v8", [P, 8])
        lm = sb("lm", [P, 2, SEQ])
        mx = sb("mx_blk", [P, H])
        nmx = sb("nmx_blk", [P, H])
        rs = sb("rs_blk", [P, H])
        ri = sb("ri_blk", [P, H])
        pT = sb("pT_blk", [P, 2, NB, P])
        og = sb("og_blk", [P, 2, DM])
        ogT = sb("ogT_blk", [P, H, P])
        ring = ctx.enter_context(nc.psum_tensor("ring", [P, 2, SEQ], F32))
        tpb = ctx.enter_context(nc.psum_tensor("tp_blk", [P, 2, 4, P], F32))
        ops = ctx.enter_context(nc.psum_tensor("o_blk", [P, 2, 512], F32))

        once = env["stores"]["pa_once"]
        q_in = [sem("q_in0"), sem("q_in1")]
        iq_in = [sem("iq_in0"), sem("iq_in1")]
        ring_done = sem("ring_done")
        relu_ok = sem("relu_blk_ok")
        acc_ok = sem("acc_ok")
        lm_ok = sem("lm_ok")
        y_ok = sem("y_ok")
        exp_ok = sem("p_ok")
        tp_done = sem("tpb_done")
        tp_evac = sem("tpb_evac")
        o_done = sem("ob_done")
        og_ok = sem("og_ok")
        ogT_use = sem("ogT_use")
        y_out = [env["stores"][f"y1_out{u}"] for u in range(2)]
        dv = sem("dve_chain_pa")

        uses = [("y", 0)]
        for i in range(NB):
            if FREE <= i + 1 < NB:
                uses += [("s", (i + 1 - FREE) * IH + h) for h in range(IH)]
            uses += [("l", i * H + h) for h in range(H)] + [("y", i + 1)]
        at = {u: n for n, u in enumerate(uses)}
        emptied = {"y": y_ok, "s": relu_ok, "l": lm_ok}
        tp_at, n = {}, 0
        for i in range(NB):
            for h in range(H + 1):
                tp_at[i, h] = n
                n += (i + 4) // 4 if h < H else 2

        block = ctx.enter_context(nc.Block())

        @block.sync
        def _(sp):
            sp.dma_start(causal[:], d["c_causal"]).then_inc(once, 16)
            sp.dma_start(wo[:], d["att_w_out"].rearrange("l (h p) n -> p (l h) n", p=P)).then_inc(once, 16)
            sp.dma_start(x[:, 0, :], d["x_all"][0:P, :]).then_inc(once, 16)
            sp.wait_ge(y_ok, 1)
            sp.dma_start(d["y1_d"][0:P, :], x[:, 0, :]).then_inc(once, 16)
            sp.wait_ge(once, 64)
            for i in range(NB):
                u, r = i % 2, slice((i + 1) * P, (i + 2) * P)
                if i >= 2:
                    sp.wait_ge(y_ok, i)
                    sp.dma_start(d["y1_d"][(i - 1) * P:i * P, :], x[:, u, :]).then_inc(y_out[u], 16)
                    sp.wait_ge(y_out[u], 16 * (i // 2))
                sp.dma_start(q[:, u, :, :].rearrange("p a b -> p (a b)"), d["qT_d"][r, :]).then_inc(q_in[u], 16)
                sp.dma_start(gate[:, u, :], d["gate_d"][r, :]).then_inc(q_in[u], 16)
                sp.dma_start(x[:, u, :], d["x_all"][r, :]).then_inc(q_in[u], 16)
                if FREE <= i + 1 < NB:
                    if i > FREE:
                        sp.wait_ge(relu_ok, (i - FREE) * IH)
                    sp.dma_start(iq[:, 1 - u, :, :].rearrange("p a b -> p (a b)"),
                                 d["iqT_d"][(i + 2) * P:(i + 3) * P, :]).then_inc(iq_in[1 - u], 16)
            for i in (NB, NB + 1):
                u = i % 2
                sp.wait_ge(y_ok, i)
                sp.dma_start(d["y1_d"][(i - 1) * P:i * P, :], x[:, u, :]).then_inc(y_out[u], 16)
            for u in range(2):
                sp.wait_ge(y_out[u], 16 * (NB // 2))

        @block.tensor
        def _(pe):
            def claim(u):
                n = at[u]
                if n >= 2:
                    kind, k = uses[n - 2]
                    pe.wait_ge(emptied[kind], k + 1)
                return ring[:, n % 2, :]

            def key_scores(i):
                pe.wait_ge(iq_in[i % 2], 16 * ((i - FREE) // 2 + 1))
                for h in range(IH):
                    dst, half = claim(("s", (i - FREE) * IH + h)), h % 2
                    for a in range(0, (i + 1) * P, 512):
                        w = min(512, (i + 1) * P - a)
                        ins = pe.matmul(dst[:, a:a + w], iq[half * 64:half * 64 + 64, i % 2, h // 2, :],
                                        ikT[half * 64:half * 64 + 64, P + a:P + a + w], start=True, stop=True)
                    ins.then_inc(ring_done, 1)

            def logits(i, h):
                dst = claim(("l", i * H + h))
                for a in range(0, (i + 1) * P, 512):
                    w = min(512, (i + 1) * P - a)
                    ins = pe.matmul(dst[:, a:a + w], q[:, i % 2, h, :], kT[:, h // GRP, P + a:P + a + w], start=True, stop=True)
                ins.then_inc(ring_done, 1)

            def groups(base, tiles, src):
                for n in range(0, tiles, 4):
                    b = base + n // 4
                    if b >= 2:
                        pe.wait_ge(tp_evac, b - 1)
                    for k in range(n, min(n + 4, tiles)):
                        ins = pe.transpose(tpb[:, b % 2, k - n, :], src[:, k * P:(k + 1) * P], ident[:])
                    ins.then_inc(tp_done, 1)

            def out_proj(n, lhs):
                dst = claim(("y", n))
                for a in range(0, DM, 512):
                    for h in range(H):
                        ins = pe.matmul(dst[:, a:a + 512], lhs[:, h, :], wo[:, h, a:a + 512], start=(h == 0), stop=(h == H - 1))
                ins.then_inc(ring_done, 1)

            pe.wait_ge(once, 48)
            out_proj(0, og_s)
            for i in range(NB):
                if FREE <= i + 1 < NB:
                    key_scores(i + 1)
                pe.wait_ge(q_in[i % 2], 48 * (i // 2 + 1))
                logits(i, 0)
                logits(i, 1)
                for h in range(H):
                    hc = i * H + h
                    pe.wait_ge(exp_ok, hc + 1)
                    groups(tp_at[i, h], i + 1, lm[:, hc % 2, :])
                    pe.wait_ge(tp_evac, tp_at[i, h + 1])
                    if hc >= 2:
                        pe.wait_ge(og_ok, hc - 1)
                    for k in range(i + 1):
                        g = h // GRP
                        ins = pe.matmul(ops[:, hc % 2, 0:HD], pT[:, hc % 2, k, :], v_nat[:, k + 1, g * HD:(g + 1) * HD],
                                        start=(k == 0), stop=(k == i))
                    ins.then_inc(o_done, 1)
                    if h + 2 < H:
                        logits(i, h + 2)
                pe.wait_ge(og_ok, (i + 1) * H)
                groups(tp_at[i, H], H, og[:, i % 2, :])
                pe.wait_ge(tp_evac, tp_at[i, H] + 2)
                out_proj(i + 1, ogT)

        @block.scalar
        def _(act):
            def relus(i):
                for h in range(IH):
                    n = (i - FREE) * IH + h
                    act.wait_ge(ring_done, at["s", n] + 1)
                    if n >= 2:
                        act.wait_ge(acc_ok, n - 1)
                    w = (i + 1) * P
                    act.activation(rl[:, n % 2, 0:w], ring[:, at["s", n] % 2, 0:w], ACT.Relu).then_inc(relu_ok, 1)

            def evac(base, tiles, dst):
                for n in range(0, tiles, 4):
                    b, m = base + n // 4, min(4, tiles - n)
                    act.wait_ge(tp_done, b + 1)
                    act.copy(dst[:, n:n + m, :].rearrange("p a b -> p (a b)"),
                             tpb[:, b % 2, 0:m, :].rearrange("p a b -> p (a b)")).then_inc(tp_evac, 1)

            for i in range(NB):
                if FREE <= i + 1 < NB:
                    relus(i + 1)
                for h in range(H):
                    hc, w = i * H + h, (i + 1) * P
                    act.wait_ge(lm_ok, hc + 1)
                    act.activation(lm[:, hc % 2, 0:w], lm[:, hc % 2, 0:w], ACT.Exp, bias=nmx[:, h:h + 1],
                                   accum_out=rs[:, h:h + 1]).then_inc(exp_ok, 1)
                    if hc >= 2:
                        act.wait_ge(o_done, hc - 1)
                    evac(tp_at[i, h], i + 1, pT[:, hc % 2, :, :])
                if i >= 1:
                    act.wait_ge(ring_done, at["y", i] + 1)
                evac(tp_at[i, H], H, ogT)

        @block.vector
        def _(dve):
            link = chain(dve, dv)

            def add_heads(i):
                w = (i + 1) * P
                s = sc[:, i % 2, 0:w]
                for h in range(IH):
                    n = (i - FREE) * IH + h
                    dve.wait_ge(relu_ok, n + 1)
                    if h == 0:
                        ins = dve.tensor_scalar(s, rl[:, n % 2, 0:w], iw_nat[:, i + 1, 0:1], None, ALU.mult)
                    else:
                        dve.wait_ge(acc_ok, n)
                        ins = dve.scalar_tensor_tensor(s, rl[:, n % 2, 0:w], iw_nat[:, i + 1, h:h + 1], s, ALU.mult, ALU.add)
                    ins.then_inc(acc_ok, 1)
                dve.wait_ge(acc_ok, (i - FREE + 1) * IH)
                diag = sc[:, i % 2, i * P:w]
                link(dve.tensor_tensor(diag, diag, causal[:], ALU.add))

            def search(i, rounds):
                s = sc[:, i % 2, 0:(i + 1) * P]
                for _ in range(rounds):
                    link(dve.max(v8[:], s))
                    link(dve.match_replace(s, v8[:], s, -3e38))

            def masked(i, h):
                hc, w = i * H + h, (i + 1) * P
                dve.wait_ge(ring_done, at["l", hc] + 1)
                if hc >= 2:
                    dve.wait_ge(o_done, hc - 1)
                link(dve.tensor_tensor_reduce(lm[:, hc % 2, 0:w], ring[:, at["l", hc] % 2, 0:w], sc[:, i % 2, 0:w],
                                              1.0, -3e38, ALU.add, ALU.max, mx[:, h:h + 1]))
                dve.tensor_scalar(nmx[:, h:h + 1], mx[:, h:h + 1], -1.0, None, ALU.mult).then_inc(lm_ok, 1)

            def normed(i, h):
                hc = i * H + h
                dve.wait_ge(exp_ok, hc + 1)
                link(dve.reciprocal(ri[:, h:h + 1], rs[:, h:h + 1]))
                dve.wait_ge(o_done, hc + 1)
                dve.scalar_tensor_tensor(og[:, i % 2, h * HD:(h + 1) * HD], ops[:, hc % 2, 0:HD], ri[:, h:h + 1],
                                         gate[:, i % 2, h * HD:(h + 1) * HD], ALU.mult, ALU.mult).then_inc(og_ok, 1)

            def residual(n, xv):
                dve.wait_ge(ring_done, at["y", n] + 1)
                dve.tensor_tensor(xv, xv, ring[:, at["y", n] % 2, :], ALU.add).then_inc(y_ok, 1)

            dve.wait_ge(once, 48)
            residual(0, x[:, 0, :])
            dve.memset(sc[:, 1, 0:P], 0.0)
            dve.tensor_copy(sc[:, 0, 0:P], causal[:])
            link(dve.tensor_copy(sc[:, 1, P:2 * P], causal[:]))
            for i in range(NB):
                nxt = FREE <= i + 1 < NB
                if nxt:
                    add_heads(i + 1)
                dve.wait_ge(q_in[i % 2], 48 * (i // 2 + 1))
                if i >= 2:
                    dve.wait_ge(tp_done, tp_at[i - 2, H] + 2)
                masked(i, 0)
                for h in range(H):
                    if h + 1 < H:
                        masked(i, h + 1) if h == 0 else None
                    if nxt:
                        search(i + 1, TOPK // 8 // H)
                    normed(i, h)
                    if 0 < h + 1 < H - 1:
                        masked(i, h + 2)
                if nxt:
                    s = sc[:, (i + 1) % 2, 0:(i + 2) * P]
                    link(dve.tensor_scalar(s, s, -2e38, -BIG, ALU.is_gt, ALU.mult))
                residual(i + 1, x[:, i % 2, :])


class Ring:

    def __init__(self, size, uses):
        self.size, self.uses, self.at, self.turn, seen = size, uses, {}, {}, {}
        for n, (key, reader) in enumerate(uses):
            seen[id(reader)] = seen.get(id(reader), 0) + 1
            self.at[key], self.turn[key] = n, seen[id(reader)]

    def slot(self, key):
        return self.at[key] % self.size

    def claim(self, pe, key):
        n = self.at[key]
        if n >= self.size:
            before, reader = self.uses[n - self.size]
            pe.wait_ge(reader, self.turn[before])
        return n % self.size

    def filled(self, key):
        return self.at[key] + 1


def dn_inputs(nc, env):
    d, keep = env["dram"], env["keep"]
    ident, xT = keep["ident"], keep["xT"]
    CH = [(CONV, 512), (CONV + 512, 512), (CONV + 1024, 16)]
    with ExitStack() as ctx:
        def sb(name, shape, dt=F32):
            return ctx.enter_context(nc.sbuf_tensor(name, shape, dt))

        def sem(name):
            return new_sem(nc, env, name)

        wz = sb("w_z", [P, KT, 1040])
        x = sb("x_dn", [P, 2, DM])
        junk = sb("junk_dn", [P, DM])
        gx = sb("gain_dn", [P, DM])
        go = sb("gain_o", [P, HD])
        th = sb("tanh_z", [P, 2, DM])
        gz = sb("gz", [P, 2, DM])
        ss = sb("ss_dn", [P, 2, 1])
        rs = sb("rs_dn", [P, 2, 1])
        mhalf = sb("mhalf_dn", [P, 1])
        ba = sb("ba", [P, NT, 16])
        al = sb("a_log", [P, H])
        dtb = sb("dt_bias", [P, H])
        t1 = sb("t1_g", [P, NT, H])
        t2 = sb("t2_g", [P, NT, H])
        tpb = ctx.enter_context(nc.psum_tensor("tp_dn", [P, 2, 4, P], F32))
        acc = ctx.enter_context(nc.psum_tensor("acc_dn", [P, 6, 512], F32))
        beta, g = keep["beta"], keep["g"]

        once = sem("dn_once")
        x_in = [sem("dx_in0"), sem("dx_in1")]
        ss_ok, rs_ok, xn_ok = sem("dss_ok"), sem("drs_ok"), sem("dxn_ok")
        tp_done, tp_evac = sem("dtp_done"), sem("dtp_evac")
        mm_done, th_ok, gz_ok, ba_ok, z_rd = sem("dmm_done"), sem("dth_ok"), sem("dgz_ok"), sem("dba_ok"), sem("dz_rd")
        st = [env["stores"][f"z_out{u}"] for u in range(2)]
        pch, ach, dch = sem("pool_chain_dn"), sem("act_chain_dn"), sem("dve_chain_dn")
        ga, gb = sem("g_act"), sem("g_dve")
        block = ctx.enter_context(nc.Block())

        @block.sync
        def _(sp):
            for n in range(NT):
                if n >= 2:
                    sp.wait_ge(tp_done, 2 * (n - 1))
                sp.dma_start(x[:, n % 2, :], d["y1_d"][n * P:(n + 1) * P, :]).then_inc(x_in[n % 2], 16)
                if n == 0:
                    sp.dma_start(gx[:], d["dn_norm"][0:1, :].partition_broadcast(P)).then_inc(once, 16)
                    sp.dma_start(go[:], d["dn_o_gain"][0:1, :].partition_broadcast(P)).then_inc(once, 16)
                    sp.dma_start(al[:], d["dn_A_log"][0:1, :].partition_broadcast(P)).then_inc(once, 16)
                    sp.dma_start(dtb[:], d["dn_dt_bias"][0:1, :].partition_broadcast(P)).then_inc(once, 16)
                    sp.dma_start(wz[:], d["dn_w_in"].rearrange("l (k p) n -> p (l k) n", p=P)[:, :, CONV:]).then_inc(once, 16)
                if n >= 1:
                    sp.wait_ge(gz_ok, n)
                    sp.dma_start(d["z_d"][(n - 1) * P:n * P, :], gz[:, (n - 1) % 2, :]).then_inc(st[(n - 1) % 2], 16)
            sp.wait_ge(gz_ok, NT)
            sp.dma_start(d["z_d"][(NT - 1) * P:, :], gz[:, (NT - 1) % 2, :]).then_inc(st[(NT - 1) % 2], 16)
            sp.wait_ge(st[0], 16 * 5)
            sp.wait_ge(st[1], 16 * 4)

        @block.gpsimd
        def _(pool):
            link = chain(pool, pch)
            link(pool.memset(mhalf[:], -0.5))

            def rms(n):
                pool.wait_ge(ss_ok, n + 1)
                link(pool.tensor_scalar(ss[:, n % 2, :], ss[:, n % 2, :], 1.0 / DM, EPS, ALU.mult, ALU.add))
                pool.tensor_tensor(rs[:, n % 2, :], ss[:, n % 2, :], mhalf[:], ALU.pow).then_inc(rs_ok, 1)

            rms(0)
            pool.wait_ge(once, 80)
            link(pool.tensor_scalar(go[:], go[:], 0.5, None, ALU.mult))
            for n in range(NT):
                if n + 1 < NT:
                    rms(n + 1)
                pool.wait_ge(z_rd, n + 1)
                if n >= 2:
                    pool.wait_ge(st[n % 2], 16 * (n // 2))
                pool.tensor_tensor(gz[:, n % 2, :].rearrange("p (h e) -> p h e", h=H), th[:, n % 2, :].rearrange("p (h e) -> p h e", h=H),
                                   go[:].unsqueeze(1).broadcast_to([P, H, HD]), ALU.mult).then_inc(gz_ok, 1)

        @block.tensor
        def _(pe):
            def turn(n):
                pe.wait_ge(xn_ok, n + 1)
                for u in range(2):
                    if n >= 1:
                        pe.wait_ge(tp_evac, 2 * n - 1 + u)
                    for j in range(4):
                        ins = pe.transpose(tpb[:, u, j, :], x[:, n % 2, (4 * u + j) * P:(4 * u + j + 1) * P], ident[:])
                    ins.then_inc(tp_done, 1)
            turn(0)
            pe.wait_ge(once, 80)
            for n in range(NT):
                if n + 1 < NT:
                    turn(n + 1)
                pe.wait_ge(tp_evac, 2 * n + 2)
                for c, (a, w) in enumerate(CH):
                    if n >= 2:
                        pe.wait_ge(z_rd if c < 2 else ba_ok, n - 1)
                    for k in range(KT):
                        ins = pe.matmul(acc[:, 3 * (n % 2) + c, 0:w], xT[:, k, n * P:(n + 1) * P], wz[:, k, a - CONV:a - CONV + w],
                                        start=(k == 0), stop=(k == KT - 1))
                    ins.then_inc(mm_done, 1)

        @block.scalar
        def _(act):
            def square(n):
                act.wait_ge(x_in[n % 2], 16 * (n // 2 + 1))
                if n >= 2:
                    act.wait_ge(rs_ok, n - 1)
                act.activation(junk[:], x[:, n % 2, :], ACT.Square, accum_out=ss[:, n % 2, :]).then_inc(ss_ok, 1)

            def evac(n):
                for u in range(2):
                    act.wait_ge(tp_done, 2 * n + u + 1)
                    act.copy(xT[:, 4 * u:4 * u + 4, n * P:(n + 1) * P], tpb[:, u, :, :]).then_inc(tp_evac, 1)
            square(0)
            evac(0)
            for n in range(NT):
                if n + 1 < NT:
                    square(n + 1)
                    evac(n + 1)
                if n >= 2:
                    act.wait_ge(gz_ok, n - 1)
                for c in range(2):
                    act.wait_ge(mm_done, 3 * n + c + 1)
                    act.activation(th[:, n % 2, c * 512:(c + 1) * 512], acc[:, 3 * (n % 2) + c, :], ACT.Tanh, scale=0.5).then_inc(th_ok, 1)
                act.wait_ge(mm_done, 3 * n + 3)
                act.copy(ba[:, n, :], acc[:, 3 * (n % 2) + 2, 0:16]).then_inc(ba_ok, 1)
            act.wait_ge(gb, 1)
            act.activation(beta[:], ba[:, :, 0:H], ACT.Exp, scale=-1.0).then_inc(ga, 1)
            act.activation(al[:], al[:], ACT.Exp)
            act.activation(t2[:], t2[:], ACT.Exp, scale=-1.0).then_inc(ach, 1)
            act.wait_ge(ach, 1)
            act.activation(t2[:], t2[:], ACT.Ln, bias=1.0).then_inc(ga, 1)

        @block.vector
        def _(dve):
            link = chain(dve, dch)

            def norm(n):
                dve.wait_ge(rs_ok, n + 1)
                dve.scalar_tensor_tensor(x[:, n % 2, :], x[:, n % 2, :], rs[:, n % 2, :], gx[:], ALU.mult, ALU.mult).then_inc(xn_ok, 1)
            dve.wait_ge(once, 80)
            norm(0)
            for n in range(NT):
                if n + 1 < NT:
                    norm(n + 1)
                dve.wait_ge(th_ok, 2 * n + 2)
                for c in range(2):
                    v = th[:, n % 2, c * 512:(c + 1) * 512]
                    ins = dve.scalar_tensor_tensor(v, v, 1.0, acc[:, 3 * (n % 2) + c, :], ALU.add, ALU.mult)
                ins.then_inc(z_rd, 1)
            dve.wait_ge(ba_ok, NT)
            link(dve.tensor_tensor(t1[:], ba[:, :, H:], dtb[:].unsqueeze(1).broadcast_to([P, NT, H]), ALU.add))
            dve.scalar_tensor_tensor(t2[:], t1[:], -1.0, t1[:], ALU.mult, ALU.max).then_inc(gb, 1)
            dve.wait_ge(ga, 1)
            link(dve.tensor_scalar(beta[:], beta[:], 1.0, None, ALU.add))
            link(dve.reciprocal(beta[:], beta[:]))
            dve.wait_ge(ga, 2)
            link(dve.scalar_tensor_tensor(t1[:], t1[:], 0.0, t2[:], ALU.max, ALU.add))
            link(dve.scalar_tensor_tensor(g[:], t1[:], -1.0, al[:].unsqueeze(1).broadcast_to([P, NT, H]), ALU.mult, ALU.mult))


def dn_conv(nc, env):
    d, keep = env["dram"], env["keep"]
    ident, xT = keep["ident"], keep["xT"]
    NCH = CONV // P
    CW = ROWS // 3
    NB3 = DB * (CW_TAPS - 1)
    WR = 3
    with ExitStack() as ctx:
        def sb(name, shape, dt=F32):
            return ctx.enter_context(nc.sbuf_tensor(name, shape, dt))

        def sem(name):
            return new_sem(nc, env, name)

        w = sb("w_ch", [P, WR, KT, P])
        cw_n = sb("conv_w_nat", [4 * NCH, P])
        cw = sb("conv_w", [P, 4 * NCH])
        cb_n = sb("conv_buf_nat", [NB3, CONV])
        xp = sb("x_pad", [P, 2, 3 + SEQ])
        xs = sb("x_pad_s", [P, 2, DB, 3 + DS])
        tail = sb("tail", [P, 2, 27])
        nb = sb("new_buf", [27, CONV])
        y = sb("y_ch", [P, 2, ROWS])
        th = sb("th_ch", [P, ROWS])
        sq = sb("sq_ch", [P, ROWS])
        rn = sb("rn_ch", [P, ROWS])
        ones = sb("ones_ch", [P, P])
        nw = sb("newton", [P, ROWS])
        ssx = sb("ss_eps", [P, ROWS])
        epsc = sb("eps_ch", [P, 1])
        acc = ctx.enter_context(nc.psum_tensor("acc_ch", [P, 3, 512], F32))
        sps = ctx.enter_context(nc.psum_tensor("ss_ch", [P, 3, 512], F32))
        tps = ctx.enter_context(nc.psum_tensor("tp_ch", [P, 2, 512], F32))

        once = sem("ch_once")
        w_in = [sem(f"w_ch_in{i}") for i in range(WR)]
        cw_t, cw_ok, zero_ok = sem("cw_t"), sem("cw_ok"), sem("zero_ok")
        mm, buf_t, x_ok, buf_ok, tail_ok, tail_t, nb_ok = (sem("ch_" + s) for s in ("mm", "buf_t", "x_ok", "buf_ok", "tail_ok", "tail_t", "nb_ok"))
        conv_ok, th_ok, silu_ok, sq_ok, ss_done, ssc_ok, rn_ok, out_ok = (
            sem("ch_" + s) for s in ("conv_ok", "th_ok", "silu_ok", "sq_ok", "ss_done", "ssc_ok", "rn_ok", "out_ok"))
        st = [env["stores"][f"qkv_out{u}"] for u in range(2)]
        nb_out = env["stores"]["nb_out"]
        dch, pch, act_ch = sem("dve_chain_ch"), sem("pool_chain_ch"), sem("act_chain_ch")
        block = ctx.enter_context(nc.Block())

        @block.sync
        def _(sp):
            wv = d["dn_w_in"].rearrange("l (k p) n -> p (l k) n", p=P)

            def load(c):
                if c >= WR:
                    sp.wait_ge(mm, c - WR + 1)
                sp.dma_start(w[:, c % WR, :, :], wv[:, :, c * P:(c + 1) * P]).then_inc(w_in[c % WR], 16)
            load(0)
            sp.dma_start(cw_n[:], d["dn_conv_w"].rearrange("l i (n p) -> (l i n) p", p=P)).then_inc(once, 16)
            sp.dma_start(cb_n[:], d["state_dn_conv"].rearrange("b l i n -> (b l i) n")).then_inc(once, 16)
            load(1)
            load(2)
            for c in range(NCH):
                sp.wait_ge(*((out_ok, c + 1) if c < 2 * H else (silu_ok, c + 1)))
                sp.dma_start(d["qkv_d"][c], y[:, c % 2, :]).then_inc(st[c % 2], 16)
                if c + WR < NCH:
                    load(c + WR)
            sp.wait_ge(nb_ok, NCH)
            sp.dma_start(d["newbuf_s"], nb[0:NB3, :]).then_inc(nb_out, 16)
            sp.dma_start(d["newbuf_p"], nb[NB3:27, :]).then_inc(nb_out, 16)
            sp.wait_ge(nb_out, 32)
            sp.wait_ge(st[0], 16 * NCH // 2)
            sp.wait_ge(st[1], 16 * NCH // 2)

        @block.tensor
        def _(pe):
            pe.wait_ge(once, 32)
            pe.transpose(tps[:, 0, 0:4 * NCH], cw_n[:], ident[0:4 * NCH, 0:4 * NCH]).then_inc(cw_t, 1)
            pe.wait_ge(cw_ok, 1)

            def project(c):
                pe.wait_ge(w_in[c % WR], 16 * (c // WR + 1))
                if c >= 1:
                    pe.wait_ge(x_ok, c)
                for j in range(3):
                    for k in range(KT):
                        ins = pe.matmul(acc[:, j, 0:CW], w[:, c % WR, k, :], xT[:, k, j * CW:(j + 1) * CW],
                                        start=(k == 0), stop=(k == KT - 1))
                ins.then_inc(mm, 1)
                if c >= 1:
                    pe.wait_ge(buf_ok, c)
                pe.transpose(tps[:, 0, 0:NB3], cb_n[:, c * P:(c + 1) * P], ident[0:NB3, 0:NB3]).then_inc(buf_t, 1)

            def after(c):
                pe.wait_ge(tail_ok, c + 1)
                if c >= 1:
                    pe.wait_ge(nb_ok, c)
                pe.transpose(tps[0:27, 1, 0:P], tail[:, c % 2, :], ident[:]).then_inc(tail_t, 1)
                if c < 2 * H:
                    pe.wait_ge(sq_ok, c + 1)
                    if c >= 1:
                        pe.wait_ge(ssc_ok, c)
                    for j in range(3):
                        ins = pe.matmul(sps[:, j, 0:CW], ones[:], sq[:, j * CW:(j + 1) * CW], start=True, stop=True)
                    ins.then_inc(ss_done, 1)
            for c in range(NCH):
                project(c)
                if c >= 1:
                    after(c - 1)
            after(NCH - 1)

        @block.scalar
        def _(act):
            def take(c):
                act.wait_ge(mm, c + 1)
                if c >= 2:
                    act.wait_ge(conv_ok, c - 1)
                    act.wait_ge(tail_ok, c - 1)
                act.wait_ge(zero_ok, 1)
                act.copy(xs[:, c % 2, :, 3:], acc[:, 0, 0:NS].rearrange("p (b t) -> p b t", b=DB))
                act.copy(xp[:, c % 2, 3:3 + CW - P], acc[:, 0, P:CW])
                for j in (1, 2):
                    a = 3 + j * CW - P
                    ins = act.copy(xp[:, c % 2, a:a + CW], acc[:, j, 0:CW])
                ins.then_inc(x_ok, 1)
                act.wait_ge(buf_t, c + 1)
                act.copy(xs[:, c % 2, :, 0:3], tps[:, 0, 0:NB3].rearrange("p (b i) -> p b i", b=DB)).then_inc(buf_ok, 1)

            def finish(c):
                act.wait_ge(conv_ok, c + 1)
                if c >= 1:
                    act.wait_ge(silu_ok, c)
                act.activation(th[:], y[:, c % 2, :], ACT.Tanh).then_inc(th_ok, 1)
                if c < 2 * H:
                    act.wait_ge(silu_ok, c + 1)
                    if c >= 1:
                        act.wait_ge(ss_done, c)
                    act.activation(sq[:], y[:, c % 2, :], ACT.Square).then_inc(sq_ok, 1)
                act.wait_ge(tail_t, c + 1)
                act.copy(nb[:, c * P:(c + 1) * P], tps[0:27, 1, 0:P]).then_inc(nb_ok, 1)
                if c < 2 * H:
                    act.wait_ge(ss_done, c + 1)
                    if c >= 1:
                        act.wait_ge(rn_ok, c)
                        act.wait_ge(out_ok, c)
                    for j in range(3):
                        act.activation(ssx[:, j * CW:(j + 1) * CW], sps[:, j, 0:CW], ACT.Identity, bias=epsc[:])
                        ins = act.activation(rn[:, j * CW:(j + 1) * CW], sps[:, j, 0:CW], ACT.Ln, bias=epsc[:])
                    ins.then_inc(act_ch, 1)
                    act.wait_ge(act_ch, c + 1)
                    act.activation(rn[:], rn[:], ACT.Exp, scale=-0.5).then_inc(ssc_ok, 1)
            take(0)
            for c in range(NCH):
                if c + 1 < NCH:
                    take(c + 1)
                finish(c)

        @block.gpsimd
        def _(pool):
            link = chain(pool, pch)
            pool.memset(epsc[:], EPS)
            pool.memset(ones[:], 1.0)
            pool.memset(y[:], 0.0)
            link(pool.memset(xp[:], 0.0))
            pool.memset(xs[:], 0.0).then_inc(zero_ok, 1)
            for c in range(NCH):
                pool.wait_ge(x_ok, c + 1)
                if c >= 2:
                    pool.wait_ge(tail_t, c - 1)
                pool.tensor_copy(tail[:, c % 2, 0:NB3].rearrange("p (b i) -> p b i", b=DB), xs[:, c % 2, :, DS:])
                pool.tensor_copy(tail[:, c % 2, NB3:], xp[:, c % 2, SEQ:]).then_inc(tail_ok, 1)
                if c < 2 * H:
                    pool.wait_ge(ssc_ok, c + 1)
                    link(pool.tensor_tensor(nw[:], rn[:], rn[:], ALU.mult))
                    link(pool.tensor_tensor(nw[:], nw[:], ssx[:], ALU.mult))
                    s = HD ** -0.5 if c < H else 1.0
                    link(pool.tensor_scalar(nw[:], nw[:], -0.5 * s, 1.5 * s, ALU.mult, ALU.add))
                    pool.tensor_tensor(rn[:], rn[:], nw[:], ALU.mult).then_inc(rn_ok, 1)

        @block.vector
        def _(dve):
            link = chain(dve, dch)
            dve.wait_ge(cw_t, 1)
            dve.tensor_scalar(cw[:], tps[:, 0, 0:4 * NCH], 0.5, None, ALU.mult).then_inc(cw_ok, 1)
            dve.wait_ge(cw_ok, 1)
            dve.wait_ge(zero_ok, 1)

            def conv(c):
                dve.wait_ge(x_ok, c + 1)
                dve.wait_ge(buf_ok, c + 1)
                if c >= 2:
                    dve.wait_ge(st[c % 2], 16 * (c // 2))
                ys = y[:, c % 2, 0:NS].rearrange("p (b t) -> p b t", b=DB)
                yp = y[:, c % 2, P:]
                for i in range(4):
                    tap = cw[:, i * NCH + c:i * NCH + c + 1]
                    for out, src in ((ys, xs[:, c % 2, :, i:i + DS]), (yp, xp[:, c % 2, i:i + SEQ])):
                        if i == 0:
                            ins = dve.tensor_scalar(out, src, tap, None, ALU.mult)
                        else:
                            ins = dve.scalar_tensor_tensor(out, src, tap, out, ALU.mult, ALU.add)
                    if i < 3:
                        link(ins)
                ins.then_inc(conv_ok, 1)

            def finish(c):
                yv = y[:, c % 2, :]
                dve.wait_ge(th_ok, c + 1)
                ins = dve.scalar_tensor_tensor(yv, th[:], 1.0, yv, ALU.add, ALU.mult)
                ins.then_inc(silu_ok, 1)
                if c < 2 * H:
                    dve.wait_ge(silu_ok, c + 1)
                    dve.wait_ge(sq_ok, c + 1)
                    dve.wait_ge(rn_ok, c + 1)
                    ins = dve.tensor_tensor(yv, yv, rn[:], ALU.mult)
                    ins.then_inc(out_ok, 1)
            conv(0)
            for c in range(NCH):
                if c + 1 < NCH:
                    conv(c + 1)
                finish(c)


def dn_scan(nc, env):
    d, keep = env["dram"], env["keep"]
    ident, beta, g = keep["ident"], keep["beta"], keep["g"]
    HG = H // 2
    with ExitStack() as ctx:
        def sb(name, shape, dt=F32):
            return ctx.enter_context(nc.sbuf_tensor(name, shape, dt))

        def sem(name):
            return new_sem(nc, env, "sc_" + name)

        wo = sb("w_out_dn", [P, H, DM])
        S = sb("S_p", [P, H, HD])
        Ss = sb("S_s", [P, DB, H, HD])
        qkv = sb("qkv_t", [P, 2, 3 * H, P])
        gz = sb("gz_t", [P, 2, DM])
        y = sb("y_t", [P, 2, DM])
        tri = sb("tri", [P, 2, P])
        blk = sb("blk", [P, 2, P])
        m1c = sb("m1c", [P, 2, P])
        m2c = sb("m2c", [P, 2, P])
        lev = sb("lev", [P, 7, P])
        bsel = sb("bsel", [P, DB])
        gsel = sb("gsel", [P, DB, H])
        eglS = sb("eglS", [P, DB, H])
        tg = sb("tri_g", [P, H, P])
        dec = sb("decay", [P, H, P])
        qk = sb("qk_decay", [P, 2, H, P])
        A = dec
        L = sb("L", [P, 2, H, P])
        T = sb("T", [P, H, P])
        TT = sb("TT", [P, 2, H, P])
        Y = sb("Y", [P, H, P])
        bv = sb("beta_v", [P, 2, H, P])
        kd = sb("k_decay", [P, 2, H, P])
        gcl = sb("gcl", [P, 2, 2, H])
        ngc = sb("ngc", [P, 2, H])
        ex = sb("exps", [P, 2, 3, H])
        nbe = sb("nbe", [P, 2, H])
        rhs = sb("rhs", [P, H, HD])
        qs = sb("qS_s", [P, H, HD])
        u = sb("u", [P, H, HD])
        o = sb("o_t", [P, H, HD])
        sqo = rhs
        sso = sb("ss_o", [P, H])
        rso = sb("rs_o", [P, H])
        mhalf = sb("mhalf_o", [P, H])
        ogT = sb("ogT_dn", [P, H, P])
        mgc = sb("minus_gc", [P, 2, H])
        xsb = sb("xS_s", [P, H, 2, NS])
        kdm = sb("k_masked", [P, 2, H, P])
        PA = ctx.enter_context(nc.psum_tensor("PA", [P, 4, 512], F32))
        PB = ctx.enter_context(nc.psum_tensor("PB", [P, 4, 512], F32))

        once, s_in = sem("once"), sem("s_in")
        in_ = [sem("in0"), sem("in1")]
        fa, fb = sem("PA_filled"), sem("PB_filled")
        a_dve, a_act = sem("PA_read_dve"), sem("PA_read_act")
        b_dve, b_act = sem("PB_read_dve"), sem("PB_read_act")
        gvec_ok, ex_ok, tg_ok, ed_ok, L_ok, T1_ok = (sem(s) for s in ("gvec_ok", "ex_ok", "tg_ok", "ed_ok", "L_ok", "T1_ok"))
        sq_ok, ssr_ok, rso_ok, og_ok, kdm_ok, gsel_ok, s_zero = (
            sem(s) for s in ("sq_ok", "ssr_ok", "rso_ok", "og_ok", "kdm_ok", "gsel_ok", "s_zero"))
        st = [env["stores"][f"y2_out{u}"] for u in range(2)]
        s_out = env["stores"]["s_out"]
        dch, pch = sem("dve_chain"), sem("pool_chain")

        def levels(n):
            return 3 if n == 0 else 7

        ua, ub, lbase = [], [], {}
        for n in range(NT):
            ua.append((("gc", n), a_dve))
            if n == 0:
                ua.append((("gs", n), a_act))
            for r in range(2):
                ua += [(("R", n, r), a_dve), (("vt", n, r), a_act), (("kt", n, r), a_act), (("kk", n, r), a_dve), (("qk", n, r), a_dve)]
            ua += [(("L1", n, r), a_dve) for r in range(2)]
            for l in range(1, levels(n)):
                ua += [(("Y", n, l, r), a_act) for r in range(2)]
                for r in range(2):
                    ua.append((("dTT", n, l, r), a_dve))
                    if l < levels(n) - 1:
                        ua.append((("dT", n, l, r), a_dve))
            if n == 0:
                ub += [(("XS", n, r), b_dve) for r in range(2)]
            for r in range(2):
                ub += [(("kS", n, r), b_dve), (("qS", n, r), b_act)]
            ub += [(("u", n, r), b_act) for r in range(2)]
            ub += [(("oi", n, r), b_dve) for r in range(2)]
            if n == 0:
                ub += [(("Sn", n, b, r), b_dve) for b in range(DB) for r in range(2)]
            else:
                ub += [(("Sn", n, r), b_dve) for r in range(2)]
            ub += [(("oT", n, r), b_act) for r in range(2)] + [(("y", n, r), b_dve) for r in range(2)]
            lbase[n] = sum(levels(m) for m in range(n))
        ra, rb = Ring(4, ua), Ring(4, ub)

        def a4(key):
            return PA[:, ra.slot(key), :].rearrange("p (h e) -> p h e", h=HG)

        def b4(key):
            return PB[:, rb.slot(key), :].rearrange("p (h e) -> p h e", h=HG)

        def hs(r):
            return slice(HG * r, HG * r + HG)

        def kind(n):
            return 0 if n == 0 else 1
        block = ctx.enter_context(nc.Block())

        @block.sync
        def _(sp):
            def load(n):
                p = n % 2
                sp.dma_start(qkv[:, p, :, :], d["qkv_d"][:, :, n * P:(n + 1) * P].rearrange("c e t -> e c t")).then_inc(in_[p], 16)
                sp.dma_start(gz[:, p, :], d["z_d"][n * P:(n + 1) * P, :]).then_inc(in_[p], 16)
                sp.dma_start(y[:, p, :], d["y1_d"][n * P:(n + 1) * P, :]).then_inc(in_[p], 16)
            load(0)
            for t, name in ((tri, "c_tri"), (blk, "c_blk"), (m1c, "c_m1"), (m2c, "c_m2"), (lev, "c_lev")):
                sp.dma_start(t[:].rearrange("p a b -> p (a b)"), d[name]).then_inc(once, 16)
            sp.dma_start(bsel[:], d["c_bsel"]).then_inc(once, 16)
            load(1)
            sp.dma_start(Ss[:].rearrange("p b h v -> p (b h) v"), d["state_dn_S"].rearrange("b l h e v -> e (b l h) v")).then_inc(s_in, 16)
            sp.dma_start(wo[:], d["dn_w_out"].rearrange("l (h p) n -> p (l h) n", p=P)).then_inc(s_in, 16)
            for n in range(NT):
                p = n % 2
                sp.wait_ge(b_dve, rb.turn["y", n, 1])
                sp.dma_start(d["y_all"][n * P:(n + 1) * P, :], y[:, p, :]).then_inc(st[p], 16)
                if n == 0:
                    sp.wait_ge(b_dve, rb.turn["Sn", 0, DB - 1, 1])
                    sp.dma_start(d["S_s"].rearrange("b h e v -> e (b h) v"), Ss[:].rearrange("p b h v -> p (b h) v")).then_inc(s_out, 16)
                if n + 2 < NT:
                    sp.wait_ge(st[p], 16 * (n // 2 + 1))
                    load(n + 2)
            sp.dma_start(d["S_p"].rearrange("h e v -> e h v"), S[:]).then_inc(s_out, 16)
            sp.wait_ge(s_out, 32)
            sp.wait_ge(st[0], 16 * 5)
            sp.wait_ge(st[1], 16 * 4)

        @block.tensor
        def _(pe):
            def prep(n):
                p, k = n % 2, kind(n)
                c = ra.claim(pe, ("gc", n))
                if n == 0:
                    pe.wait_ge(once, 96)
                pe.matmul(PA[:, c, 0:H], tri[:, k, :], g[:, n, :], start=True, stop=True)
                pe.matmul(PA[:, c, H:2 * H], blk[:, k, :], g[:, n, :], start=True, stop=True).then_inc(fa, 1)
                if n == 0:
                    pe.wait_ge(gsel_ok, 1)
                    c = ra.claim(pe, ("gs", n))
                    pe.matmul(PA[:, c, 0:NS], blk[:, 1, :], gsel[:].rearrange("p b h -> p (b h)"), start=True, stop=True).then_inc(fa, 1)
                pe.wait_ge(in_[p], 48 * (n // 2 + 1))
                for r in range(2):
                    c = ra.claim(pe, ("R", n, r))
                    pe.wait_ge(tg_ok, n + 1)
                    pe.matmul(PA[:, c, :], blk[:, 1, :], tg[:, hs(r), :].rearrange("p h e -> p (h e)"), start=True, stop=True).then_inc(fa, 1)
                    for what, off in (("vt", 2 * H), ("kt", H)):
                        ra.claim(pe, (what, n, r))
                        for h in range(HG):
                            ins = pe.transpose(a4((what, n, r))[:, h, :], qkv[:, p, off + HG * r + h, :], ident[:])
                        ins.then_inc(fa, 1)
                    for what, off in (("kk", H), ("qk", 0)):
                        ra.claim(pe, (what, n, r))
                        for h in range(HG):
                            hh = HG * r + h
                            ins = pe.matmul(a4((what, n, r))[:, h, :], qkv[:, p, H + hh, :], qkv[:, p, off + hh, :], start=True, stop=True)
                        ins.then_inc(fa, 1)
                for r in range(2):
                    ra.claim(pe, ("L1", n, r))
                    pe.wait_ge(L_ok, lbase[n] + 1)
                    for h in range(HG):
                        ins = pe.transpose(a4(("L1", n, r))[:, h, :], L[:, lbase[n] % 2, HG * r + h, :], ident[:])
                    ins.then_inc(fa, 1)
                for l in range(1, levels(n)):
                    last = l == levels(n) - 1
                    for r in range(2):
                        ra.claim(pe, ("Y", n, l, r))
                        pe.wait_ge(L_ok, lbase[n] + l + 1)
                        pe.wait_ge(a_dve, ra.turn["L1", n, r] if l == 1 else ra.turn["dTT", n, l - 1, r])
                        for h in range(HG):
                            hh = HG * r + h
                            ins = pe.matmul(a4(("Y", n, l, r))[:, h, :], L[:, (lbase[n] + l) % 2, hh, :], TT[:, p, hh, :], start=True, stop=True)
                        ins.then_inc(fa, 1)
                    for r in range(2):
                        pe.wait_ge(a_act, ra.turn["Y", n, l, r])
                        pe.wait_ge(*((T1_ok, n + 1) if l == 1 else (a_dve, ra.turn["dT", n, l - 1, r])))
                        ra.claim(pe, ("dTT", n, l, r))
                        for h in range(HG):
                            hh = HG * r + h
                            ins = pe.matmul(a4(("dTT", n, l, r))[:, h, :], T[:, hh, :], Y[:, hh, :], start=True, stop=True)
                        ins.then_inc(fa, 1)
                        if not last:
                            ra.claim(pe, ("dT", n, l, r))
                            for h in range(HG):
                                hh = HG * r + h
                                ins = pe.matmul(a4(("dT", n, l, r))[:, h, :], Y[:, hh, :], T[:, hh, :], start=True, stop=True)
                            ins.then_inc(fa, 1)

            def scan(n):
                p = n % 2
                if n == 0:
                    pe.wait_ge(s_in, 32)
                    for r in range(2):
                        c = rb.claim(pe, ("XS", n, r))
                        for h in range(HG):
                            for b in range(DB):
                                hh = HG * r + h
                                out = PB[:, c, h * P:(h + 1) * P].rearrange("p (w t) -> p w t", w=2)[:, :, b * DS:(b + 1) * DS]
                                src = qkv[:, p, hh:hh + H + 1:H, b * DS:(b + 1) * DS]
                                ins = pe.matmul(out, Ss[:, b, hh, :], src, start=True, stop=True)
                        ins.then_inc(fb, 1)
                for r in range(2):
                    for what, w in (("kS", 1), ("qS", 0)):
                        rb.claim(pe, (what, n, r))
                        if n == 0:
                            pe.wait_ge(b_dve, rb.turn["XS", n, r])
                        elif n == 1:
                            pe.wait_ge(s_zero, 1)
                        else:
                            pe.wait_ge(b_dve, rb.turn["Sn", n - 1, r])
                        for h in range(HG):
                            hh = HG * r + h
                            if n == 0:
                                ins = pe.transpose(b4((what, n, r))[0:NS, h, :], xsb[:, hh, w, :], ident[:])
                            else:
                                ins = pe.matmul(b4((what, n, r))[:, h, :], qkv[:, p, H * w + hh, :], S[:, hh, :], start=True, stop=True)
                        ins.then_inc(fb, 1)
                for r in range(2):
                    rb.claim(pe, ("u", n, r))
                    pe.wait_ge(b_dve, rb.turn["kS", n, r])
                    pe.wait_ge(a_dve, ra.turn["dTT", n, levels(n) - 1, r])
                    for h in range(HG):
                        hh = HG * r + h
                        ins = pe.matmul(b4(("u", n, r))[:, h, :], TT[:, p, hh, :], rhs[:, hh, :], start=True, stop=True)
                    ins.then_inc(fb, 1)
                for r in range(2):
                    rb.claim(pe, ("oi", n, r))
                    pe.wait_ge(b_act, rb.turn["u", n, r])
                    pe.wait_ge(a_dve, ra.turn["qk", n, r])
                    for h in range(HG):
                        hh = HG * r + h
                        ins = pe.matmul(b4(("oi", n, r))[:, h, :], qk[:, p, hh, :], u[:, hh, :], start=True, stop=True)
                    ins.then_inc(fb, 1)
                pe.wait_ge(a_act, ra.turn["kt", n, 1])
                if n == 0:
                    for b in range(DB):
                        pe.wait_ge(kdm_ok, b + 1)
                        for r in range(2):
                            rb.claim(pe, ("Sn", n, b, r))
                            for h in range(HG):
                                hh = HG * r + h
                                ins = pe.matmul(b4(("Sn", n, b, r))[:, h, :], kdm[:, b % 2, hh, :], u[:, hh, :], start=True, stop=True)
                            ins.then_inc(fb, 1)
                else:
                    for r in range(2):
                        rb.claim(pe, ("Sn", n, r))
                        for h in range(HG):
                            hh = HG * r + h
                            ins = pe.matmul(b4(("Sn", n, r))[:, h, :], kd[:, p, hh, :], u[:, hh, :], start=True, stop=True)
                        ins.then_inc(fb, 1)
                for r in range(2):
                    rb.claim(pe, ("oT", n, r))
                    pe.wait_ge(og_ok, n + 1)
                    for h in range(HG):
                        ins = pe.transpose(b4(("oT", n, r))[:, h, :], o[:, HG * r + h, :], ident[:])
                    ins.then_inc(fb, 1)
                for r in range(2):
                    c = rb.claim(pe, ("y", n, r))
                    pe.wait_ge(b_act, rb.turn["oT", n, 1])
                    for h in range(H):
                        ins = pe.matmul(PB[:, c, :], ogT[:, h, :], wo[:, h, r * 512:(r + 1) * 512], start=(h == 0), stop=(h == H - 1))
                    ins.then_inc(fb, 1)
            prep(0)
            for n in range(NT):
                if n + 1 < NT:
                    prep(n + 1)
                scan(n)

        @block.scalar
        def _(act):
            def prep(n):
                p = n % 2
                if n == 0:
                    act.wait_ge(fa, ra.filled(("gs", n)))
                    act.activation(eglS[:].rearrange("p b h -> p (b h)"), PA[:, ra.slot(("gs", n)), 0:NS], ACT.Exp).then_inc(a_act, 1)
                act.wait_ge(gvec_ok, n + 1)
                act.activation(ex[:, p, 0, :], gcl[:, p, 0, :], ACT.Exp)
                act.activation(ex[:, p, 1, :], gcl[:, p, 1, :], ACT.Exp)
                act.activation(ex[:, p, 2, :], ngc[:, p, :], ACT.Exp).then_inc(ex_ok, 1)
                act.wait_ge(ex_ok, n + 1)
                for r in range(2):
                    act.wait_ge(a_dve, ra.turn["R", n, r])
                    for h in range(HG * r, HG * r + HG):
                        act.activation(dec[:, h, :], dec[:, h, :], ACT.Exp, bias=gcl[:, p, 0, h:h + 1], scale=-1.0)
                        ins = act.activation(qk[:, p, h, :], qk[:, p, h, :], ACT.Exp, bias=mgc[:, p, h:h + 1])
                    ins.then_inc(ed_ok, 1)
                    act.wait_ge(fa, ra.filled(("vt", n, r)))
                    for h in range(HG):
                        ins = act.mul(bv[:, p, HG * r + h, :], a4(("vt", n, r))[:, h, :], beta[:, n, HG * r + h:HG * r + h + 1])
                    ins.then_inc(a_act, 1)
                    act.wait_ge(fa, ra.filled(("kt", n, r)))
                    for h in range(HG):
                        ins = act.mul(kd[:, p, HG * r + h, :], a4(("kt", n, r))[:, h, :], ex[:, p, 2, HG * r + h:HG * r + h + 1])
                    ins.then_inc(a_act, 1)
                for l in range(1, levels(n)):
                    for r in range(2):
                        act.wait_ge(fa, ra.filled(("Y", n, l, r)))
                        act.copy(Y[:, hs(r), :], a4(("Y", n, l, r))).then_inc(a_act, 1)

            def scan(n):
                p = n % 2
                m = NS if n == 0 else P
                for r in range(2):
                    act.wait_ge(fb, rb.filled(("qS", n, r)))
                    if n >= 1:
                        act.wait_ge(b_dve, rb.turn["oi", n - 1, r])
                    for h in range(HG):
                        hh = HG * r + h
                        ins = act.mul(qs[0:m, hh, :], b4(("qS", n, r))[0:m, h, :], ex[0:m, p, 0, hh:hh + 1])
                    ins.then_inc(b_act, 1)
                for r in range(2):
                    act.wait_ge(fb, rb.filled(("u", n, r)))
                    act.copy(u[:, hs(r), :], b4(("u", n, r))).then_inc(b_act, 1)
                act.wait_ge(b_dve, rb.turn["oi", n, 1])
                if n >= 1:
                    act.wait_ge(ssr_ok, n)
                act.activation(sqo[:], o[:], ACT.Square).then_inc(sq_ok, 1)
                for r in range(2):
                    act.wait_ge(fb, rb.filled(("oT", n, r)))
                    act.copy(ogT[:, hs(r), :], b4(("oT", n, r))).then_inc(b_act, 1)
            prep(0)
            for n in range(NT):
                if n + 1 < NT:
                    prep(n + 1)
                scan(n)

        @block.gpsimd
        def _(pool):
            link = chain(pool, pch)
            pool.memset(S[:], 0.0).then_inc(s_zero, 1)
            link(pool.memset(mhalf[:], -0.5))
            pool.wait_ge(once, 96)
            pool.tensor_tensor(gsel[:], g[:, 0, :].unsqueeze(1).broadcast_to([P, DB, H]), bsel[:].unsqueeze(2).broadcast_to([P, DB, H]), ALU.mult).then_inc(gsel_ok, 1)

            def prep(n):
                if n >= 1:
                    pool.wait_ge(fa, ra.filled(("R", n - 1, 1)))
                pool.tensor_tensor(tg[:], tri[:, kind(n), :].unsqueeze(1).broadcast_to([P, H, P]),
                                   g[:, n, :].unsqueeze(2).broadcast_to([P, H, P]), ALU.mult).then_inc(tg_ok, 1)
                for l in range(levels(n)):
                    if l == 0:
                        pool.wait_ge(a_dve, ra.turn["qk", n, 1])
                    if l >= 2:
                        pool.wait_ge(fa, ra.filled(("Y", n, l - 2, 1) if l > 2 else ("L1", n, 1)))
                        if l == 2:
                            pool.wait_ge(T1_ok, n + 1)
                    elif n >= 1:
                        pool.wait_ge(fa, ra.filled(("dTT", n - 1, levels(n - 1) - 1, 1)))
                    pool.tensor_tensor(L[:, (lbase[n] + l) % 2, :, :], A[:], lev[:, l, :].unsqueeze(1).broadcast_to([P, H, P]), ALU.mult).then_inc(L_ok, 1)

            def scan(n):
                if n == 0:
                    pool.wait_ge(a_act, ra.turn["kt", n, 1])
                    for b in range(DB):
                        if b >= 2:
                            pool.wait_ge(fb, rb.filled(("Sn", 0, b - 2, 1)))
                        pool.tensor_scalar(kdm[:, b % 2, :, :], kd[:, 0, :, :], bsel[:, b:b + 1], None, ALU.mult).then_inc(kdm_ok, 1)
                pool.wait_ge(ssr_ok, n + 1)
                link(pool.tensor_scalar(sso[:], sso[:], 1.0 / HD, EPS, ALU.mult, ALU.add))
                pool.tensor_tensor(rso[:], sso[:], mhalf[:], ALU.pow).then_inc(rso_ok, 1)
            prep(0)
            for n in range(NT):
                if n + 1 < NT:
                    prep(n + 1)
                scan(n)

        @block.vector
        def _(dve):
            link = chain(dve, dch)
            idb = ident[:].unsqueeze(1).broadcast_to([P, HG, P])

            def prep(n):
                p, k = n % 2, kind(n)
                dve.wait_ge(fa, ra.filled(("gc", n)))
                link(dve.tensor_copy(gcl[:, p, :, :].rearrange("p a b -> p (a b)"), PA[:, ra.slot(("gc", n)), 0:2 * H]))
                dve.tensor_scalar(mgc[:, p, :], gcl[:, p, 0, :], -1.0, None, ALU.mult).then_inc(a_dve, 1)
                dve.tensor_tensor(ngc[:, p, :], gcl[:, p, 1, :], gcl[:, p, 0, :], ALU.subtract).then_inc(gvec_ok, 1)
                dve.wait_ge(ex_ok, n + 1)
                dve.scalar_tensor_tensor(nbe[:, p, :], ex[:, p, 0, :], -1.0, beta[:, n, :], ALU.mult, ALU.mult)
                if n >= 1:
                    dve.wait_ge(L_ok, lbase[n])
                for r in range(2):
                    dve.wait_ge(fa, ra.filled(("R", n, r)))
                    dve.tensor_tensor(dec[:, hs(r), :], a4(("R", n, r)), m1c[:, k, :].unsqueeze(1).broadcast_to([P, HG, P]), ALU.add)
                    dve.tensor_tensor(qk[:, p, hs(r), :], a4(("R", n, r)), m2c[:, k, :].unsqueeze(1).broadcast_to([P, HG, P]), ALU.add).then_inc(a_dve, 1)
                    dve.wait_ge(fa, ra.filled(("kk", n, r)))
                    dve.wait_ge(ed_ok, 2 * n + r + 1)
                    for h in range(HG):
                        hh = HG * r + h
                        ins = dve.scalar_tensor_tensor(A[:, hh, :], a4(("kk", n, r))[:, h, :], beta[:, n, hh:hh + 1], dec[:, hh, :], ALU.mult, ALU.mult)
                    ins.then_inc(a_dve, 1)
                    dve.wait_ge(fa, ra.filled(("qk", n, r)))
                    dve.tensor_tensor(qk[:, p, hs(r), :], a4(("qk", n, r)), qk[:, p, hs(r), :], ALU.mult).then_inc(a_dve, 1)
                dve.wait_ge(L_ok, lbase[n] + 1)
                for r in range(2):
                    ins = dve.tensor_tensor(T[:, hs(r), :], idb, L[:, lbase[n] % 2, hs(r), :], ALU.subtract)
                ins.then_inc(T1_ok, 1)
                for r in range(2):
                    dve.wait_ge(fa, ra.filled(("L1", n, r)))
                    dve.tensor_tensor(TT[:, p, hs(r), :], idb, a4(("L1", n, r)), ALU.subtract).then_inc(a_dve, 1)
                for l in range(1, levels(n)):
                    for r in range(2):
                        dve.wait_ge(fa, ra.filled(("dTT", n, l, r)))
                        dve.tensor_tensor(TT[:, p, hs(r), :], TT[:, p, hs(r), :], a4(("dTT", n, l, r)), ALU.subtract).then_inc(a_dve, 1)
                        if l < levels(n) - 1:
                            dve.wait_ge(fa, ra.filled(("dT", n, l, r)))
                            dve.tensor_tensor(T[:, hs(r), :], T[:, hs(r), :], a4(("dT", n, l, r)), ALU.subtract).then_inc(a_dve, 1)

            def scan(n):
                p = n % 2
                m = NS if n == 0 else P
                if n == 0:
                    dve.memset(rhs[NS:, :, :], 0.0)
                    link(dve.memset(qs[NS:, :, :], 0.0))
                    for r in range(2):
                        dve.wait_ge(fb, rb.filled(("XS", n, r)))
                        dve.tensor_copy(xsb[:, hs(r), :, :], PB[:, rb.slot(("XS", n, r)), :].rearrange("p (h w t) -> p h w t", h=HG, w=2)).then_inc(b_dve, 1)
                for r in range(2):
                    dve.wait_ge(fb, rb.filled(("kS", n, r)))
                    dve.wait_ge(a_act, ra.turn["vt", n, r])
                    for h in range(HG):
                        hh = HG * r + h
                        ins = dve.scalar_tensor_tensor(rhs[0:m, hh, :], b4(("kS", n, r))[0:m, h, :], nbe[0:m, p, hh:hh + 1], bv[0:m, p, hh, :], ALU.mult, ALU.add)
                    ins.then_inc(b_dve, 1)
                for r in range(2):
                    dve.wait_ge(fb, rb.filled(("oi", n, r)))
                    dve.wait_ge(b_act, rb.turn["qS", n, r])
                    dve.tensor_tensor(o[:, hs(r), :], b4(("oi", n, r)), qs[:, hs(r), :], ALU.add).then_inc(b_dve, 1)
                if n == 0:
                    for b in range(DB):
                        for r in range(2):
                            dve.wait_ge(fb, rb.filled(("Sn", n, b, r)))
                            for h in range(HG):
                                hh = HG * r + h
                                ins = dve.scalar_tensor_tensor(Ss[:, b, hh, :], Ss[:, b, hh, :], eglS[:, b, hh:hh + 1], b4(("Sn", n, b, r))[:, h, :], ALU.mult, ALU.add)
                            ins.then_inc(b_dve, 1)
                else:
                    for r in range(2):
                        dve.wait_ge(fb, rb.filled(("Sn", n, r)))
                        for h in range(HG):
                            hh = HG * r + h
                            ins = dve.scalar_tensor_tensor(S[:, hh, :], S[:, hh, :], ex[:, p, 1, hh:hh + 1], b4(("Sn", n, r))[:, h, :], ALU.mult, ALU.add)
                        ins.then_inc(b_dve, 1)
                dve.wait_ge(sq_ok, n + 1)
                if n >= 1:
                    dve.wait_ge(rso_ok, n)
                dve.tensor_reduce(sso[:], sqo[:], AX.X, ALU.add).then_inc(ssr_ok, 1)
                dve.wait_ge(rso_ok, n + 1)
                for h in range(H):
                    ins = dve.scalar_tensor_tensor(o[:, h, :], o[:, h, :], rso[:, h:h + 1], gz[:, p, h * HD:(h + 1) * HD], ALU.mult, ALU.mult)
                ins.then_inc(og_ok, 1)
                for r in range(2):
                    dve.wait_ge(fb, rb.filled(("y", n, r)))
                    v = y[:, p, r * 512:(r + 1) * 512]
                    ins = dve.tensor_tensor(v, v, PB[:, rb.slot(("y", n, r)), :], ALU.add)
                    ins.then_inc(b_dve, 1)
            prep(0)
            for n in range(NT):
                if n + 1 < NT:
                    prep(n + 1)
                scan(n)


def constants():
    p = np.arange(P)
    b2, h, t = p // 64, (p // 8) % 8, p % 8
    c = {"c_ident": np.eye(P)}
    col = np.arange(16)
    c["c_delta16"] = (b2[:, None] == col[None] // 8) & (t[:, None] == col[None] % 8)
    c["c_new_causal"] = np.where((p[:, None] >= 64) & (np.arange(8)[None] <= t[:, None]), 0.0, -BIG)
    c["c_e4"] = np.arange(4)[:, None] == p[None] // 32
    c["c_causal"] = np.where(p[None] <= p[:, None], 0.0, -BIG)
    c["c_j32"] = (p % 32)[:, None]
    c["c_half_off"] = ((p >= 64) * (PAST // 2))[:, None]
    e = np.zeros((NS, 4, P))
    for tt in range(4):
        for r in range(P):
            e[16 * tt + r // 8, tt, r] = 1
    c["c_expand_q"] = e.reshape(NS, 4 * P)
    q, hh = p // 8, p % 8
    n = np.arange(32)
    ok = (hh[:, None] // GRP == n[None] // 16) & (q[:, None] // 8 == (n[None] % 16) // 8)
    c["c_new_allowed"] = np.where(ok, 0.0, -BIG)
    i, j = p[:, None], p[None]
    same = [i // DS == j // DS, i >= 0 * j]
    two = lambda f: np.stack([f(m) for m in same], 1).reshape(P, 2 * P)
    c["c_tri"] = two(lambda m: (i <= j) & m)
    c["c_blk"] = two(lambda m: m & (j >= 0))
    c["c_m1"] = two(lambda m: np.where((j < i) & m, 0.0, BIG))
    c["c_m2"] = two(lambda m: np.where((i <= j) & m, 0.0, -BIG))
    c["c_lev"] = np.stack([(i // (2 << l) == j // (2 << l)) & (i % (2 << l) >= 1 << l) & (j % (2 << l) < 1 << l) for l in range(7)], 1).reshape(P, 7 * P)
    c["c_bsel"] = i // DS == np.arange(DB)[None]
    return {k: np.ascontiguousarray(v, dtype=np.float32) for k, v in c.items()}


def build(nc, d):
    with ExitStack() as ctx:
        def sb(name, shape, dt=F32, c=ctx):
            return c.enter_context(nc.sbuf_tensor(name, shape, dt))
        keep = {"ident": sb("ident", [P, P]), "beta": sb("beta", [P, NT, H]), "g": sb("g", [P, NT, H])}
        stores = {k: ctx.enter_context(nc.semaphore(k)) for k in (
            "st0_0", "st1_0", "st0_1", "st1_1", "iwl_out", "pa_once", "y1_out0", "y1_out1", "z_out0", "z_out1",
            "qkv_out0", "qkv_out1", "nb_out", "y2_out0", "y2_out1", "s_out")}
        env = {"dram": d, "keep": keep, "stores": stores, "sems": []}
        with ExitStack() as att:
            for name, shape, dt in (("kT", [P, G, ROWS], F32), ("v_nat", [P, NT, G * HD], F32), ("ikT", [P, ROWS], F32),
                                    ("iw_nat", [P, NT, IH], F32), ("top_v", [P, TOPK], F32), ("top_i", [P, TOPK], U32)):
                keep[name] = sb(name, shape, dt, att)
            with ExitStack() as proj:
                keep["scores"] = sb("scores", [P, PAST // 2 + DS], F32, proj)
                keep["w"] = sb("w_att", [P, KT, ATT_IN], F32, proj)
                for k, n in (("gx", DM), ("gq", HD), ("gqs", HD), ("gk", HD), ("gik", ID)):
                    keep[k] = sb(k, [P, n], F32, proj)
                att_project(nc, env, 0, 1, True, lambda dve, n: None)
                sample_scores(nc, env)
                att_project(nc, env, 1, NT - 1, False, extraction(env, new_sem(nc, env, "extract_chain")))
            for name, shape, dt in (("rowidx", [P, 2, NS], U32), ("mask_s", [P, 4, TOPK], F32),
                                    ("mask_n", [P, 4, 32], F32), ("og_s", [P, H, P], F32)):
                keep[name] = sb(name, shape, dt, att)
            sample_select(nc, env)
            sample_attend(nc, env)
            prompt_attend(nc, env)
        clear_sems(nc, env)
        with ExitStack() as dn:
            keep["xT"] = sb("xT", [P, KT, ROWS], F32, dn)
            dn_inputs(nc, env)
            dn_conv(nc, env)
        dn_scan(nc, env)


def kernel(**inputs):
    import concourse.bacc as _bacc
    from concourse.bass_utils import run_bass_kernel_spmd as _run

    nc = _bacc.Bacc("TRN2", target_bir_lowering=False, num_devices=1)
    arrays, d = {}, {}
    a = {k: np.ascontiguousarray(v) for k, v in inputs.items()}
    x_all = np.zeros((ROWS, DM), np.float32)
    x_all[0:NS] = a["x_sample"].reshape(NS, DM)
    x_all[P:] = a["x_prompt"].reshape(SEQ, DM)
    ins = {k: v for k, v in a.items() if k not in ("x_sample", "x_prompt")}
    ins["x_all"] = x_all
    ins.update(constants())
    for name, v in ins.items():
        arrays[f"in_{name}"] = v
        d[name] = nc.dram_tensor(f"in_{name}", v.shape, mybir.dt.from_np(v.dtype), kind="ExternalInput").ap()
    scratch = {"qT_d": (ROWS, DM), "iqT_d": (ROWS, IH * ID), "gate_d": (ROWS, DM), "iwl_d": (DB, IH, DS),
               "y1_d": (ROWS, DM), "z_d": (ROWS, DM), "qkv_d": (3 * H, P, ROWS)}
    outs = {"k_all": (ROWS, G * HD), "v_all": (ROWS, G * HD), "ik_all": (ROWS, ID), "y_all": (ROWS, DM),
            "S_p": (H, HD, HD), "S_s": (DB, H, HD, HD), "newbuf_p": (CW_TAPS - 1, CONV), "newbuf_s": (DB * (CW_TAPS - 1), CONV)}
    DBG = False
    for name, shape in scratch.items():
        d[name] = nc.dram_tensor(f"out_{name}" if DBG else name, shape, F32, kind="ExternalOutput" if DBG else "Internal").ap()
    for name, shape in outs.items():
        d[name] = nc.dram_tensor(f"out_{name}", shape, F32, kind="ExternalOutput").ap()
    build(nc, d)
    r = {k[4:]: v for k, v in _run(nc, [arrays], core_ids=[0]).results[0].items()}
    k, v, ik, y = r["k_all"], r["v_all"], r["ik_all"], r["y_all"]
    return (y[P:].reshape(1, SEQ, DM), y[:NS].reshape(DB, DS, DM),
            k[P:].reshape(1, SEQ, 1, G, HD), v[P:].reshape(1, SEQ, 1, G, HD), ik[P:].reshape(1, SEQ, 1, ID),
            k[:NS].reshape(DB, DS, 1, G, HD), v[:NS].reshape(DB, DS, 1, G, HD), ik[:NS].reshape(DB, DS, 1, ID),
            r["S_p"].reshape(1, 1, H, HD, HD), r["newbuf_p"].reshape(1, 1, CW_TAPS - 1, CONV),
            r["S_s"].reshape(DB, 1, H, HD, HD), r["newbuf_s"].reshape(DB, 1, CW_TAPS - 1, CONV))
```

```python
from contextlib import ExitStack

import numpy as np
import concourse.bass as bass
from concourse import mybir

F32 = mybir.dt.float32
I32 = mybir.dt.int32
U32 = mybir.dt.uint32
ALU = mybir.AluOpType
ACT = mybir.ActivationFunctionType
AX = mybir.AxisListType

P = 128
DM = 1024
KT = DM // P
SEQ = 1024
NT = SEQ // P + 1
ROWS = NT * P
DB, DS = 8, 8
NS = DB * DS
PAST = 8192
PAGE = 128
NPG = PAST // PAGE
POOLN = 640
H, G, HD = 8, 2, 128
GRP = H // G
IH, ID = 8, 64
TOPK = 256
EPS = 1e-6
NB = SEQ // P
FREE = TOPK // P
KM = [P * i * (i + 1) // 2 for i in range(NB + 1)]
CONV = 3072
CW_TAPS = 4
BIG = 1e30

Q0, K0, V0 = 0, 1024, 1280
IQ0, IK0, IW0, G0 = 1536, 2048, 2112, 2120
ATT_IN = 3144
CHUNKS = [(0, 512), (512, 512), (1024, 512), (1536, 512), (2048, 72), (2120, 512), (2632, 512)]


def new_sem(nc, env, name):
    s = nc.alloc_semaphore(name=name)
    env["sems"].append(s)
    return s


def clear_sems(nc, env):
    nc.clear_and_free_semaphores(env["sems"])
    env["sems"] = []
    nc.all_engine_barrier()


def chain(eng, sem):
    n = [0]

    def link(ins):
        n[0] += 1
        ins.then_inc(sem, 1)
        eng.wait_ge(sem, n[0])
    return link


def att_project(nc, env, t0, m, first, between):
    d, keep = env["dram"], env["keep"]
    with ExitStack() as ctx:
        def sb(name, shape, dt=F32):
            return ctx.enter_context(nc.sbuf_tensor(f"{name}_{t0}", shape, dt))

        def sem(name):
            return new_sem(nc, env, f"{name}_{t0}")

        x = sb("x", [P, 2, DM])
        xnT = sb("xnT", [P, 2, KT, P])
        raw = sb("raw", [P, 2, ATT_IN])
        sq = sb("sq", [P, 1280 + 64])
        ikk = sb("ikk", [P, 2, 2, ID])
        sgate = sb("sgate", [P, 2, DM])
        qTb = sb("qTb", [P, H * HD])
        iqTb = sb("iqTb", [P, IH * ID])
        ssx = sb("ssx", [P, 2, 1])
        rsx = sb("rsx", [P, 2, 1])
        msx = sb("msx", [P, 2, 1])
        ssh = sb("ssh", [P, 2, 11])
        msh = sb("msh", [P, 2, 11])
        rsh = sb("rsh", [P, 2, 11])
        mhalf = sb("mhalf", [P, 16])
        tpb = ctx.enter_context(nc.psum_tensor(f"tpb_{t0}", [P, 2, 4, P], F32))
        acc = ctx.enter_context(nc.psum_tensor(f"acc_{t0}", [P, 6, 512], F32))
        w, gx, gq, gqs, gk, gik = (keep[k] for k in ("w", "gx", "gq", "gqs", "gk", "gik"))
        ident, kT, v_nat, ikT, iw_nat = keep["ident"], keep["kT"], keep["v_nat"], keep["ikT"], keep["iw_nat"]

        x_in = [sem("x_in0"), sem("x_in1")]
        w_in = [sem(f"w_in{c}") for c in range(7)]
        const_in = sem("const_in")
        gains_ok = sem("gains_ok")
        ssx_ok = sem("ssx_ok")
        rsx_ok = sem("rsx_ok")
        pool_chain = sem("pool_chain")
        xn_ok = sem("xn_ok")
        tp_done = sem("tp_done")
        tp_evac = sem("tp_evac")
        mm_done = sem("mm_done")
        raw_ok = sem("raw_ok")
        sq_ok = sem("sq_ok")
        ssh_ok = sem("ssh_ok")
        rsh_ok = sem("rsh_ok")
        tanh_ok = sem("tanh_ok")
        gate_ok = sem("gate_ok")
        nat_ok = sem("nat_ok")
        st = [env["stores"][f"st{u}_{t0}"] for u in range(2)]
        NST = 6

        def run(step):
            for n in range(m):
                step(n, n % 2, n // 2)

        t_base, q_base, uses = {}, {}, 0
        for what, n in [("T", 0)] + [e for i in range(m) for e in (("T", i + 1), ("Q", i - 1))] + [("Q", m - 1)]:
            if 0 <= n < m:
                (t_base if what == "T" else q_base)[n] = uses
                uses += 2 if what == "T" else 4

        block = ctx.enter_context(nc.Block())

        @block.gpsimd
        def _(pool):
            if first:
                pool.dma_start(ident[:], d["c_ident"]).then_inc(const_in, 16)
                pool.dma_start(gx[:], d["att_norm"][0:1, :].partition_broadcast(P)).then_inc(const_in, 16)
                pool.dma_start(gq[:], d["att_q_gain"][0:1, :].partition_broadcast(P)).then_inc(const_in, 16)
                pool.dma_start(gk[:], d["att_k_gain"][0:1, :].partition_broadcast(P)).then_inc(const_in, 16)
                pool.dma_start(gik[:], d["att_ik_gain"][0:1, :].partition_broadcast(P)).then_inc(const_in, 16)
            link = chain(pool, pool_chain)
            link(pool.memset(mhalf[:], -0.5))

            def rms_x(n, par):
                pool.wait_ge(ssx_ok, n + 1)
                link(pool.tensor_scalar(msx[:, par, :], ssx[:, par, :], 1.0 / DM, EPS, ALU.mult, ALU.add))
                pool.tensor_tensor(rsx[:, par, :], msx[:, par, :], mhalf[:, 0:1], ALU.pow).then_inc(rsx_ok, 1)
            rms_x(0, 0)
            if m > 1:
                rms_x(1, 1)

            def step(n, par, k):
                if n + 2 < m:
                    rms_x(n + 2, par)
                pool.wait_ge(ssh_ok, n + 1)
                pool.tensor_scalar(msh[:, par, 0:10], ssh[:, par, 0:10], 1.0 / HD, EPS, ALU.mult, ALU.add)
                link(pool.tensor_scalar(msh[:, par, 10:11], ssh[:, par, 10:11], 1.0 / ID, EPS, ALU.mult, ALU.add))
                pool.tensor_tensor(rsh[:, par, :], msh[:, par, :], mhalf[:, 0:11], ALU.pow).then_inc(rsh_ok, 1)
                pool.wait_ge(tanh_ok, n + 1)
                link(pool.tensor_scalar(sgate[:, par, :], sgate[:, par, :], 0.5, 0.5, ALU.mult, ALU.add))
                pool.tensor_tensor(sgate[:, par, :], sgate[:, par, :], raw[:, par, G0:ATT_IN], ALU.mult).then_inc(gate_ok, 1)
            run(step)

        @block.sync
        def _(sp):
            def rows(t, n):
                return t[(t0 + n) * P:(t0 + n + 1) * P, :]

            def load(n, par):
                sp.dma_start(x[:, par, :], rows(d["x_all"], n)).then_inc(x_in[par], 16)
            load(0, 0)
            if m > 1:
                load(1, 1)
            wv = d["att_w_in"].rearrange("l (k p) n -> p (l k) n", p=P)
            if first:
                sp.wait_ge(const_in, 80)
            for c, (a, cw) in enumerate(CHUNKS if first else ()):
                sp.dma_start(w[:, :, a:a + cw], wv[:, :, a:a + cw]).then_inc(w_in[c], 16)

            def store(n, par):
                sp.wait_ge(tp_evac, q_base[n] + 4)
                sp.wait_ge(gate_ok, n + 1)
                sp.dma_start(rows(d["qT_d"], n), qTb[:]).then_inc(st[par], 16)
                sp.dma_start(rows(d["iqT_d"], n), iqTb[:]).then_inc(st[par], 16)
                sp.dma_start(rows(d["gate_d"], n), sgate[:, par, :]).then_inc(st[par], 16)
                sp.dma_start(rows(d["k_all"], n), raw[:, par, K0:K0 + 256]).then_inc(st[par], 16)
                sp.dma_start(rows(d["v_all"], n), v_nat[:, t0 + n, :]).then_inc(st[par], 16)
                sp.dma_start(rows(d["ik_all"], n), ikk[:, par, 0, :]).then_inc(st[par], 16)

            def step(n, par, k):
                if n + 2 < m:
                    sp.wait_ge(tp_done, t_base[n] + 2)
                    load(n + 2, par)
                if n > 0:
                    store(n - 1, 1 - par)
            run(step)
            store(m - 1, (m - 1) % 2)
            sp.wait_ge(st[0], 16 * NST * ((m + 1) // 2))
            sp.wait_ge(st[1], 16 * NST * (m // 2))

        @block.tensor
        def _(pe):
            def transposes_x(n, par):
                b = t_base[n]
                pe.wait_ge(xn_ok, n + 1)
                for u in range(2):
                    if n > 0:
                        pe.wait_ge(tp_evac, b + u - 1)
                    for j in range(4):
                        k = 4 * u + j
                        ins = pe.transpose(tpb[:, u, j, :], x[:, par, k * P:(k + 1) * P], ident[:])
                    ins.then_inc(tp_done, 1)

            def project(n, par, k):
                pe.wait_ge(tp_evac, t_base[n] + 2)
                for c, (a, cw) in enumerate(CHUNKS):
                    if n == 0 and first:
                        pe.wait_ge(w_in[c], 16)
                    if n > 0 or c == 6:
                        pe.wait_ge(raw_ok, 7 * n if c == 0 else 7 * n + 1 if c == 6 else 7 * n + c - 6)
                    for kk in range(KT):
                        ins = pe.matmul(acc[:, c % 6, 0:cw], xnT[:, par, kk, :], w[:, kk, a:a + cw],
                                        start=(kk == 0), stop=(kk == KT - 1))
                    ins.then_inc(mm_done, 1)

            def transposes_q(n, par):
                b = q_base[n]
                pe.wait_ge(nat_ok, n + 1)
                for u in range(4):
                    pe.wait_ge(tp_evac, b + u - 1)
                    if u < 2:
                        src = [raw[:, par, (4 * u + j) * P:(4 * u + j + 1) * P] for j in range(4)]
                    elif u == 2:
                        src = [raw[:, par, IQ0 + j * P:IQ0 + (j + 1) * P] for j in range(4)]
                    else:
                        src = [raw[:, par, K0 + j * P:K0 + (j + 1) * P] for j in range(2)]
                        src.append(ikk[:, par, :, :].rearrange("p a d -> p (a d)"))
                    for j, s in enumerate(src):
                        ins = pe.transpose(tpb[:, u % 2, j, :], s, ident[:])
                    ins.then_inc(tp_done, 1)

            if first:
                pe.wait_ge(const_in, 80)
            transposes_x(0, 0)

            def step(n, par, k):
                if n + 1 < m:
                    transposes_x(n + 1, 1 - par)
                project(n, par, k)
                if n > 0:
                    transposes_q(n - 1, 1 - par)
            run(step)
            transposes_q(m - 1, (m - 1) % 2)

        @block.scalar
        def _(act):
            def square_x(n, par, k):
                act.wait_ge(x_in[par], 16 * (k + 1))
                if n > 0:
                    act.wait_ge(ssx_ok, n)
                if n > 1:
                    act.wait_ge(rsx_ok, n - 1)
                if n > 2:
                    act.wait_ge(ssh_ok, n - 2)
                act.activation(sq[:, 0:DM], x[:, par, :], ACT.Square, accum_out=ssx[:, par, :]).then_inc(ssx_ok, 1)

            def evac_x(n, par):
                b = t_base[n]
                if n > 1:
                    act.wait_ge(mm_done, 7 * (n - 1))
                for u in range(2):
                    act.wait_ge(tp_done, b + u + 1)
                    act.copy(xnT[:, par, 4 * u:4 * u + 4, :], tpb[:, u, :, :]).then_inc(tp_evac, 1)

            def evac_q(n, par, k):
                b = q_base[n]
                if n > 0:
                    act.wait_ge(st[1 - par], 16 * NST * ((n - 1) // 2 + 1))
                for u in range(4):
                    act.wait_ge(tp_done, b + u + 1)
                    if u < 2:
                        ins = act.copy(qTb[:, u * 512:(u + 1) * 512], tpb[:, u, :, :].rearrange("p a b -> p (a b)"))
                    elif u == 2:
                        ins = act.copy(iqTb[:], tpb[:, 0, :, :].rearrange("p a b -> p (a b)"))
                    else:
                        act.copy(kT[:, :, (t0 + n) * P:(t0 + n + 1) * P], tpb[:, 1, 0:2, :])
                        ins = act.copy(ikT[:, (t0 + n) * P:(t0 + n + 1) * P], tpb[:, 1, 2, :])
                    ins.then_inc(tp_evac, 1)

            def copy_raw(n, par, k):
                if n > 1:
                    act.wait_ge(tp_done, q_base[n - 2] + 4)
                    act.wait_ge(gate_ok, n - 1)
                act.wait_ge(st[par], 16 * NST * k)
                for c, (a, cw) in enumerate(CHUNKS):
                    act.wait_ge(mm_done, 7 * n + c + 1)
                    src = acc[:, c % 6, 0:cw]
                    if c == 2:
                        act.copy(v_nat[:, t0 + n, :], src[:, 256:512])
                        ins = act.copy(raw[:, par, K0:K0 + 256], src[:, 0:256])
                    elif c == 4:
                        act.mul(iw_nat[:, t0 + n, :], src[:, 64:72], IH ** -0.5 * ID ** -0.5)
                        ins = act.copy(raw[:, par, IK0:IK0 + 64], src[:, 0:64])
                    else:
                        ins = act.copy(raw[:, par, a:a + cw], src)
                    ins.then_inc(raw_ok, 1)

            def squares(n, par):
                if n > 0:
                    act.wait_ge(ssh_ok, n)
                act.wait_ge(raw_ok, 7 * n + 5)
                act.activation(sq[:, 0:1280], raw[:, par, 0:1280], ACT.Square)
                act.activation(sq[:, 1280:1344], raw[:, par, IK0:IK0 + 64], ACT.Square).then_inc(sq_ok, 1)
                act.wait_ge(raw_ok, 7 * n + 7)
                act.activation(sgate[:, par, :], raw[:, par, G0:ATT_IN], ACT.Tanh, scale=0.5).then_inc(tanh_ok, 1)

            square_x(0, 0, 0)
            if m > 1:
                square_x(1, 1, 0)
            evac_x(0, 0)

            def step(n, par, k):
                if n + 1 < m:
                    evac_x(n + 1, 1 - par)
                if n + 2 < m:
                    square_x(n + 2, par, k + 1)
                copy_raw(n, par, k)
                if n > 0:
                    evac_q(n - 1, 1 - par, k if par else k - 1)
                squares(n, par)
            run(step)
            evac_q(m - 1, (m - 1) % 2, (m - 1) // 2)

        @block.vector
        def _(dve):
            if first:
                dve.wait_ge(const_in, 80)
                dve.tensor_scalar(gqs[:], gq[:], HD ** -0.5, None, ALU.mult).then_inc(gains_ok, 1)
                dve.wait_ge(gains_ok, 1)

            def norm_x(n, par):
                dve.wait_ge(rsx_ok, n + 1)
                dve.scalar_tensor_tensor(x[:, par, :], x[:, par, :], rsx[:, par, :], gx[:], ALU.mult, ALU.mult).then_inc(xn_ok, 1)
            norm_x(0, 0)
            if m > 1:
                norm_x(1, 1)

            def step(n, par, k):
                if n + 2 < m:
                    norm_x(n + 2, par)
                between(dve, n)
                dve.wait_ge(sq_ok, n + 1)
                if n > 1:
                    dve.wait_ge(rsh_ok, n - 1)
                dve.tensor_reduce(ssh[:, par, 0:10], sq[:, 0:1280].rearrange("p (h d) -> p h d", h=10), AX.X, ALU.add)
                dve.tensor_reduce(ssh[:, par, 10:11], sq[:, 1280:1344], AX.X, ALU.add).then_inc(ssh_ok, 1)
                dve.wait_ge(rsh_ok, n + 1)
                for h in range(10):
                    r = raw[:, par, h * HD:(h + 1) * HD]
                    dve.scalar_tensor_tensor(r, r, rsh[:, par, h:h + 1], (gqs if h < H else gk)[:], ALU.mult, ALU.mult)
                r = raw[:, par, IK0:IK0 + 64]
                dve.wait_ge(st[par], 16 * NST * k)
                for a in range(2):
                    ins = dve.scalar_tensor_tensor(ikk[:, par, a, :], r, rsh[:, par, 10:11], gik[:], ALU.mult, ALU.mult)
                ins.then_inc(nat_ok, 1)
            run(step)


def sample_scores(nc, env):
    d, keep = env["dram"], env["keep"]
    HALF, CW = PAST // 2, 512
    NSTEP = 64
    RING = 4
    with ExitStack() as ctx:
        def sb(name, shape, dt=F32):
            return ctx.enter_context(nc.sbuf_tensor(name, shape, dt))

        def sem(name):
            return new_sem(nc, env, name)

        iqs = sb("iqs", [P, 4, P])
        bd = sb("iq_blockdiag", [P, 4, P])
        wred = sb("iw_reduce", [P, 4, 2, P])
        iwcol = sb("iwcol", [P, 4])
        delta16 = sb("delta16", [P, 16])
        ikn = sb("ik_new", [P, 4, DS])
        cmn = sb("new_causal", [P, DS])
        pti = sb("pt_int", [4, 8 * 16], I32)
        ptf = sb("pt_f", [4, 8 * 16])
        e4 = sb("e4", [4, P])
        j32 = sb("j32", [P, 1])
        idxf = sb("idx_f", [P, 8 * 16])
        idx = sb("idx_page", [P, 8, 16], U32)
        kraw = sb("kraw", [P, RING, 2, 4, ID])
        kTs = sb("kTs", [P, 2, CW])
        rl = sb("relu_s", [P, 2, CW])
        tps = ctx.enter_context(nc.psum_tensor("tps", [P, 2, 4, P], F32))
        sps = ctx.enter_context(nc.psum_tensor("sps", [P, 2, CW], F32))
        rps = ctx.enter_context(nc.psum_tensor("rps", [P, 2, CW], F32))
        mps = ctx.enter_context(nc.psum_tensor("mps", [P, CW], F32))
        ident, ikT, iw_nat, scores = keep["ident"], keep["ikT"], keep["iw_nat"], keep["scores"]

        loads = sem("loads")
        iwl_out = env["stores"]["iwl_out"]
        iwl_in = sem("iwl_in")
        zeroed = sem("zeroed")
        ptf_ok = sem("ptf_ok")
        ptb_ok = sem("ptb_ok")
        idx_ok = sem("idx_ok")
        prep_ok = sem("prep_ok")
        k_in = [sem(f"k_in{i}") for i in range(RING)]
        kT_done = sem("kT_done")
        kT_ok = sem("kT_ok")
        s_done = sem("s_done")
        relu_ok = sem("relu_ok")
        red_done = sem("red_done")
        sc_ok = sem("sc_ok")
        dv = sem("dve_chain_scores")
        steps = [(c, s, p) for c in range(HALF // CW) for s in range(2) for p in range(4)]

        block = ctx.enter_context(nc.Block())

        @block.sync
        def _(sp):
            sp.dma_start(iqs[:].rearrange("p a b -> p (a b)"), d["iqT_d"][0:P, :]).then_inc(loads, 16)
            sp.dma_start(delta16[:], d["c_delta16"]).then_inc(loads, 16)
            sp.dma_start(cmn[:], d["c_new_causal"]).then_inc(loads, 16)
            sp.dma_start(e4[:], d["c_e4"]).then_inc(loads, 16)
            sp.dma_start(j32[:], d["c_j32"]).then_inc(loads, 16)
            with nc.allow_non_contiguous_dma(reason="512 page ids"):
                sp.dma_start(pti[:], d["page_table"].rearrange("b (g k) -> k (b g)", k=4)).then_inc(loads, 16)
                for b in range(DB):
                    sp.dma_start(d["iwl_d"][b].rearrange("h t -> t h"), iw_nat[b * DS:(b + 1) * DS, 0, :]).then_inc(iwl_out, 16)
                sp.wait_ge(iwl_out, 16 * DB)
                sp.dma_start(iwcol[:], d["iwl_d"].rearrange("(p b) h t -> (b h t) p", p=4)).then_inc(iwl_in, 16)

        @block.gpsimd
        def _(pool):
            pool.memset(bd[:], 0.0)
            pool.memset(wred[:], 0.0).then_inc(zeroed, 1)
            pool.wait_ge(idx_ok, 1)
            rows = d["cache_idx_k"].rearrange("n (j r) l e -> (n j) (r l e)", r=4)
            for j, (c, s, p) in enumerate(steps):
                if j >= RING:
                    pool.wait_ge(kT_done, j - RING + 1)
                for b2 in range(2):
                    pool.indirect_dma_start(
                        kraw[:, j % RING, b2, :, :].rearrange("p r e -> p (r e)"), None, rows,
                        bass.IndirectOffsetOnAxis(ap=idx[:, 2 * p + b2, s * 8 + c:s * 8 + c + 1], axis=0),
                    ).then_inc(k_in[j % RING], 16)

        @block.tensor
        def _(pe):
            pe.wait_ge(ptf_ok, 1)
            pe.matmul(mps[:, 0:128], e4[:], ptf[:], start=True, stop=True).then_inc(ptb_ok, 1)

            def turn(j):
                pe.wait_ge(k_in[j % RING], 32 * (j // RING + 1))
                if j >= 2:
                    pe.wait_ge(kT_ok, j - 1)
                for b2 in range(2):
                    for rp in range(2):
                        ins = pe.transpose(tps[:, j % 2, 2 * b2 + rp, :],
                                           kraw[:, j % RING, b2, 2 * rp:2 * rp + 2, :].rearrange("p r e -> p (r e)"), ident[:])
                ins.then_inc(kT_done, 1)

            def dots(j):
                c, s, p = steps[j]
                pe.wait_ge(kT_ok, j + 1)
                if j >= 2:
                    pe.wait_ge(relu_ok, j - 1)
                pe.matmul(sps[:, j % 2, :], bd[:, p, :], kTs[:, j % 2, :], start=True, stop=True).then_inc(s_done, 1)

            def head_sum(j):
                c, s, p = steps[j]
                pe.wait_ge(relu_ok, j + 1)
                if c >= 2 and s == 0 and p == 0:
                    pe.wait_ge(sc_ok, c - 1)
                pe.matmul(rps[:, c % 2, :], wred[:, p, s, :], rl[:, j % 2, :],
                          start=(s == 0 and p == 0), stop=(s == 1 and p == 3)).then_inc(red_done, 1)

            pe.wait_ge(prep_ok, 1)
            turn(0)
            for j in range(NSTEP):
                if j + 1 < NSTEP:
                    turn(j + 1)
                dots(j)
                if j >= 1:
                    head_sum(j - 1)
            head_sum(NSTEP - 1)
            for p in range(4):
                j = NSTEP + p
                pe.wait_ge(relu_ok, j - 1)
                pe.matmul(sps[:, j % 2, 0:DS], bd[:, p, :], ikn[:, p, :], start=True, stop=True).then_inc(s_done, 1)
                if p == 0:
                    pe.wait_ge(ptb_ok, 1)
                    pe.wait_ge(idx_ok, 1)
                pe.wait_ge(relu_ok, j + 1)
                pe.matmul(mps[:, 0:DS], wred[:, p, 1, :], rl[:, j % 2, 0:DS], start=(p == 0), stop=(p == 3)).then_inc(red_done, 1)

        @block.scalar
        def _(act):
            def scores_out(c):
                act.wait_ge(red_done, 8 * (c + 1))
                act.copy(scores[:, c * CW:(c + 1) * CW], rps[:, c % 2, :]).then_inc(sc_ok, 1)
            for j in range(NSTEP + 4):
                act.wait_ge(s_done, j + 1)
                if j >= 2:
                    act.wait_ge(red_done, j - 1)
                n = CW if j < NSTEP else DS
                act.activation(rl[:, j % 2, 0:n], sps[:, j % 2, 0:n], ACT.Relu).then_inc(relu_ok, 1)
                if j % 8 == 1 and 8 < j:
                    scores_out(j // 8 - 1)

        @block.vector
        def _(dve):
            link = chain(dve, dv)
            dve.wait_ge(loads, 96)
            dve.tensor_copy(ptf[:], pti[:]).then_inc(ptf_ok, 1)
            dve.wait_ge(ptb_ok, 1)
            link(dve.tensor_scalar(idxf[:], mps[:, 0:128], 32.0, j32[:], ALU.mult, ALU.add))
            dve.tensor_copy(idx[:].rearrange("p a b -> p (a b)"), idxf[:]).then_inc(idx_ok, 1)
            dve.wait_ge(zeroed, 1)
            for b2 in range(2):
                for hp in range(2):
                    dst = bd[b2 * 64:(b2 + 1) * 64, :, b2 * 64:(b2 + 1) * 64].rearrange("k p (hh two t) -> k p hh two t", two=2, t=DS)[:, :, :, hp, :]
                    src = iqs[hp * 64:(hp + 1) * 64, :, 0:NS].rearrange("k hh (p two t) -> k p hh two t", two=2, t=DS)[:, :, :, b2, :]
                    dve.tensor_copy(dst, src)
                dve.tensor_copy(ikn[b2 * 64:(b2 + 1) * 64, :, :],
                                ikT[b2 * 64:(b2 + 1) * 64, 0:NS].rearrange("k (p two t) -> k p two t", two=2, t=DS)[:, :, b2, :])
            dve.wait_ge(iwl_in, 16)
            for p in range(4):
                for s in range(2):
                    a = 64 * s + 16 * p
                    ins = dve.tensor_scalar(wred[:, p, s, a:a + 16], delta16[:], iwcol[:, p:p + 1], None, ALU.mult)
            ins.then_inc(prep_ok, 1)
            for j in range(NSTEP):
                dve.wait_ge(kT_done, j + 1)
                if j >= 2:
                    dve.wait_ge(s_done, j - 1)
                for b2 in range(2):
                    for r2 in range(2):
                        dst = kTs[b2 * 64:(b2 + 1) * 64, j % 2, :].rearrange("k (q rp r2) -> k rp q r2", r2=2, rp=2)[:, :, :, r2]
                        ins = dve.tensor_copy(dst, tps[r2 * 64:(r2 + 1) * 64, j % 2, 2 * b2:2 * b2 + 2, :])
                ins.then_inc(kT_ok, 1)
            dve.wait_ge(red_done, NSTEP + 4)
            dve.tensor_copy(scores[:, HALF - CW:HALF], rps[:, (HALF // CW - 1) % 2, :])
            link(dve.tensor_tensor(scores[:, HALF:HALF + DS], mps[:, 0:DS], cmn[:], ALU.add))


def extraction(env, sem):
    keep = env["keep"]
    scores, top_v, top_i = keep["scores"], keep["top_v"], keep["top_i"]
    state = {}

    def rounds(dve, n):
        link = state.setdefault("link", chain(dve, sem))
        for r in range(4 * n, 4 * n + 4):
            v = top_v[:, 8 * r:8 * r + 8]
            link(dve.max(v, scores[:]))
            dve.max_index(top_i[:, 8 * r:8 * r + 8], v, scores[:])
            link(dve.match_replace(scores[:], v, scores[:], -3e38))
    return rounds


def sample_select(nc, env):
    d, keep = env["dram"], env["keep"]
    top_v, top_i, ident = keep["top_v"], keep["top_i"], keep["ident"]
    rowidx, mask_s, mask_n = keep["rowidx"], keep["mask_s"], keep["mask_n"]
    with ExitStack() as ctx:
        def sb(name, shape, dt=F32):
            return ctx.enter_context(nc.sbuf_tensor(name, shape, dt))

        def sem(name):
            return new_sem(nc, env, name)

        off = sb("half_off", [P, 1])
        idxf = sb("key_f", [P, TOPK])
        rv = sb("rev_v", [NS, TOPK])
        ri = sb("rev_i", [NS, TOPK])
        take = sb("take_a", [NS, TOPK])
        key = sb("key", [NS, TOPK])
        keyi = sb("key_i", [NS, TOPK], I32)
        pgi = sb("page_i", [NS, TOPK], I32)
        ofi = sb("off_i", [NS, TOPK], I32)
        pg = sb("page_f", [NS, TOPK])
        of = sb("off_f", [NS, TOPK])
        phys = sb("phys", [NS, TOPK])
        pg2 = sb("page_of_half", [P, TOPK])
        found = sb("page_found", [P, NPG // 2, TOPK])
        phys2 = sb("phys_of_half", [P, TOPK])
        pti = sb("pt_rows_i", [P, NPG // 2], I32)
        ptf = sb("pt_rows", [P, NPG // 2])
        bias = sb("slot_bias", [NS, TOPK])
        sel = sb("sel_new", [NS, DS])
        selb = sb("sel_bias", [NS, 4, DS])
        hit = sb("hit", [NS, DS, TOPK])
        eq = sb("expand_q", [NS, 4, P])
        cmn = sb("new_allowed", [P, 32])
        tp = ctx.enter_context(nc.psum_tensor("tp_rows", [P, 2, NS], F32))
        mp = ctx.enter_context(nc.psum_tensor("mp", [P, 4, 512], F32))
        loads = sem("sel_loads")
        key_ok = sem("key_ok")
        rows_ok = sem("rows_ok")
        mm = sem("sel_mm")
        dv = sem("dve_chain_select")
        block = ctx.enter_context(nc.Block())

        @block.sync
        def _(sp):
            sp.dma_start(off[:], d["c_half_off"]).then_inc(loads, 16)
            sp.dma_start(eq[:].rearrange("p a b -> p (a b)"), d["c_expand_q"]).then_inc(loads, 16)
            sp.dma_start(cmn[:], d["c_new_allowed"]).then_inc(loads, 16)
            for b in range(DB):
                for u in range(2):
                    sp.dma_start(pti[u * NS + b * DS:u * NS + (b + 1) * DS, :],
                                 d["page_table"][b:b + 1, u * NPG // 2:(u + 1) * NPG // 2].partition_broadcast(DS)).then_inc(loads, 16)

        @block.vector
        def _(dve):
            link = chain(dve, dv)
            dve.wait_ge(loads, 16 * (3 + 2 * DB))
            link(dve.tensor_copy(idxf[:], top_i[:]))
            link(dve.tensor_scalar(idxf[:], idxf[:], off[:], None, ALU.add))
            link(dve.tensor_copy(rv[:], top_v[NS:P, ::-1]))
            link(dve.tensor_copy(ri[:], idxf[NS:P, ::-1]))
            link(dve.tensor_tensor(take[:], top_v[0:NS, :], rv[:], ALU.is_ge))
            link(dve.tensor_tensor(key[:], idxf[0:NS, :], ri[:], ALU.subtract))
            link(dve.tensor_tensor(key[:], key[:], take[:], ALU.mult))
            link(dve.tensor_tensor(key[:], key[:], ri[:], ALU.add))
            link(dve.tensor_scalar(bias[:], key[:], float(PAST), -BIG, ALU.is_ge, ALU.mult))
            for s in range(DS):
                ins = dve.tensor_scalar(hit[:, s, :], key[:], float(PAST + s), 0.0, ALU.is_equal, ALU.add, accum_out=sel[:, s:s + 1])
            link(ins)
            for a in range(4):
                dve.tensor_scalar(selb[:, a, :], sel[:], -1.0, BIG, ALU.add, ALU.mult)
            link(dve.tensor_copy(keyi[:], key[:]))
            link(dve.tensor_scalar(pgi[:], keyi[:], 7, None, ALU.arith_shift_right))
            link(dve.tensor_scalar(ofi[:], keyi[:], 127, None, ALU.bitwise_and))
            link(dve.tensor_copy(pg[:], pgi[:]))
            dve.tensor_copy(of[:], ofi[:])
            dve.tensor_copy(ptf[:], pti[:])
            dve.tensor_copy(pg2[0:NS, :], pg[:])
            link(dve.tensor_scalar(pg2[NS:, :], pg[:], float(-NPG // 2), None, ALU.add))
            for g in range(NPG // 2):
                ins = dve.tensor_scalar(found[:, g, :], pg2[:], float(g), ptf[:, g:g + 1], ALU.is_equal, ALU.mult)
            link(ins)
            link(dve.tensor_reduce(phys2[:], found[:].rearrange("p g k -> p k g"), AX.X, ALU.add))
            link(dve.tensor_copy(phys[:], phys2[NS:, :]))
            link(dve.tensor_tensor(phys[:], phys[:], phys2[0:NS, :], ALU.add))
            dve.scalar_tensor_tensor(phys[:], phys[:], float(PAGE), of[:], ALU.mult, ALU.add).then_inc(key_ok, 1)
            dve.wait_ge(mm, 1)
            dve.tensor_copy(rowidx[:], tp[:])
            dve.wait_ge(mm, 2)
            dve.tensor_copy(mask_s[:], mp[:, :, 0:TOPK])
            for t in range(4):
                ins = dve.tensor_tensor(mask_n[:, t, :], mp[:, t, TOPK:TOPK + 32], cmn[:], ALU.add)
            link(ins)

        @block.tensor
        def _(pe):
            pe.wait_ge(key_ok, 1)
            for c in range(2):
                ins = pe.transpose(tp[:, c, :], phys[:, c * P:(c + 1) * P], ident[0:NS, 0:NS])
            ins.then_inc(mm, 1)
            for t in range(4):
                pe.matmul(mp[:, t, 0:TOPK], eq[:, t, :], bias[:], start=True, stop=True)
                ins = pe.matmul(mp[:, t, TOPK:TOPK + 32], eq[:, t, :], selb[:].rearrange("p a b -> p (a b)"), start=True, stop=True)
            ins.then_inc(mm, 1)


def sample_attend(nc, env):
    d, keep = env["dram"], env["keep"]
    ident, kT, og = keep["ident"], keep["kT"], keep["og_s"]
    ikT, iw_nat, key_mask = keep["ikT"], keep["iw_nat"], keep["key_mask"]
    rowidx, mask_s, mask_n = keep["rowidx"], keep["mask_s"], keep["mask_n"]
    KR = 16
    QT = 16
    NQT = NS // QT
    ROUNDS = TOPK // 8
    parts = [(i, h, a) for i in range(FREE, NB) for h in range(IH) for a in range(0, (i + 1) * P, 512)]
    first_part = {i: min(n for n, q in enumerate(parts) if q[0] == i) for i in range(FREE, NB)}
    first_part[NB] = len(parts)
    starts = dict(zip(range(FREE + 1, NB), (2, 16, 33, 50, 70)))
    part_after = {starts[q[0]] + n - first_part[q[0]]: n for n, q in enumerate(parts) if q[0] > FREE}
    LOGITS_AT, EXP_AT, TURN_AT = 0, 8, 14
    V_AT, V_STEP = 16, 2
    turns = {"shifted": ((4, 6), (6, 4), (7, 5)), "normed": ((4, 20), (6, 9), (7, 11)),
             "copy_probs": ((5, 0), (6, 16), (7, 17)), "gated": ((6, 2), (7, 4), (7, 31))}
    sample_turn = {at: (what, t) for what, ats in turns.items() for t, at in enumerate(ats)}
    with ExitStack() as ctx:
        def sb(name, shape, dt=F32):
            return ctx.enter_context(nc.sbuf_tensor(name, shape, dt))

        def sem(name):
            return new_sem(nc, env, name)

        qs = sb("qs", [P, H, P])
        qTq = sb("qTq", [P, NS, H])
        kg = sb("kg", [P, KR, 256])
        vg = sb("vg", [P, 2, 2 * QT, 256])
        ktg = sb("ktg", [P, 2, 2, P])
        vnew = sb("vnew", [32, NQT, HD])
        gnat = sb("gnat", [NS, DM])
        gT = sb("gT", [P, H, NS])
        lt = sb("lt", [P, 2, P])
        lg = sb("lg", [P, TOPK + 32])
        pr = sb("pr", [P, TOPK + 32])
        mx = sb("mx", [P, 1])
        rs = sb("rs", [P, 1])
        pT = sb("pT", [P, 3, P])
        iqp = sb("iq_prompt", [P, 2, IH // 2, P])
        rl = sb("relu_parts", [P, IH, SEQ])
        causal = sb("causal_p", [P, P])
        v8 = sb("v8", [P, 8])
        ksp = ctx.enter_context(nc.psum_tensor("key_score", [P, 2, 512], F32))
        tpk = ctx.enter_context(nc.psum_tensor("tpk", [P, 2, 512], F32))
        ltp = ctx.enter_context(nc.psum_tensor("ltp", [P, 512], F32))
        lgp = ctx.enter_context(nc.psum_tensor("lgp", [P, 512], F32))
        ptp = ctx.enter_context(nc.psum_tensor("ptp", [P, 512], F32))
        op = ctx.enter_context(nc.psum_tensor("op", [P, 512], F32))
        loads = sem("sa_loads")
        k_in = [sem(f"kg_in{i}") for i in range(KR)]
        v_in = [sem("vg_in0"), sem("vg_in1")]
        qTq_ok = sem("qTq_ok")
        gT_done = sem("gT_done")
        gT_ok = sem("gT_ok")
        kT_done = sem("kgT_done")
        kT_ok = sem("kgT_ok")
        dot_done = sem("dot_done")
        lt_done = sem("lt_done")
        lt_ok = sem("lt_ok")
        lg_done = sem("lg_done")
        mx_ok = sem("mx_ok")
        ex_ok = sem("ex_ok")
        pr_ok = sem("pr_ok")
        pt_done = sem("pt_done")
        pt_ok = sem("pt_ok")
        o_done = sem("o_done")
        o_ok = sem("o_ok")
        dv = sem("dve_chain_sa")
        causal_in = sem("causal_in")
        iq_in = [sem("iq_in0"), sem("iq_in1")]
        ks_done = sem("ks_done")
        relu_ok = sem("relu_part_ok")
        added = sem("heads_added")
        block = ctx.enter_context(nc.Block())
        ck = d["cache_k"].rearrange("n j l g e -> (n j) (l g e)")
        cv = d["cache_v"].rearrange("n j l g e -> (n j) (l g e)")

        @block.sync
        def _(sp):
            sp.dma_start(qs[:].rearrange("p a b -> p (a b)"), d["qT_d"][0:P, :]).then_inc(loads, 16)
            sp.dma_start(gnat[:], d["gate_d"][0:NS, :]).then_inc(loads, 16)
            for g in range(G):
                sp.dma_start(vnew[g * QT:(g + 1) * QT, :, :],
                             d["v_all"][0:NS, g * HD:(g + 1) * HD].rearrange("(t q) e -> q t e", t=NQT)).then_inc(loads, 16)
            sp.dma_start(causal[:], d["c_causal"]).then_inc(causal_in, 16)
            for i in range(FREE, NB):
                if i >= FREE + 2:
                    sp.wait_ge(ks_done, first_part[i - 1])
                sp.dma_start(iqp[:, i % 2, :, :].rearrange("p a b -> p (a b)"),
                             d["iqT_d"][(i + 1) * P:(i + 2) * P, :]).then_inc(iq_in[i % 2], 16)

        @block.gpsimd
        def _(pool):
            for t in range(NQT):
                for u in range(2 * QT):
                    q, c = t * QT + u // 2, u % 2
                    j = t * 2 * QT + u
                    if j >= KR:
                        pool.wait_ge(kT_done, j - KR + 1)
                    pool.indirect_dma_start(kg[:, j % KR, :], None, ck,
                                            bass.IndirectOffsetOnAxis(ap=rowidx[:, c, q:q + 1], axis=0)).then_inc(k_in[j % KR], 16)
                    if t >= 2 and u == 0:
                        pool.wait_ge(o_done, t - 1)
                    pool.indirect_dma_start(vg[:, t % 2, u, :], None, cv,
                                            bass.IndirectOffsetOnAxis(ap=rowidx[:, c, q:q + 1], axis=0)).then_inc(v_in[t % 2], 16)

        @block.tensor
        def _(pe):
            pe.wait_ge(loads, 64)
            for h in range(H):
                ins = pe.transpose(tpk[:, h // 4, (h % 4) * NS:(h % 4 + 1) * NS], gnat[:, h * HD:(h + 1) * HD], ident[0:NS, 0:NS])
            ins.then_inc(gT_done, 1)
            pe.wait_ge(gT_ok, 1)
            pe.wait_ge(qTq_ok, 1)

            def turn(j):
                pe.wait_ge(k_in[j % KR], 16 * (j // KR + 1))
                if j >= 2:
                    pe.wait_ge(kT_ok, j - 1)
                for g in range(G):
                    ins = pe.transpose(tpk[:, j % 2, g * P:(g + 1) * P], kg[:, j % KR, g * HD:(g + 1) * HD], ident[:])
                ins.then_inc(kT_done, 1)

            def dots(j):
                t, u = divmod(j, 2 * QT)
                q, c = t * QT + u // 2, u % 2
                pe.wait_ge(kT_ok, j + 1)
                if u == 0 and t >= 1:
                    pe.wait_ge(lt_ok, t)
                for g in range(G):
                    a = c * P + (u // 2) * H + g * GRP
                    ins = pe.matmul(ltp[:, a:a + GRP], ktg[:, j % 2, g, :], qTq[:, q, g * GRP:(g + 1) * GRP], start=True, stop=True)
                ins.then_inc(dot_done, 1)

            def key_score(n):
                i, h, a = parts[n]
                half, w = h % 2, min(512, (i + 1) * P - a)
                pe.wait_ge(iq_in[i % 2], 16 * ((i - FREE) // 2 + 1))
                if n >= 2:
                    pe.wait_ge(relu_ok, n - 1)
                pe.matmul(ksp[:, n % 2, 0:w], iqp[half * 64:half * 64 + 64, i % 2, h // 2, :],
                          ikT[half * 64:half * 64 + 64, P + a:P + a + w], start=True, stop=True).then_inc(ks_done, 1)

            NJ = NQT * 2 * QT
            for n in range(first_part[FREE + 1]):
                key_score(n)
            turn(0)

            def logits(t):
                pe.wait_ge(lt_ok, t + 1)
                if t >= 1:
                    pe.wait_ge(mx_ok, t)
                for c in range(2):
                    pe.transpose(lgp[:, c * P:(c + 1) * P], lt[:, c, :], ident[:])
                pe.matmul(lgp[:, TOPK:TOPK + 32], qTq[:, t * QT:(t + 1) * QT, :].rearrange("p a b -> p (a b)"),
                          kT[:, :, t * QT:(t + 1) * QT], start=True, stop=True).then_inc(lg_done, 1)

            def turn_probs(t):
                pe.wait_ge(pr_ok, t + 1)
                if t >= 1:
                    pe.wait_ge(pt_ok, t)
                for c in range(2):
                    pe.transpose(ptp[:, c * P:(c + 1) * P], pr[:, c * P:(c + 1) * P], ident[:])
                pe.transpose(ptp[0:32, 256:256 + P], pr[:, TOPK:TOPK + 32], ident[:]).then_inc(pt_done, 1)

            def weigh(t, u):
                if u == 0:
                    pe.wait_ge(pt_ok, t + 1)
                    pe.wait_ge(v_in[t % 2], 16 * 2 * QT * (t // 2 + 1))
                    if t >= 1:
                        pe.wait_ge(o_ok, t)
                    pe.matmul(op[:, 0:P], vnew[:, t, :], pT[0:32, 2, :], start=True, stop=False, skip_group_check=True)
                for g in range(G):
                    a = (u // 2) * H + g * GRP
                    ins = pe.matmul(op[:, a:a + GRP], vg[:, t % 2, u, g * HD:(g + 1) * HD], pT[:, u % 2, a:a + GRP],
                                    start=False, stop=(u == 2 * QT - 1 and g == G - 1), skip_group_check=True)
                if u == 2 * QT - 1:
                    ins.then_inc(o_done, 1)

            def behind(t, u):
                if u == LOGITS_AT:
                    logits(t)
                if u == TURN_AT:
                    turn_probs(t)
                for v in range(V_STEP * (u - V_AT), V_STEP * (u - V_AT + 1)):
                    if 0 <= v < 2 * QT:
                        weigh(t, v)
            for t in range(NQT):
                for u in range(2 * QT):
                    j = t * 2 * QT + u
                    if j + 1 < NJ:
                        turn(j + 1)
                    dots(j)
                    if j in part_after:
                        key_score(part_after[j])
                    if t >= 1:
                        behind(t - 1, u)
            for u in range(2 * QT):
                behind(NQT - 1, u)

        @block.scalar
        def _(act):
            def key_relu(n):
                i, h, a = parts[n]
                w = min(512, (i + 1) * P - a)
                act.wait_ge(ks_done, n + 1)
                if i > FREE:
                    act.wait_ge(added, i - FREE)
                act.activation(rl[:, h, a:a + w], ksp[:, n % 2, 0:w], ACT.Relu).then_inc(relu_ok, 1)

            def copy_logits(t):
                act.wait_ge(dot_done, (t + 1) * 2 * QT)
                if t >= 1:
                    act.wait_ge(lg_done, t)
                act.copy(lt[:].rearrange("p a b -> p (a b)"), ltp[:, 0:256]).then_inc(lt_ok, 1)

            def exps(t):
                act.wait_ge(mx_ok, t + 1)
                if t >= 1:
                    act.wait_ge(pt_done, t)
                act.activation(pr[:], lg[:], ACT.Exp, bias=mx[:], accum_out=rs[:]).then_inc(ex_ok, 1)
            for n in range(first_part[FREE + 1]):
                key_relu(n)
            for t in range(NQT):
                for u in range(2 * QT):
                    j = t * 2 * QT + u
                    act.wait_ge(kT_done, j + 1)
                    if j >= 2:
                        act.wait_ge(dot_done, j - 1)
                    act.copy(ktg[:, j % 2, :, :].rearrange("p a b -> p (a b)"), tpk[:, j % 2, 0:256]).then_inc(kT_ok, 1)
                    if j in part_after:
                        key_relu(part_after[j])
                    if t >= 1 and u == EXP_AT:
                        exps(t - 1)
                copy_logits(t)
            exps(NQT - 1)

        @block.vector
        def _(dve):
            link = chain(dve, dv)
            dve.wait_ge(loads, 64)
            dve.tensor_copy(qTq[:], qs[:, :, 0:NS].rearrange("p h q -> p q h")).then_inc(qTq_ok, 1)
            dve.memset(og[:], 0.0)
            dve.wait_ge(gT_done, 1)
            for a in range(2):
                ins = dve.tensor_copy(gT[:, 4 * a:4 * a + 4, :].rearrange("p a b -> p (a b)"), tpk[:, a, 0:256])
            ins.then_inc(gT_ok, 1)
            dve.wait_ge(gT_ok, 1)

            def shifted(t):
                dve.wait_ge(lg_done, t + 1)
                if t >= 1:
                    dve.wait_ge(ex_ok, t)
                link(dve.tensor_tensor(lg[:, 0:TOPK], lgp[:, 0:TOPK], mask_s[:, t, :], ALU.add))
                link(dve.tensor_tensor(lg[:, TOPK:], lgp[:, TOPK:TOPK + 32], mask_n[:, t, :], ALU.add))
                dve.tensor_reduce(mx[:], lg[:], AX.X, ALU.max, negate=True).then_inc(mx_ok, 1)

            def normed(t):
                dve.wait_ge(ex_ok, t + 1)
                link(dve.reciprocal(rs[:], rs[:]))
                dve.tensor_scalar(pr[:], pr[:], rs[:], None, ALU.mult).then_inc(pr_ok, 1)

            def copy_probs(t):
                dve.wait_ge(pt_done, t + 1)
                if t >= 1:
                    dve.wait_ge(o_done, t)
                dve.tensor_copy(pT[:, 0:2, :].rearrange("p a b -> p (a b)"), ptp[:, 0:256])
                dve.tensor_copy(pT[0:32, 2, :], ptp[0:32, 256:256 + P]).then_inc(pt_ok, 1)

            def gated(t):
                dve.wait_ge(o_done, t + 1)
                dve.tensor_tensor(og[:, :, t * QT:(t + 1) * QT], op[:, 0:P].rearrange("p (q h) -> p h q", h=H),
                                  gT[:, :, t * QT:(t + 1) * QT], ALU.mult).then_inc(o_ok, 1)

            def add_heads(i):
                w = (i + 1) * P
                s = key_mask[:, KM[i]:KM[i] + w]
                dve.wait_ge(relu_ok, first_part[i + 1])
                link(dve.tensor_scalar(s, rl[:, 0, 0:w], iw_nat[:, i + 1, 0:1], None, ALU.mult))
                for h in range(1, IH):
                    ins = dve.scalar_tensor_tensor(s, rl[:, h, 0:w], iw_nat[:, i + 1, h:h + 1], s, ALU.mult, ALU.add)
                    if h < IH - 1:
                        link(ins)
                ins.then_inc(added, 1)
                dve.wait_ge(added, i - FREE + 1)
                diag = key_mask[:, KM[i] + i * P:KM[i] + w]
                link(dve.tensor_tensor(diag, diag, causal[:], ALU.add))

            stages = {"shifted": shifted, "normed": normed, "copy_probs": copy_probs, "gated": gated}

            dve.wait_ge(causal_in, 16)
            for i in range(FREE):
                if i > 0:
                    dve.memset(key_mask[:, KM[i]:KM[i] + i * P], 0.0)
                dve.tensor_copy(key_mask[:, KM[i] + i * P:KM[i + 1]], causal[:])
            for i in range(FREE, NB):
                add_heads(i)
                s = key_mask[:, KM[i]:KM[i + 1]]
                for r in range(ROUNDS):
                    link(dve.max(v8[:], s))
                    link(dve.match_replace(s, v8[:], s, -3e38))
                    if (i, r) in sample_turn:
                        what, t = sample_turn[i, r]
                        stages[what](t)
                link(dve.tensor_scalar(s, s, -2e38, -BIG, ALU.is_gt, ALU.mult))
            for what in ("shifted", "normed", "copy_probs", "gated"):
                stages[what](NQT - 1)


def prompt_attend(nc, env):
    d, keep = env["dram"], env["keep"]
    ident, kT, v_nat, og_s, key_mask = (keep[k] for k in ("ident", "kT", "v_nat", "og_s", "key_mask"))
    with ExitStack() as ctx:
        def sb(name, shape, dt=F32):
            return ctx.enter_context(nc.sbuf_tensor(name, shape, dt))

        def sem(name):
            return new_sem(nc, env, name)

        wo = sb("w_out_att", [P, H, DM])
        q = sb("q_blk", [P, 2, H, P])
        gate = sb("gate_blk", [P, 2, DM])
        x = sb("x_blk", [P, 2, DM])
        lm = sb("lm", [P, 2, SEQ])
        mx = sb("mx_blk", [P, H])
        nmx = sb("nmx_blk", [P, H])
        rs = sb("rs_blk", [P, H])
        ri = sb("ri_blk", [P, H])
        pT = sb("pT_blk", [P, 2, NB, P])
        og = sb("og_blk", [P, 2, DM])
        ogT = sb("ogT_blk", [P, H, P])
        ring = ctx.enter_context(nc.psum_tensor("ring", [P, 2, SEQ], F32))
        tpb = ctx.enter_context(nc.psum_tensor("tp_blk", [P, 2, 4, P], F32))
        ops = ctx.enter_context(nc.psum_tensor("o_blk", [P, 2, 512], F32))

        once = env["stores"]["pa_once"]
        q_in = [sem("q_in0"), sem("q_in1")]
        ring_done = sem("ring_done")
        lm_ok = sem("lm_ok")
        y_ok = sem("y_ok")
        exp_ok = sem("p_ok")
        tp_done = sem("tpb_done")
        tp_evac = sem("tpb_evac")
        o_done = sem("ob_done")
        og_ok = sem("og_ok")
        ogT_use = sem("ogT_use")
        y_out = [env["stores"][f"y1_out{u}"] for u in range(2)]
        dv = sem("dve_chain_pa")

        uses = [("y", 0)]
        for i in range(NB):
            uses += [("l", i * H + h) for h in range(H)] + [("y", i + 1)]
        at = {u: n for n, u in enumerate(uses)}
        emptied = {"y": y_ok, "l": lm_ok}
        tp_at, n = {}, 0
        for i in range(NB):
            for h in range(H + 1):
                tp_at[i, h] = n
                n += (i + 4) // 4 if h < H else 2

        block = ctx.enter_context(nc.Block())

        @block.sync
        def _(sp):
            sp.dma_start(wo[:], d["att_w_out"].rearrange("l (h p) n -> p (l h) n", p=P)).then_inc(once, 16)
            sp.dma_start(x[:, 0, :], d["x_all"][0:P, :]).then_inc(once, 16)
            sp.wait_ge(y_ok, 1)
            sp.dma_start(d["y1_d"][0:P, :], x[:, 0, :]).then_inc(once, 16)
            sp.wait_ge(once, 48)
            for i in range(NB):
                u, r = i % 2, slice((i + 1) * P, (i + 2) * P)
                if i >= 2:
                    sp.wait_ge(y_ok, i)
                    sp.dma_start(d["y1_d"][(i - 1) * P:i * P, :], x[:, u, :]).then_inc(y_out[u], 16)
                    sp.wait_ge(y_out[u], 16 * (i // 2))
                sp.dma_start(q[:, u, :, :].rearrange("p a b -> p (a b)"), d["qT_d"][r, :]).then_inc(q_in[u], 16)
                sp.dma_start(gate[:, u, :], d["gate_d"][r, :]).then_inc(q_in[u], 16)
                sp.dma_start(x[:, u, :], d["x_all"][r, :]).then_inc(q_in[u], 16)
            for i in (NB, NB + 1):
                u = i % 2
                sp.wait_ge(y_ok, i)
                sp.dma_start(d["y1_d"][(i - 1) * P:i * P, :], x[:, u, :]).then_inc(y_out[u], 16)
            for u in range(2):
                sp.wait_ge(y_out[u], 16 * (NB // 2))

        @block.tensor
        def _(pe):
            def claim(u):
                n = at[u]
                if n >= 2:
                    kind, k = uses[n - 2]
                    pe.wait_ge(emptied[kind], k + 1)
                return ring[:, n % 2, :]

            def logits(i, h):
                dst = claim(("l", i * H + h))
                for a in range(0, (i + 1) * P, 512):
                    w = min(512, (i + 1) * P - a)
                    ins = pe.matmul(dst[:, a:a + w], q[:, i % 2, h, :], kT[:, h // GRP, P + a:P + a + w], start=True, stop=True)
                ins.then_inc(ring_done, 1)

            def groups(base, tiles, src):
                for n in range(0, tiles, 4):
                    b = base + n // 4
                    if b >= 2:
                        pe.wait_ge(tp_evac, b - 1)
                    for k in range(n, min(n + 4, tiles)):
                        ins = pe.transpose(tpb[:, b % 2, k - n, :], src[:, k * P:(k + 1) * P], ident[:])
                    ins.then_inc(tp_done, 1)

            def out_proj(n, lhs):
                dst = claim(("y", n))
                for a in range(0, DM, 512):
                    for h in range(H):
                        ins = pe.matmul(dst[:, a:a + 512], lhs[:, h, :], wo[:, h, a:a + 512], start=(h == 0), stop=(h == H - 1))
                ins.then_inc(ring_done, 1)

            pe.wait_ge(once, 32)
            out_proj(0, og_s)
            for i in range(NB):
                pe.wait_ge(q_in[i % 2], 48 * (i // 2 + 1))
                logits(i, 0)
                logits(i, 1)
                for h in range(H):
                    hc = i * H + h
                    pe.wait_ge(exp_ok, hc + 1)
                    groups(tp_at[i, h], i + 1, lm[:, hc % 2, :])
                    pe.wait_ge(tp_evac, tp_at[i, h + 1])
                    if hc >= 2:
                        pe.wait_ge(og_ok, hc - 1)
                    for k in range(i + 1):
                        g = h // GRP
                        ins = pe.matmul(ops[:, hc % 2, 0:HD], pT[:, hc % 2, k, :], v_nat[:, k + 1, g * HD:(g + 1) * HD],
                                        start=(k == 0), stop=(k == i))
                    ins.then_inc(o_done, 1)
                    if h + 2 < H:
                        logits(i, h + 2)
                pe.wait_ge(og_ok, (i + 1) * H)
                groups(tp_at[i, H], H, og[:, i % 2, :])
                pe.wait_ge(tp_evac, tp_at[i, H] + 2)
                out_proj(i + 1, ogT)

        @block.scalar
        def _(act):
            def evac(base, tiles, dst):
                for n in range(0, tiles, 4):
                    b, m = base + n // 4, min(4, tiles - n)
                    act.wait_ge(tp_done, b + 1)
                    act.copy(dst[:, n:n + m, :].rearrange("p a b -> p (a b)"),
                             tpb[:, b % 2, 0:m, :].rearrange("p a b -> p (a b)")).then_inc(tp_evac, 1)

            for i in range(NB):
                for h in range(H):
                    hc, w = i * H + h, (i + 1) * P
                    act.wait_ge(lm_ok, hc + 1)
                    act.activation(lm[:, hc % 2, 0:w], lm[:, hc % 2, 0:w], ACT.Exp, bias=nmx[:, h:h + 1],
                                   accum_out=rs[:, h:h + 1]).then_inc(exp_ok, 1)
                    if hc >= 2:
                        act.wait_ge(o_done, hc - 1)
                    evac(tp_at[i, h], i + 1, pT[:, hc % 2, :, :])
                if i >= 1:
                    act.wait_ge(ring_done, at["y", i] + 1)
                evac(tp_at[i, H], H, ogT)

        @block.vector
        def _(dve):
            link = chain(dve, dv)

            def masked(i, h):
                hc, w = i * H + h, (i + 1) * P
                dve.wait_ge(ring_done, at["l", hc] + 1)
                if hc >= 2:
                    dve.wait_ge(o_done, hc - 1)
                link(dve.tensor_tensor_reduce(lm[:, hc % 2, 0:w], ring[:, at["l", hc] % 2, 0:w], key_mask[:, KM[i]:KM[i] + w],
                                              1.0, -3e38, ALU.add, ALU.max, mx[:, h:h + 1]))
                dve.tensor_scalar(nmx[:, h:h + 1], mx[:, h:h + 1], -1.0, None, ALU.mult).then_inc(lm_ok, 1)

            def normed(i, h):
                hc = i * H + h
                dve.wait_ge(exp_ok, hc + 1)
                link(dve.reciprocal(ri[:, h:h + 1], rs[:, h:h + 1]))
                dve.wait_ge(o_done, hc + 1)
                dve.scalar_tensor_tensor(og[:, i % 2, h * HD:(h + 1) * HD], ops[:, hc % 2, 0:HD], ri[:, h:h + 1],
                                         gate[:, i % 2, h * HD:(h + 1) * HD], ALU.mult, ALU.mult).then_inc(og_ok, 1)

            def residual(n, xv):
                dve.wait_ge(ring_done, at["y", n] + 1)
                dve.tensor_tensor(xv, xv, ring[:, at["y", n] % 2, :], ALU.add).then_inc(y_ok, 1)

            dve.wait_ge(once, 32)
            residual(0, x[:, 0, :])
            for i in range(NB):
                dve.wait_ge(q_in[i % 2], 48 * (i // 2 + 1))
                if i >= 2:
                    dve.wait_ge(tp_done, tp_at[i - 2, H] + 2)
                masked(i, 0)
                masked(i, 1)
                for h in range(H):
                    normed(i, h)
                    if h + 2 < H:
                        masked(i, h + 2)
                residual(i + 1, x[:, i % 2, :])


class Ring:

    def __init__(self, size, uses):
        self.size, self.uses, self.at, self.turn, seen = size, uses, {}, {}, {}
        for n, (key, reader) in enumerate(uses):
            seen[id(reader)] = seen.get(id(reader), 0) + 1
            self.at[key], self.turn[key] = n, seen[id(reader)]

    def slot(self, key):
        return self.at[key] % self.size

    def claim(self, pe, key):
        n = self.at[key]
        if n >= self.size:
            before, reader = self.uses[n - self.size]
            pe.wait_ge(reader, self.turn[before])
        return n % self.size

    def filled(self, key):
        return self.at[key] + 1


def dn_inputs(nc, env):
    d, keep = env["dram"], env["keep"]
    ident, xT = keep["ident"], keep["xT"]
    XR = 3
    CH = [(CONV, 512), (CONV + 512, 512), (CONV + 1024, 16)]
    with ExitStack() as ctx:
        def sb(name, shape, dt=F32):
            return ctx.enter_context(nc.sbuf_tensor(name, shape, dt))

        def sem(name):
            return new_sem(nc, env, name)

        wz = sb("w_z", [P, KT, 1040])
        x = sb("x_dn", [P, XR, DM])
        junk = sb("junk_dn", [P, DM])
        gx = sb("gain_dn", [P, DM])
        go = sb("gain_o", [P, HD])
        th = sb("tanh_z", [P, 2, DM])
        gz = sb("gz", [P, 2, DM])
        ss = sb("ss_dn", [P, 2, 1])
        rs = sb("rs_dn", [P, 2, 1])
        mhalf = sb("mhalf_dn", [P, 1])
        ba = sb("ba", [P, NT, 16])
        al = sb("a_log", [P, H])
        dtb = sb("dt_bias", [P, H])
        t1 = sb("t1_g", [P, NT, H])
        t2 = sb("t2_g", [P, NT, H])
        tpb = ctx.enter_context(nc.psum_tensor("tp_dn", [P, 2, 4, P], F32))
        acc = ctx.enter_context(nc.psum_tensor("acc_dn", [P, 6, 512], F32))
        beta, g = keep["beta"], keep["g"]

        once = sem("dn_once")
        wz_in = [sem(f"wz_in{c}") for c in range(3)]
        x_in = [sem(f"dx_in{i}") for i in range(XR)]
        ss_ok, rs_ok, xn_ok = sem("dss_ok"), sem("drs_ok"), sem("dxn_ok")
        tp_done, tp_evac = sem("dtp_done"), sem("dtp_evac")
        mm_done, th_ok, gz_ok, ba_ok, z_rd = sem("dmm_done"), sem("dth_ok"), sem("dgz_ok"), sem("dba_ok"), sem("dz_rd")
        st = [env["stores"][f"z_out{u}"] for u in range(2)]
        pch, ach, dch = sem("pool_chain_dn"), sem("act_chain_dn"), sem("dve_chain_dn")
        ga, gb = sem("g_act"), sem("g_dve")
        block = ctx.enter_context(nc.Block())

        @block.sync
        def _(sp):
            def load(n):
                sp.dma_start(x[:, n % XR, :], d["y1_d"][n * P:(n + 1) * P, :]).then_inc(x_in[n % XR], 16)
            load(0)
            sp.dma_start(gx[:], d["dn_norm"][0:1, :].partition_broadcast(P)).then_inc(once, 16)
            sp.dma_start(go[:], d["dn_o_gain"][0:1, :].partition_broadcast(P)).then_inc(once, 16)
            sp.dma_start(al[:], d["dn_A_log"][0:1, :].partition_broadcast(P)).then_inc(once, 16)
            sp.dma_start(dtb[:], d["dn_dt_bias"][0:1, :].partition_broadcast(P)).then_inc(once, 16)
            load(1)
            for c, (a, w) in enumerate(CH):
                sp.dma_start(wz[:, :, a - CONV:a - CONV + w],
                             d["dn_w_in"].rearrange("l (k p) n -> p (l k) n", p=P)[:, :, a:a + w]).then_inc(wz_in[c], 16)
            load(2)
            for n in range(NT):
                if n + XR < NT:
                    sp.wait_ge(tp_done, 2 * (n + 1))
                    load(n + XR)
                sp.wait_ge(gz_ok, n + 1)
                sp.dma_start(d["z_d"][n * P:(n + 1) * P, :], gz[:, n % 2, :]).then_inc(st[n % 2], 16)
            sp.wait_ge(st[0], 16 * 5)
            sp.wait_ge(st[1], 16 * 4)

        @block.gpsimd
        def _(pool):
            link = chain(pool, pch)
            link(pool.memset(mhalf[:], -0.5))

            def rms(n):
                pool.wait_ge(ss_ok, n + 1)
                link(pool.tensor_scalar(ss[:, n % 2, :], ss[:, n % 2, :], 1.0 / DM, EPS, ALU.mult, ALU.add))
                pool.tensor_tensor(rs[:, n % 2, :], ss[:, n % 2, :], mhalf[:], ALU.pow).then_inc(rs_ok, 1)

            rms(0)
            rms(1)
            pool.wait_ge(once, 64)
            link(pool.tensor_scalar(go[:], go[:], 0.5, None, ALU.mult))
            for n in range(NT):
                if n + 2 < NT:
                    rms(n + 2)
                pool.wait_ge(z_rd, n + 1)
                if n >= 2:
                    pool.wait_ge(st[n % 2], 16 * (n // 2))
                pool.tensor_tensor(gz[:, n % 2, :].rearrange("p (h e) -> p h e", h=H), th[:, n % 2, :].rearrange("p (h e) -> p h e", h=H),
                                   go[:].unsqueeze(1).broadcast_to([P, H, HD]), ALU.mult).then_inc(gz_ok, 1)

        @block.tensor
        def _(pe):
            def turn(n):
                pe.wait_ge(xn_ok, n + 1)
                for u in range(2):
                    if n >= 1:
                        pe.wait_ge(tp_evac, 2 * n - 1 + u)
                    for j in range(4):
                        ins = pe.transpose(tpb[:, u, j, :], x[:, n % XR, (4 * u + j) * P:(4 * u + j + 1) * P], ident[:])
                    ins.then_inc(tp_done, 1)
            turn(0)
            for n in range(NT):
                if n + 1 < NT:
                    turn(n + 1)
                pe.wait_ge(tp_evac, 2 * n + 2)
                for c, (a, w) in enumerate(CH):
                    if n == 0:
                        pe.wait_ge(wz_in[c], 16)
                    if n >= 2:
                        pe.wait_ge(z_rd if c < 2 else ba_ok, n - 1)
                    for k in range(KT):
                        ins = pe.matmul(acc[:, 3 * (n % 2) + c, 0:w], xT[:, k, n * P:(n + 1) * P], wz[:, k, a - CONV:a - CONV + w],
                                        start=(k == 0), stop=(k == KT - 1))
                    ins.then_inc(mm_done, 1)

        @block.scalar
        def _(act):
            def square(n):
                act.wait_ge(x_in[n % XR], 16 * (n // XR + 1))
                if n >= 2:
                    act.wait_ge(rs_ok, n - 1)
                if n >= 1:
                    act.wait_ge(ss_ok, n)
                act.activation(junk[:], x[:, n % XR, :], ACT.Square, accum_out=ss[:, n % 2, :]).then_inc(ss_ok, 1)

            def evac(n):
                for u in range(2):
                    act.wait_ge(tp_done, 2 * n + u + 1)
                    act.copy(xT[:, 4 * u:4 * u + 4, n * P:(n + 1) * P], tpb[:, u, :, :]).then_inc(tp_evac, 1)
            square(0)
            square(1)
            evac(0)
            for n in range(NT):
                if n + 1 < NT:
                    evac(n + 1)
                if n + 2 < NT:
                    square(n + 2)
                if n >= 2:
                    act.wait_ge(gz_ok, n - 1)
                for c in range(2):
                    act.wait_ge(mm_done, 3 * n + c + 1)
                    act.activation(th[:, n % 2, c * 512:(c + 1) * 512], acc[:, 3 * (n % 2) + c, :], ACT.Tanh, scale=0.5).then_inc(th_ok, 1)
                act.wait_ge(mm_done, 3 * n + 3)
                act.copy(ba[:, n, :], acc[:, 3 * (n % 2) + 2, 0:16]).then_inc(ba_ok, 1)
            act.wait_ge(gb, 1)
            act.activation(beta[:], ba[:, :, 0:H], ACT.Exp, scale=-1.0).then_inc(ga, 1)
            act.activation(al[:], al[:], ACT.Exp)
            act.activation(t2[:], t2[:], ACT.Exp, scale=-1.0).then_inc(ach, 1)
            act.wait_ge(ach, 1)
            act.activation(t2[:], t2[:], ACT.Ln, bias=1.0).then_inc(ga, 1)

        @block.vector
        def _(dve):
            link = chain(dve, dch)

            def norm(n):
                dve.wait_ge(rs_ok, n + 1)
                dve.scalar_tensor_tensor(x[:, n % XR, :], x[:, n % XR, :], rs[:, n % 2, :], gx[:], ALU.mult, ALU.mult).then_inc(xn_ok, 1)
            dve.wait_ge(once, 64)
            norm(0)
            norm(1)
            for n in range(NT):
                if n + 2 < NT:
                    norm(n + 2)
                dve.wait_ge(th_ok, 2 * n + 2)
                for c in range(2):
                    v = th[:, n % 2, c * 512:(c + 1) * 512]
                    ins = dve.scalar_tensor_tensor(v, v, 1.0, acc[:, 3 * (n % 2) + c, :], ALU.add, ALU.mult)
                ins.then_inc(z_rd, 1)
            dve.wait_ge(ba_ok, NT)
            link(dve.tensor_tensor(t1[:], ba[:, :, H:], dtb[:].unsqueeze(1).broadcast_to([P, NT, H]), ALU.add))
            dve.scalar_tensor_tensor(t2[:], t1[:], -1.0, t1[:], ALU.mult, ALU.max).then_inc(gb, 1)
            dve.wait_ge(ga, 1)
            link(dve.tensor_scalar(beta[:], beta[:], 1.0, None, ALU.add))
            link(dve.reciprocal(beta[:], beta[:]))
            dve.wait_ge(ga, 2)
            link(dve.scalar_tensor_tensor(t1[:], t1[:], 0.0, t2[:], ALU.max, ALU.add))
            link(dve.scalar_tensor_tensor(g[:], t1[:], -1.0, al[:].unsqueeze(1).broadcast_to([P, NT, H]), ALU.mult, ALU.mult))


def dn_conv(nc, env):
    d, keep = env["dram"], env["keep"]
    ident, xT = keep["ident"], keep["xT"]
    NCH = CONV // P
    CW = ROWS // 3
    NB3 = DB * (CW_TAPS - 1)
    WR = 3
    YR = 6
    with ExitStack() as ctx:
        def sb(name, shape, dt=F32):
            return ctx.enter_context(nc.sbuf_tensor(name, shape, dt))

        def sem(name):
            return new_sem(nc, env, name)

        w = sb("w_ch", [P, WR, KT, P])
        cw_n = sb("conv_w_nat", [4 * NCH, P])
        cw = sb("conv_w", [P, 4 * NCH])
        cb_n = sb("conv_buf_nat", [NB3, CONV])
        xp = sb("x_pad", [P, 2, 3 + SEQ])
        xs = sb("x_pad_s", [P, 2, DB, 3 + DS])
        tail = sb("tail", [P, 2, 27])
        nb = sb("new_buf", [27, CONV])
        y = sb("y_ch", [P, YR, ROWS])
        th = sb("th_ch", [P, ROWS])
        sq = sb("sq_ch", [P, 2, ROWS])
        rn = sb("rn_ch", [P, 2, ROWS])
        ones = sb("ones_ch", [P, P])
        nw = sb("newton", [P, ROWS])
        ssx = sb("ss_eps", [P, ROWS])
        epsc = sb("eps_ch", [P, 1])
        acc = ctx.enter_context(nc.psum_tensor("acc_ch", [P, 3, 512], F32))
        sps = ctx.enter_context(nc.psum_tensor("ss_ch", [P, 3, 512], F32))
        tps = ctx.enter_context(nc.psum_tensor("tp_ch", [P, 2, 512], F32))

        once = sem("ch_once")
        w_in = [sem(f"w_ch_in{i}") for i in range(WR)]
        cw_t, cw_ok, zero_ok = sem("cw_t"), sem("cw_ok"), sem("zero_ok")
        mm, buf_t, x_ok, buf_ok, tail_ok, tail_t, nb_ok = (sem("ch_" + s) for s in ("mm", "buf_t", "x_ok", "buf_ok", "tail_ok", "tail_t", "nb_ok"))
        conv_ok, th_ok, silu_ok, sq_ok, ss_done, ssc_ok, rn_ok, out_ok = (
            sem("ch_" + s) for s in ("conv_ok", "th_ok", "silu_ok", "sq_ok", "ss_done", "ssc_ok", "rn_ok", "out_ok"))
        st = [env["stores"][f"qkv_out{u}"] for u in range(YR)]
        nb_out = env["stores"]["nb_out"]
        dch, pch, act_ch = sem("dve_chain_ch"), sem("pool_chain_ch"), sem("act_chain_ch")
        block = ctx.enter_context(nc.Block())

        @block.sync
        def _(sp):
            wv = d["dn_w_in"].rearrange("l (k p) n -> p (l k) n", p=P)

            def load(c):
                if c >= WR:
                    sp.wait_ge(mm, 3 * (c - WR + 1))
                sp.dma_start(w[:, c % WR, :, :], wv[:, :, c * P:(c + 1) * P]).then_inc(w_in[c % WR], 16)
            load(0)
            sp.dma_start(cw_n[:], d["dn_conv_w"].rearrange("l i (n p) -> (l i n) p", p=P)).then_inc(once, 16)
            sp.dma_start(cb_n[:], d["state_dn_conv"].rearrange("b l i n -> (b l i) n")).then_inc(once, 16)
            load(1)
            load(2)

            def store(c):
                sp.wait_ge(*((out_ok, c + 1) if c < 2 * H else (silu_ok, c + 1)))
                sp.dma_start(d["qkv_d"][c], y[:, c % YR, :]).then_inc(st[c % YR], 16)
            for c in range(NCH):
                if c + WR < NCH:
                    load(c + WR)
                if c >= 3:
                    store(c - 3)
            for c in range(NCH - 3, NCH):
                store(c)
            sp.wait_ge(nb_ok, NCH)
            sp.dma_start(d["newbuf_s"], nb[0:NB3, :]).then_inc(nb_out, 16)
            sp.dma_start(d["newbuf_p"], nb[NB3:27, :]).then_inc(nb_out, 16)
            sp.wait_ge(nb_out, 32)
            for s in st:
                sp.wait_ge(s, 16 * NCH // YR)

        @block.tensor
        def _(pe):
            pe.wait_ge(once, 32)
            pe.transpose(tps[:, 0, 0:4 * NCH], cw_n[:], ident[0:4 * NCH, 0:4 * NCH]).then_inc(cw_t, 1)
            pe.wait_ge(cw_ok, 1)

            def project(c):
                pe.wait_ge(w_in[c % WR], 16 * (c // WR + 1))
                for j in range(3):
                    if c >= 1:
                        pe.wait_ge(x_ok, 3 * (c - 1) + j + 1)
                    for k in range(KT):
                        ins = pe.matmul(acc[:, j, 0:CW], w[:, c % WR, k, :], xT[:, k, j * CW:(j + 1) * CW],
                                        start=(k == 0), stop=(k == KT - 1))
                    ins.then_inc(mm, 1)
                if c >= 1:
                    pe.wait_ge(buf_ok, c)
                pe.transpose(tps[:, 0, 0:NB3], cb_n[:, c * P:(c + 1) * P], ident[0:NB3, 0:NB3]).then_inc(buf_t, 1)

            def after(c):
                pe.wait_ge(tail_ok, c + 1)
                if c >= 1:
                    pe.wait_ge(nb_ok, c)
                pe.transpose(tps[0:27, 1, 0:P], tail[:, c % 2, :], ident[:]).then_inc(tail_t, 1)
                if c < 2 * H:
                    pe.wait_ge(sq_ok, c + 1)
                    if c >= 1:
                        pe.wait_ge(ssc_ok, c)
                    for j in range(3):
                        ins = pe.matmul(sps[:, j, 0:CW], ones[:], sq[:, c % 2, j * CW:(j + 1) * CW], start=True, stop=True)
                    ins.then_inc(ss_done, 1)
            for c in range(NCH):
                project(c)
                if c >= 2:
                    after(c - 2)
            after(NCH - 2)
            after(NCH - 1)

        @block.scalar
        def _(act):
            def take(c):
                act.wait_ge(mm, 3 * c + 1)
                if c >= 2:
                    act.wait_ge(conv_ok, c - 1)
                    act.wait_ge(tail_ok, c - 1)
                act.wait_ge(zero_ok, 1)
                act.copy(xs[:, c % 2, :, 3:], acc[:, 0, 0:NS].rearrange("p (b t) -> p b t", b=DB))
                act.copy(xp[:, c % 2, 3:3 + CW - P], acc[:, 0, P:CW]).then_inc(x_ok, 1)
                for j in (1, 2):
                    a = 3 + j * CW - P
                    act.wait_ge(mm, 3 * c + j + 1)
                    act.copy(xp[:, c % 2, a:a + CW], acc[:, j, 0:CW]).then_inc(x_ok, 1)
                act.wait_ge(buf_t, c + 1)
                act.copy(xs[:, c % 2, :, 0:3], tps[:, 0, 0:NB3].rearrange("p (b i) -> p b i", b=DB)).then_inc(buf_ok, 1)

            def gate(c):
                act.wait_ge(conv_ok, c + 1)
                if c >= 1:
                    act.wait_ge(silu_ok, c)
                act.activation(th[:], y[:, c % YR, :], ACT.Tanh).then_inc(th_ok, 1)

            def squares(c):
                if c < 2 * H:
                    act.wait_ge(silu_ok, c + 1)
                    if c >= 2:
                        act.wait_ge(ss_done, c - 1)
                    act.activation(sq[:, c % 2, :], y[:, c % YR, :], ACT.Square).then_inc(sq_ok, 1)

            def new_rows(c):
                act.wait_ge(tail_t, c + 1)
                act.copy(nb[:, c * P:(c + 1) * P], tps[0:27, 1, 0:P]).then_inc(nb_ok, 1)

            def root(c):
                act.wait_ge(ss_done, c + 1)
                if c >= 1:
                    act.wait_ge(rn_ok, c)
                if c >= 2:
                    act.wait_ge(out_ok, c - 1)
                for j in range(3):
                    act.activation(ssx[:, j * CW:(j + 1) * CW], sps[:, j, 0:CW], ACT.Identity, bias=epsc[:])
                    ins = act.activation(rn[:, c % 2, j * CW:(j + 1) * CW], sps[:, j, 0:CW], ACT.Ln, bias=epsc[:])
                ins.then_inc(act_ch, 1)
                act.wait_ge(act_ch, c + 1)
                act.activation(rn[:, c % 2, :], rn[:, c % 2, :], ACT.Exp, scale=-0.5).then_inc(ssc_ok, 1)
            take(0)
            for c in range(NCH):
                gate(c)
                if 2 <= c < 2 * H + 2:
                    root(c - 2)
                if c >= 2:
                    new_rows(c - 2)
                squares(c)
                if c + 1 < NCH:
                    take(c + 1)
            new_rows(NCH - 2)
            new_rows(NCH - 1)

        @block.gpsimd
        def _(pool):
            link = chain(pool, pch)
            pool.memset(epsc[:], EPS)
            pool.memset(ones[:], 1.0)
            pool.memset(y[:], 0.0)
            link(pool.memset(xp[:], 0.0))
            pool.memset(xs[:], 0.0).then_inc(zero_ok, 1)
            for c in range(NCH):
                pool.wait_ge(x_ok, 3 * (c + 1))
                if c >= 2:
                    pool.wait_ge(tail_t, c - 1)
                pool.tensor_copy(tail[:, c % 2, 0:NB3].rearrange("p (b i) -> p b i", b=DB), xs[:, c % 2, :, DS:])
                pool.tensor_copy(tail[:, c % 2, NB3:], xp[:, c % 2, SEQ:]).then_inc(tail_ok, 1)
                if 2 <= c < 2 * H + 2:
                    pool.wait_ge(ssc_ok, c - 1)
                    r = rn[:, c % 2, :]
                    link(pool.tensor_tensor(nw[:], r, r, ALU.mult))
                    link(pool.tensor_tensor(nw[:], nw[:], ssx[:], ALU.mult))
                    s = HD ** -0.5 if c - 2 < H else 1.0
                    link(pool.tensor_scalar(nw[:], nw[:], -0.5 * s, 1.5 * s, ALU.mult, ALU.add))
                    pool.tensor_tensor(r, r, nw[:], ALU.mult).then_inc(rn_ok, 1)

        @block.vector
        def _(dve):
            link = chain(dve, dch)
            dve.wait_ge(cw_t, 1)
            dve.tensor_scalar(cw[:], tps[:, 0, 0:4 * NCH], 0.5, None, ALU.mult).then_inc(cw_ok, 1)
            dve.wait_ge(cw_ok, 1)
            dve.wait_ge(zero_ok, 1)

            def conv(c):
                dve.wait_ge(x_ok, 3 * (c + 1))
                dve.wait_ge(buf_ok, c + 1)
                if c >= YR:
                    dve.wait_ge(st[c % YR], 16 * (c // YR))
                ys = y[:, c % YR, 0:NS].rearrange("p (b t) -> p b t", b=DB)
                yp = y[:, c % YR, P:]
                for i in range(4):
                    tap = cw[:, i * NCH + c:i * NCH + c + 1]
                    for out, src in ((ys, xs[:, c % 2, :, i:i + DS]), (yp, xp[:, c % 2, i:i + SEQ])):
                        if i == 0:
                            ins = dve.tensor_scalar(out, src, tap, None, ALU.mult)
                        else:
                            ins = dve.scalar_tensor_tensor(out, src, tap, out, ALU.mult, ALU.add)
                    if i < 3:
                        link(ins)
                ins.then_inc(conv_ok, 1)

            def gated(c):
                yv = y[:, c % YR, :]
                dve.wait_ge(th_ok, c + 1)
                dve.scalar_tensor_tensor(yv, th[:], 1.0, yv, ALU.add, ALU.mult).then_inc(silu_ok, 1)

            def scaled(c):
                yv = y[:, c % YR, :]
                dve.wait_ge(sq_ok, c + 1)
                dve.wait_ge(rn_ok, c + 1)
                dve.tensor_tensor(yv, yv, rn[:, c % 2, :], ALU.mult).then_inc(out_ok, 1)
            conv(0)
            for c in range(NCH):
                gated(c)
                if 3 <= c < 2 * H + 3:
                    scaled(c - 3)
                if c + 1 < NCH:
                    conv(c + 1)


def dn_scan(nc, env):
    d, keep = env["dram"], env["keep"]
    ident, beta, g = keep["ident"], keep["beta"], keep["g"]
    HG = H // 2
    with ExitStack() as ctx:
        def sb(name, shape, dt=F32):
            return ctx.enter_context(nc.sbuf_tensor(name, shape, dt))

        def sem(name):
            return new_sem(nc, env, "sc_" + name)

        wo = sb("w_out_dn", [P, H, DM])
        S = sb("S_p", [P, H, HD])
        Ss = sb("S_s", [P, DB, H, HD])
        qkv = sb("qkv_t", [P, 2, 3 * H, P])
        gz = sb("gz_t", [P, 2, DM])
        y = sb("y_t", [P, 2, DM])
        tri = sb("tri", [P, 2, P])
        blk = sb("blk", [P, 2, P])
        m1c = sb("m1c", [P, 2, P])
        m2c = sb("m2c", [P, 2, P])
        lev = sb("lev", [P, 7, P])
        bsel = sb("bsel", [P, DB])
        gsel = sb("gsel", [P, DB, H])
        eglS = sb("eglS", [P, DB, H])
        tg = sb("tri_g", [P, H, P])
        dec = sb("decay", [P, H, P])
        qk = sb("qk_decay", [P, 2, H, P])
        A = dec
        L = sb("L", [P, 2, H, P])
        T = sb("T", [P, H, P])
        TT = sb("TT", [P, 2, H, P])
        Y = sb("Y", [P, H, P])
        bv = sb("beta_v", [P, 2, H, P])
        kd = sb("k_decay", [P, 2, H, P])
        gcl = sb("gcl", [P, 2, 2, H])
        ngc = sb("ngc", [P, 2, H])
        ex = sb("exps", [P, 2, 3, H])
        nbe = sb("nbe", [P, 2, H])
        rhs = sb("rhs", [P, H, HD])
        qs = sb("qS_s", [P, H, HD])
        u = sb("u", [P, H, HD])
        o = sb("o_t", [P, H, HD])
        sqo = rhs
        sso = sb("ss_o", [P, H])
        rso = sb("rs_o", [P, H])
        mhalf = sb("mhalf_o", [P, H])
        ogT = sb("ogT_dn", [P, H, P])
        mgc = sb("minus_gc", [P, 2, H])
        xsb = sb("xS_s", [P, H, 2, NS])
        kdm = sb("k_masked", [P, 2, H, P])
        PA = ctx.enter_context(nc.psum_tensor("PA", [P, 4, 512], F32))
        PB = ctx.enter_context(nc.psum_tensor("PB", [P, 4, 512], F32))

        once, s_in = sem("once"), sem("s_in")
        in_ = [sem("in0"), sem("in1")]
        gz_in, y_in = [sem("gz_in0"), sem("gz_in1")], [sem("y_in0"), sem("y_in1")]
        fa, fb = sem("PA_filled"), sem("PB_filled")
        a_dve, a_act = sem("PA_read_dve"), sem("PA_read_act")
        b_dve, b_act = sem("PB_read_dve"), sem("PB_read_act")
        gvec_ok, ex_ok, tg_ok, ed_ok, L_ok, T1_ok = (sem(s) for s in ("gvec_ok", "ex_ok", "tg_ok", "ed_ok", "L_ok", "T1_ok"))
        sq_ok, ssr_ok, rso_ok, og_ok, kdm_ok, gsel_ok, s_zero = (
            sem(s) for s in ("sq_ok", "ssr_ok", "rso_ok", "og_ok", "kdm_ok", "gsel_ok", "s_zero"))
        st = [env["stores"][f"y2_out{u}"] for u in range(2)]
        s_out = env["stores"]["s_out"]
        dch, pch = sem("dve_chain"), sem("pool_chain")

        def levels(n):
            return 3 if n == 0 else 7

        ua, ub, lbase = [], [], {}
        for n in range(NT):
            ua.append((("gc", n), a_dve))
            if n == 0:
                ua.append((("gs", n), a_act))
            for r in range(2):
                ua += [(("R", n, r), a_dve), (("vt", n, r), a_act), (("kt", n, r), a_act), (("kk", n, r), a_dve), (("qk", n, r), a_dve)]
            ua += [(("L1", n, r), a_dve) for r in range(2)]
            for l in range(1, levels(n)):
                ua += [(("Y", n, l, r), a_act) for r in range(2)]
                for r in range(2):
                    ua.append((("dTT", n, l, r), a_dve))
                    if l < levels(n) - 1:
                        ua.append((("dT", n, l, r), a_dve))
            if n == 0:
                ub += [(("XS", n, r), b_dve) for r in range(2)]
            for r in range(2):
                ub += [(("kS", n, r), b_dve), (("qS", n, r), b_act)]
            ub += [(("u", n, r), b_act) for r in range(2)]
            ub += [(("oi", n, r), b_dve) for r in range(2)]
            if n == 0:
                ub += [(("Sn", n, b, r), b_dve) for b in range(DB) for r in range(2)]
            else:
                ub += [(("Sn", n, r), b_dve) for r in range(2)]
            ub += [(("oT", n, r), b_act) for r in range(2)] + [(("y", n, r), b_dve) for r in range(2)]
            lbase[n] = sum(levels(m) for m in range(n))
        ra, rb = Ring(4, ua), Ring(4, ub)

        def a4(key):
            return PA[:, ra.slot(key), :].rearrange("p (h e) -> p h e", h=HG)

        def b4(key):
            return PB[:, rb.slot(key), :].rearrange("p (h e) -> p h e", h=HG)

        def hs(r):
            return slice(HG * r, HG * r + HG)

        def kind(n):
            return 0 if n == 0 else 1

        def in_turn(prep, first, level, read_state, solve, update, norm, gated, turned, output):
            prep(0)
            first(0)
            for l in range(1, levels(0)):
                level(0, l)
            for n in range(NT):
                more = n + 1 < NT
                if more:
                    prep(n + 1)
                read_state(n)
                if more:
                    first(n + 1)
                    level(n + 1, 1)
                solve(n)
                if more:
                    level(n + 1, 2)
                update(n)
                if more:
                    level(n + 1, 3)
                norm(n)
                if more:
                    level(n + 1, 4)
                gated(n)
                if more:
                    level(n + 1, 5)
                turned(n)
                if more:
                    level(n + 1, 6)
                output(n)

        def nothing(n):
            pass
        block = ctx.enter_context(nc.Block())

        @block.sync
        def _(sp):
            def load_qkv(n):
                sp.dma_start(qkv[:, n % 2, :, :], d["qkv_d"][:, :, n * P:(n + 1) * P].rearrange("c e t -> e c t")).then_inc(in_[n % 2], 16)

            def load_gz(n):
                sp.dma_start(gz[:, n % 2, :], d["z_d"][n * P:(n + 1) * P, :]).then_inc(gz_in[n % 2], 16)

            def load_y(n):
                sp.dma_start(y[:, n % 2, :], d["y1_d"][n * P:(n + 1) * P, :]).then_inc(y_in[n % 2], 16)
            load_qkv(0)
            for t, name in ((tri, "c_tri"), (blk, "c_blk"), (m1c, "c_m1"), (m2c, "c_m2"), (lev, "c_lev")):
                sp.dma_start(t[:].rearrange("p a b -> p (a b)"), d[name]).then_inc(once, 16)
            sp.dma_start(bsel[:], d["c_bsel"]).then_inc(once, 16)
            sp.dma_start(Ss[:].rearrange("p b h v -> p (b h) v"), d["state_dn_S"].rearrange("b l h e v -> e (b l h) v")).then_inc(s_in, 16)
            load_qkv(1)
            sp.dma_start(wo[:], d["dn_w_out"].rearrange("l (h p) n -> p (l h) n", p=P)).then_inc(s_in, 16)
            for n in range(2):
                load_gz(n)
                load_y(n)
            for n in range(NT):
                p = n % 2
                if n + 2 < NT:
                    sp.wait_ge(fb, rb.filled(("qS", n, 1)))
                    load_qkv(n + 2)
                    sp.wait_ge(og_ok, n + 1)
                    load_gz(n + 2)
                sp.wait_ge(b_dve, rb.turn["y", n, 1])
                sp.dma_start(d["y_all"][n * P:(n + 1) * P, :], y[:, p, :]).then_inc(st[p], 16)
                if n == 0:
                    sp.wait_ge(b_dve, rb.turn["Sn", 0, DB - 1, 1])
                    sp.dma_start(d["S_s"].rearrange("b h e v -> e (b h) v"), Ss[:].rearrange("p b h v -> p (b h) v")).then_inc(s_out, 16)
                if n + 2 < NT:
                    sp.wait_ge(st[p], 16 * (n // 2 + 1))
                    load_y(n + 2)
            sp.dma_start(d["S_p"].rearrange("h e v -> e h v"), S[:]).then_inc(s_out, 16)
            sp.wait_ge(s_out, 32)
            sp.wait_ge(st[0], 16 * 5)
            sp.wait_ge(st[1], 16 * 4)

        @block.tensor
        def _(pe):
            def prep(n):
                p, k = n % 2, kind(n)
                c = ra.claim(pe, ("gc", n))
                if n == 0:
                    pe.wait_ge(once, 96)
                pe.matmul(PA[:, c, 0:H], tri[:, k, :], g[:, n, :], start=True, stop=True)
                pe.matmul(PA[:, c, H:2 * H], blk[:, k, :], g[:, n, :], start=True, stop=True).then_inc(fa, 1)
                if n == 0:
                    pe.wait_ge(gsel_ok, 1)
                    c = ra.claim(pe, ("gs", n))
                    pe.matmul(PA[:, c, 0:NS], blk[:, 1, :], gsel[:].rearrange("p b h -> p (b h)"), start=True, stop=True).then_inc(fa, 1)
                pe.wait_ge(in_[p], 16 * (n // 2 + 1))
                for r in range(2):
                    c = ra.claim(pe, ("R", n, r))
                    pe.wait_ge(tg_ok, n + 1)
                    pe.matmul(PA[:, c, :], blk[:, 1, :], tg[:, hs(r), :].rearrange("p h e -> p (h e)"), start=True, stop=True).then_inc(fa, 1)
                    for what, off in (("vt", 2 * H), ("kt", H)):
                        ra.claim(pe, (what, n, r))
                        for h in range(HG):
                            ins = pe.transpose(a4((what, n, r))[:, h, :], qkv[:, p, off + HG * r + h, :], ident[:])
                        ins.then_inc(fa, 1)
                    for what, off in (("kk", H), ("qk", 0)):
                        ra.claim(pe, (what, n, r))
                        for h in range(HG):
                            hh = HG * r + h
                            ins = pe.matmul(a4((what, n, r))[:, h, :], qkv[:, p, H + hh, :], qkv[:, p, off + hh, :], start=True, stop=True)
                        ins.then_inc(fa, 1)

            def first(n):
                for r in range(2):
                    ra.claim(pe, ("L1", n, r))
                    pe.wait_ge(L_ok, lbase[n] + 1)
                    for h in range(HG):
                        ins = pe.transpose(a4(("L1", n, r))[:, h, :], L[:, lbase[n] % 2, HG * r + h, :], ident[:])
                    ins.then_inc(fa, 1)

            def level(n, l):
                p = n % 2
                last = l == levels(n) - 1
                for r in range(2):
                    ra.claim(pe, ("Y", n, l, r))
                    pe.wait_ge(L_ok, lbase[n] + l + 1)
                    pe.wait_ge(a_dve, ra.turn["L1", n, r] if l == 1 else ra.turn["dTT", n, l - 1, r])
                    for h in range(HG):
                        hh = HG * r + h
                        ins = pe.matmul(a4(("Y", n, l, r))[:, h, :], L[:, (lbase[n] + l) % 2, hh, :], TT[:, p, hh, :], start=True, stop=True)
                    ins.then_inc(fa, 1)
                for r in range(2):
                    pe.wait_ge(a_act, ra.turn["Y", n, l, r])
                    pe.wait_ge(*((T1_ok, n + 1) if l == 1 else (a_dve, ra.turn["dT", n, l - 1, r])))
                    ra.claim(pe, ("dTT", n, l, r))
                    for h in range(HG):
                        hh = HG * r + h
                        ins = pe.matmul(a4(("dTT", n, l, r))[:, h, :], T[:, hh, :], Y[:, hh, :], start=True, stop=True)
                    ins.then_inc(fa, 1)
                    if not last:
                        ra.claim(pe, ("dT", n, l, r))
                        for h in range(HG):
                            hh = HG * r + h
                            ins = pe.matmul(a4(("dT", n, l, r))[:, h, :], Y[:, hh, :], T[:, hh, :], start=True, stop=True)
                        ins.then_inc(fa, 1)

            def read_state(n):
                p = n % 2
                if n == 0:
                    pe.wait_ge(s_in, 32)
                    for r in range(2):
                        c = rb.claim(pe, ("XS", n, r))
                        for h in range(HG):
                            for b in range(DB):
                                hh = HG * r + h
                                out = PB[:, c, h * P:(h + 1) * P].rearrange("p (w t) -> p w t", w=2)[:, :, b * DS:(b + 1) * DS]
                                src = qkv[:, p, hh:hh + H + 1:H, b * DS:(b + 1) * DS]
                                ins = pe.matmul(out, Ss[:, b, hh, :], src, start=True, stop=True)
                        ins.then_inc(fb, 1)
                for r in range(2):
                    for what, w in (("kS", 1), ("qS", 0)):
                        rb.claim(pe, (what, n, r))
                        if n == 0:
                            pe.wait_ge(b_dve, rb.turn["XS", n, r])
                        elif n == 1:
                            pe.wait_ge(s_zero, 1)
                        else:
                            pe.wait_ge(b_dve, rb.turn["Sn", n - 1, r])
                        for h in range(HG):
                            hh = HG * r + h
                            if n == 0:
                                ins = pe.transpose(b4((what, n, r))[0:NS, h, :], xsb[:, hh, w, :], ident[:])
                            else:
                                ins = pe.matmul(b4((what, n, r))[:, h, :], qkv[:, p, H * w + hh, :], S[:, hh, :], start=True, stop=True)
                        ins.then_inc(fb, 1)

            def solve(n):
                p = n % 2
                for r in range(2):
                    rb.claim(pe, ("u", n, r))
                    pe.wait_ge(b_dve, rb.turn["kS", n, r])
                    pe.wait_ge(a_dve, ra.turn["dTT", n, levels(n) - 1, r])
                    for h in range(HG):
                        hh = HG * r + h
                        ins = pe.matmul(b4(("u", n, r))[:, h, :], TT[:, p, hh, :], rhs[:, hh, :], start=True, stop=True)
                    ins.then_inc(fb, 1)

            def update(n):
                p = n % 2
                for r in range(2):
                    rb.claim(pe, ("oi", n, r))
                    pe.wait_ge(b_act, rb.turn["u", n, r])
                    pe.wait_ge(a_dve, ra.turn["qk", n, r])
                    for h in range(HG):
                        hh = HG * r + h
                        ins = pe.matmul(b4(("oi", n, r))[:, h, :], qk[:, p, hh, :], u[:, hh, :], start=True, stop=True)
                    ins.then_inc(fb, 1)
                pe.wait_ge(a_act, ra.turn["kt", n, 1])
                if n == 0:
                    for b in range(DB):
                        pe.wait_ge(kdm_ok, b + 1)
                        for r in range(2):
                            rb.claim(pe, ("Sn", n, b, r))
                            for h in range(HG):
                                hh = HG * r + h
                                ins = pe.matmul(b4(("Sn", n, b, r))[:, h, :], kdm[:, b % 2, hh, :], u[:, hh, :], start=True, stop=True)
                            ins.then_inc(fb, 1)
                else:
                    for r in range(2):
                        rb.claim(pe, ("Sn", n, r))
                        for h in range(HG):
                            hh = HG * r + h
                            ins = pe.matmul(b4(("Sn", n, r))[:, h, :], kd[:, p, hh, :], u[:, hh, :], start=True, stop=True)
                        ins.then_inc(fb, 1)

            def turned(n):
                for r in range(2):
                    rb.claim(pe, ("oT", n, r))
                    pe.wait_ge(og_ok, n + 1)
                    for h in range(HG):
                        ins = pe.transpose(b4(("oT", n, r))[:, h, :], o[:, HG * r + h, :], ident[:])
                    ins.then_inc(fb, 1)

            def output(n):
                for r in range(2):
                    c = rb.claim(pe, ("y", n, r))
                    pe.wait_ge(b_act, rb.turn["oT", n, 1])
                    for h in range(H):
                        ins = pe.matmul(PB[:, c, :], ogT[:, h, :], wo[:, h, r * 512:(r + 1) * 512], start=(h == 0), stop=(h == H - 1))
                    ins.then_inc(fb, 1)
            in_turn(prep, first, level, read_state, solve, update, nothing, nothing, turned, output)

        @block.scalar
        def _(act):
            def prep(n):
                p = n % 2
                if n == 0:
                    act.wait_ge(fa, ra.filled(("gs", n)))
                    act.activation(eglS[:].rearrange("p b h -> p (b h)"), PA[:, ra.slot(("gs", n)), 0:NS], ACT.Exp).then_inc(a_act, 1)
                act.wait_ge(gvec_ok, n + 1)
                act.activation(ex[:, p, 0, :], gcl[:, p, 0, :], ACT.Exp)
                act.activation(ex[:, p, 1, :], gcl[:, p, 1, :], ACT.Exp)
                act.activation(ex[:, p, 2, :], ngc[:, p, :], ACT.Exp).then_inc(ex_ok, 1)
                act.wait_ge(ex_ok, n + 1)
                for r in range(2):
                    act.wait_ge(a_dve, ra.turn["R", n, r])
                    for h in range(HG * r, HG * r + HG):
                        act.activation(dec[:, h, :], dec[:, h, :], ACT.Exp, bias=gcl[:, p, 0, h:h + 1], scale=-1.0)
                        ins = act.activation(qk[:, p, h, :], qk[:, p, h, :], ACT.Exp, bias=mgc[:, p, h:h + 1])
                    ins.then_inc(ed_ok, 1)
                    act.wait_ge(fa, ra.filled(("vt", n, r)))
                    for h in range(HG):
                        ins = act.mul(bv[:, p, HG * r + h, :], a4(("vt", n, r))[:, h, :], beta[:, n, HG * r + h:HG * r + h + 1])
                    ins.then_inc(a_act, 1)
                    act.wait_ge(fa, ra.filled(("kt", n, r)))
                    for h in range(HG):
                        ins = act.mul(kd[:, p, HG * r + h, :], a4(("kt", n, r))[:, h, :], ex[:, p, 2, HG * r + h:HG * r + h + 1])
                    ins.then_inc(a_act, 1)

            def level(n, l):
                for r in range(2):
                    act.wait_ge(fa, ra.filled(("Y", n, l, r)))
                    act.copy(Y[:, hs(r), :], a4(("Y", n, l, r))).then_inc(a_act, 1)

            def read_state(n):
                p = n % 2
                m = NS if n == 0 else P
                for r in range(2):
                    act.wait_ge(fb, rb.filled(("qS", n, r)))
                    if n >= 1:
                        act.wait_ge(b_dve, rb.turn["oi", n - 1, r])
                    for h in range(HG):
                        hh = HG * r + h
                        ins = act.mul(qs[0:m, hh, :], b4(("qS", n, r))[0:m, h, :], ex[0:m, p, 0, hh:hh + 1])
                    ins.then_inc(b_act, 1)

            def solve(n):
                for r in range(2):
                    act.wait_ge(fb, rb.filled(("u", n, r)))
                    act.copy(u[:, hs(r), :], b4(("u", n, r))).then_inc(b_act, 1)

            def update(n):
                act.wait_ge(b_dve, rb.turn["oi", n, 1])
                if n >= 1:
                    act.wait_ge(ssr_ok, n)
                act.activation(sqo[:], o[:], ACT.Square).then_inc(sq_ok, 1)

            def turned(n):
                for r in range(2):
                    act.wait_ge(fb, rb.filled(("oT", n, r)))
                    act.copy(ogT[:, hs(r), :], b4(("oT", n, r))).then_inc(b_act, 1)
            in_turn(prep, nothing, level, read_state, solve, update, nothing, nothing, turned, nothing)

        @block.gpsimd
        def _(pool):
            link = chain(pool, pch)
            pool.memset(S[:], 0.0).then_inc(s_zero, 1)
            link(pool.memset(mhalf[:], -0.5))
            pool.wait_ge(once, 96)
            pool.tensor_tensor(gsel[:], g[:, 0, :].unsqueeze(1).broadcast_to([P, DB, H]), bsel[:].unsqueeze(2).broadcast_to([P, DB, H]), ALU.mult).then_inc(gsel_ok, 1)

            def prep(n):
                if n >= 1:
                    pool.wait_ge(fa, ra.filled(("R", n - 1, 1)))
                pool.tensor_tensor(tg[:], tri[:, kind(n), :].unsqueeze(1).broadcast_to([P, H, P]),
                                   g[:, n, :].unsqueeze(2).broadcast_to([P, H, P]), ALU.mult).then_inc(tg_ok, 1)
                if n >= 1:
                    pool.wait_ge(fa, ra.filled(("dTT", n - 1, levels(n - 1) - 1, 1)))
                pool.wait_ge(a_dve, ra.turn["qk", n, 1])
                off_diagonal(n, 0)
                off_diagonal(n, 1)

            def off_diagonal(n, l):
                pool.tensor_tensor(L[:, (lbase[n] + l) % 2, :, :], A[:], lev[:, l, :].unsqueeze(1).broadcast_to([P, H, P]), ALU.mult).then_inc(L_ok, 1)

            def level(n, l):
                if l + 1 < levels(n):
                    pool.wait_ge(fa, ra.filled(("Y", n, l - 1, 1) if l > 1 else ("L1", n, 1)))
                    if l == 1:
                        pool.wait_ge(T1_ok, n + 1)
                    off_diagonal(n, l + 1)

            def solve(n):
                if n == 0:
                    pool.wait_ge(a_act, ra.turn["kt", n, 1])
                    for b in range(DB):
                        if b >= 2:
                            pool.wait_ge(fb, rb.filled(("Sn", 0, b - 2, 1)))
                        pool.tensor_scalar(kdm[:, b % 2, :, :], kd[:, 0, :, :], bsel[:, b:b + 1], None, ALU.mult).then_inc(kdm_ok, 1)

            def norm(n):
                pool.wait_ge(ssr_ok, n + 1)
                link(pool.tensor_scalar(sso[:], sso[:], 1.0 / HD, EPS, ALU.mult, ALU.add))
                pool.tensor_tensor(rso[:], sso[:], mhalf[:], ALU.pow).then_inc(rso_ok, 1)
            in_turn(prep, nothing, level, nothing, solve, nothing, norm, nothing, nothing, nothing)

        @block.vector
        def _(dve):
            link = chain(dve, dch)
            idb = ident[:].unsqueeze(1).broadcast_to([P, HG, P])

            def prep(n):
                p, k = n % 2, kind(n)
                dve.wait_ge(fa, ra.filled(("gc", n)))
                link(dve.tensor_copy(gcl[:, p, :, :].rearrange("p a b -> p (a b)"), PA[:, ra.slot(("gc", n)), 0:2 * H]))
                dve.tensor_scalar(mgc[:, p, :], gcl[:, p, 0, :], -1.0, None, ALU.mult).then_inc(a_dve, 1)
                dve.tensor_tensor(ngc[:, p, :], gcl[:, p, 1, :], gcl[:, p, 0, :], ALU.subtract).then_inc(gvec_ok, 1)
                dve.wait_ge(ex_ok, n + 1)
                dve.scalar_tensor_tensor(nbe[:, p, :], ex[:, p, 0, :], -1.0, beta[:, n, :], ALU.mult, ALU.mult)
                if n >= 1:
                    dve.wait_ge(L_ok, lbase[n])
                for r in range(2):
                    dve.wait_ge(fa, ra.filled(("R", n, r)))
                    dve.tensor_tensor(dec[:, hs(r), :], a4(("R", n, r)), m1c[:, k, :].unsqueeze(1).broadcast_to([P, HG, P]), ALU.add)
                    dve.tensor_tensor(qk[:, p, hs(r), :], a4(("R", n, r)), m2c[:, k, :].unsqueeze(1).broadcast_to([P, HG, P]), ALU.add).then_inc(a_dve, 1)
                    dve.wait_ge(fa, ra.filled(("kk", n, r)))
                    dve.wait_ge(ed_ok, 2 * n + r + 1)
                    for h in range(HG):
                        hh = HG * r + h
                        ins = dve.scalar_tensor_tensor(A[:, hh, :], a4(("kk", n, r))[:, h, :], beta[:, n, hh:hh + 1], dec[:, hh, :], ALU.mult, ALU.mult)
                    ins.then_inc(a_dve, 1)
                    dve.wait_ge(fa, ra.filled(("qk", n, r)))
                    dve.tensor_tensor(qk[:, p, hs(r), :], a4(("qk", n, r)), qk[:, p, hs(r), :], ALU.mult).then_inc(a_dve, 1)

            def first(n):
                p = n % 2
                dve.wait_ge(L_ok, lbase[n] + 1)
                for r in range(2):
                    ins = dve.tensor_tensor(T[:, hs(r), :], idb, L[:, lbase[n] % 2, hs(r), :], ALU.subtract)
                ins.then_inc(T1_ok, 1)
                for r in range(2):
                    dve.wait_ge(fa, ra.filled(("L1", n, r)))
                    dve.tensor_tensor(TT[:, p, hs(r), :], idb, a4(("L1", n, r)), ALU.subtract).then_inc(a_dve, 1)

            def level(n, l):
                p = n % 2
                for r in range(2):
                    dve.wait_ge(fa, ra.filled(("dTT", n, l, r)))
                    dve.tensor_tensor(TT[:, p, hs(r), :], TT[:, p, hs(r), :], a4(("dTT", n, l, r)), ALU.subtract).then_inc(a_dve, 1)
                    if l < levels(n) - 1:
                        dve.wait_ge(fa, ra.filled(("dT", n, l, r)))
                        dve.tensor_tensor(T[:, hs(r), :], T[:, hs(r), :], a4(("dT", n, l, r)), ALU.subtract).then_inc(a_dve, 1)

            def read_state(n):
                p = n % 2
                m = NS if n == 0 else P
                if n == 0:
                    dve.memset(rhs[NS:, :, :], 0.0)
                    link(dve.memset(qs[NS:, :, :], 0.0))
                    for r in range(2):
                        dve.wait_ge(fb, rb.filled(("XS", n, r)))
                        dve.tensor_copy(xsb[:, hs(r), :, :], PB[:, rb.slot(("XS", n, r)), :].rearrange("p (h w t) -> p h w t", h=HG, w=2)).then_inc(b_dve, 1)
                for r in range(2):
                    dve.wait_ge(fb, rb.filled(("kS", n, r)))
                    dve.wait_ge(a_act, ra.turn["vt", n, r])
                    for h in range(HG):
                        hh = HG * r + h
                        ins = dve.scalar_tensor_tensor(rhs[0:m, hh, :], b4(("kS", n, r))[0:m, h, :], nbe[0:m, p, hh:hh + 1], bv[0:m, p, hh, :], ALU.mult, ALU.add)
                    ins.then_inc(b_dve, 1)

            def update(n):
                p = n % 2
                for r in range(2):
                    dve.wait_ge(fb, rb.filled(("oi", n, r)))
                    dve.wait_ge(b_act, rb.turn["qS", n, r])
                    dve.tensor_tensor(o[:, hs(r), :], b4(("oi", n, r)), qs[:, hs(r), :], ALU.add).then_inc(b_dve, 1)
                if n == 0:
                    for b in range(DB):
                        for r in range(2):
                            dve.wait_ge(fb, rb.filled(("Sn", n, b, r)))
                            for h in range(HG):
                                hh = HG * r + h
                                ins = dve.scalar_tensor_tensor(Ss[:, b, hh, :], Ss[:, b, hh, :], eglS[:, b, hh:hh + 1], b4(("Sn", n, b, r))[:, h, :], ALU.mult, ALU.add)
                            ins.then_inc(b_dve, 1)
                else:
                    for r in range(2):
                        dve.wait_ge(fb, rb.filled(("Sn", n, r)))
                        for h in range(HG):
                            hh = HG * r + h
                            ins = dve.scalar_tensor_tensor(S[:, hh, :], S[:, hh, :], ex[:, p, 1, hh:hh + 1], b4(("Sn", n, r))[:, h, :], ALU.mult, ALU.add)
                        ins.then_inc(b_dve, 1)

            def norm(n):
                dve.wait_ge(sq_ok, n + 1)
                if n >= 1:
                    dve.wait_ge(rso_ok, n)
                dve.tensor_reduce(sso[:], sqo[:], AX.X, ALU.add).then_inc(ssr_ok, 1)

            def gated(n):
                p = n % 2
                dve.wait_ge(rso_ok, n + 1)
                dve.wait_ge(gz_in[p], 16 * (n // 2 + 1))
                for h in range(H):
                    ins = dve.scalar_tensor_tensor(o[:, h, :], o[:, h, :], rso[:, h:h + 1], gz[:, p, h * HD:(h + 1) * HD], ALU.mult, ALU.mult)
                ins.then_inc(og_ok, 1)

            def output(n):
                p = n % 2
                dve.wait_ge(y_in[p], 16 * (n // 2 + 1))
                for r in range(2):
                    dve.wait_ge(fb, rb.filled(("y", n, r)))
                    v = y[:, p, r * 512:(r + 1) * 512]
                    ins = dve.tensor_tensor(v, v, PB[:, rb.slot(("y", n, r)), :], ALU.add)
                    ins.then_inc(b_dve, 1)
            in_turn(prep, first, level, read_state, nothing, update, norm, gated, nothing, output)


def constants():
    p = np.arange(P)
    b2, h, t = p // 64, (p // 8) % 8, p % 8
    c = {"c_ident": np.eye(P)}
    col = np.arange(16)
    c["c_delta16"] = (b2[:, None] == col[None] // 8) & (t[:, None] == col[None] % 8)
    c["c_new_causal"] = np.where((p[:, None] >= 64) & (np.arange(8)[None] <= t[:, None]), 0.0, -BIG)
    c["c_e4"] = np.arange(4)[:, None] == p[None] // 32
    c["c_causal"] = np.where(p[None] <= p[:, None], 0.0, -BIG)
    c["c_j32"] = (p % 32)[:, None]
    c["c_half_off"] = ((p >= 64) * (PAST // 2))[:, None]
    e = np.zeros((NS, 4, P))
    for tt in range(4):
        for r in range(P):
            e[16 * tt + r // 8, tt, r] = 1
    c["c_expand_q"] = e.reshape(NS, 4 * P)
    q, hh = p // 8, p % 8
    n = np.arange(32)
    ok = (hh[:, None] // GRP == n[None] // 16) & (q[:, None] // 8 == (n[None] % 16) // 8)
    c["c_new_allowed"] = np.where(ok, 0.0, -BIG)
    i, j = p[:, None], p[None]
    same = [i // DS == j // DS, np.ones((P, P), bool)]

    def two(f):
        return np.stack([f(m) for m in same], 1).reshape(P, 2 * P)
    c["c_tri"] = two(lambda m: (i <= j) & m)
    c["c_blk"] = two(lambda m: m)
    c["c_m1"] = two(lambda m: np.where((j < i) & m, 0.0, BIG))
    c["c_m2"] = two(lambda m: np.where((i <= j) & m, 0.0, -BIG))
    c["c_lev"] = np.stack([(i // (2 << l) == j // (2 << l)) & (i % (2 << l) >= 1 << l) & (j % (2 << l) < 1 << l) for l in range(7)], 1).reshape(P, 7 * P)
    c["c_bsel"] = i // DS == np.arange(DB)[None]
    return {k: np.ascontiguousarray(v, dtype=np.float32) for k, v in c.items()}


def build(nc, d):
    with ExitStack() as ctx:
        def sb(name, shape, dt=F32, c=ctx):
            return c.enter_context(nc.sbuf_tensor(name, shape, dt))
        keep = {"ident": sb("ident", [P, P]), "beta": sb("beta", [P, NT, H]), "g": sb("g", [P, NT, H])}
        stores = {k: ctx.enter_context(nc.semaphore(k)) for k in (
            "st0_0", "st1_0", "st0_1", "st1_1", "iwl_out", "pa_once", "y1_out0", "y1_out1", "z_out0", "z_out1",
            "qkv_out0", "qkv_out1", "qkv_out2", "qkv_out3", "qkv_out4", "qkv_out5", "nb_out", "y2_out0", "y2_out1", "s_out")}
        env = {"dram": d, "keep": keep, "stores": stores, "sems": []}
        with ExitStack() as att:
            for name, shape, dt in (("kT", [P, G, ROWS], F32), ("v_nat", [P, NT, G * HD], F32), ("ikT", [P, ROWS], F32),
                                    ("iw_nat", [P, NT, IH], F32), ("top_v", [P, TOPK], F32), ("top_i", [P, TOPK], U32)):
                keep[name] = sb(name, shape, dt, att)
            with ExitStack() as proj:
                keep["scores"] = sb("scores", [P, PAST // 2 + DS], F32, proj)
                keep["w"] = sb("w_att", [P, KT, ATT_IN], F32, proj)
                for k, n in (("gx", DM), ("gq", HD), ("gqs", HD), ("gk", HD), ("gik", ID)):
                    keep[k] = sb(k, [P, n], F32, proj)
                att_project(nc, env, 0, 1, True, lambda dve, n: None)
                sample_scores(nc, env)
                att_project(nc, env, 1, NT - 1, False, extraction(env, new_sem(nc, env, "extract_chain")))
            for name, shape, dt in (("rowidx", [P, 2, NS], U32), ("mask_s", [P, 4, TOPK], F32),
                                    ("mask_n", [P, 4, 32], F32), ("og_s", [P, H, P], F32), ("key_mask", [P, KM[NB]], F32)):
                keep[name] = sb(name, shape, dt, att)
            sample_select(nc, env)
            sample_attend(nc, env)
            prompt_attend(nc, env)
        clear_sems(nc, env)
        with ExitStack() as dn:
            keep["xT"] = sb("xT", [P, KT, ROWS], F32, dn)
            dn_inputs(nc, env)
            dn_conv(nc, env)
        dn_scan(nc, env)


def kernel(**inputs):
    import concourse.bacc as _bacc
    from concourse.bass_utils import run_bass_kernel_spmd as _run

    nc = _bacc.Bacc("TRN2", target_bir_lowering=False, num_devices=1)
    arrays, d = {}, {}
    a = {k: np.ascontiguousarray(v) for k, v in inputs.items()}
    x_all = np.zeros((ROWS, DM), np.float32)
    x_all[0:NS] = a["x_sample"].reshape(NS, DM)
    x_all[P:] = a["x_prompt"].reshape(SEQ, DM)
    ins = {k: v for k, v in a.items() if k not in ("x_sample", "x_prompt")}
    ins["x_all"] = x_all
    ins.update(constants())
    for name, v in ins.items():
        arrays[f"in_{name}"] = v
        d[name] = nc.dram_tensor(f"in_{name}", v.shape, mybir.dt.from_np(v.dtype), kind="ExternalInput").ap()
    scratch = {"qT_d": (ROWS, DM), "iqT_d": (ROWS, IH * ID), "gate_d": (ROWS, DM), "iwl_d": (DB, IH, DS),
               "y1_d": (ROWS, DM), "z_d": (ROWS, DM), "qkv_d": (3 * H, P, ROWS)}
    outs = {"k_all": (ROWS, G * HD), "v_all": (ROWS, G * HD), "ik_all": (ROWS, ID), "y_all": (ROWS, DM),
            "S_p": (H, HD, HD), "S_s": (DB, H, HD, HD), "newbuf_p": (CW_TAPS - 1, CONV), "newbuf_s": (DB * (CW_TAPS - 1), CONV)}
    for name, shape in scratch.items():
        d[name] = nc.dram_tensor(name, shape, F32, kind="Internal").ap()
    for name, shape in outs.items():
        d[name] = nc.dram_tensor(f"out_{name}", shape, F32, kind="ExternalOutput").ap()
    build(nc, d)
    r = {k[4:]: v for k, v in _run(nc, [arrays], core_ids=[0]).results[0].items()}
    k, v, ik, y = r["k_all"], r["v_all"], r["ik_all"], r["y_all"]
    return (y[P:].reshape(1, SEQ, DM), y[:NS].reshape(DB, DS, DM),
            k[P:].reshape(1, SEQ, 1, G, HD), v[P:].reshape(1, SEQ, 1, G, HD), ik[P:].reshape(1, SEQ, 1, ID),
            k[:NS].reshape(DB, DS, 1, G, HD), v[:NS].reshape(DB, DS, 1, G, HD), ik[:NS].reshape(DB, DS, 1, ID),
            r["S_p"].reshape(1, 1, H, HD, HD), r["newbuf_p"].reshape(1, 1, CW_TAPS - 1, CONV),
            r["S_s"].reshape(DB, 1, H, HD, HD), r["newbuf_s"].reshape(DB, 1, CW_TAPS - 1, CONV))
```
